# Optimizing a Trainium2 kernel written in Bass

```python
import math
import jax, jax.numpy as jnp
from jax import lax
import numpy as np

D_MODEL = 1024
BATCH = 1
SEQ = 256
DEPTH = 2

CTX_LEN = 256
GRID_W = 64
N_MIXERS = 3
E_BRANCH = 2 * D_MODEL
MLA_HEADS = D_MODEL // 64
MLA_NOPE = 128
MLA_ROPE = 64
MLA_V = 128
MLA_WIDTH = MLA_HEADS * MLA_V
MLA_Q_RANK = D_MODEL // 4
MLA_KV_RANK = D_MODEL // 8
MLA_SPLITS = (MLA_Q_RANK, MLA_Q_RANK + MLA_KV_RANK, MLA_Q_RANK + MLA_KV_RANK + MLA_ROPE)
MLA_IN = MLA_Q_RANK + MLA_KV_RANK + MLA_ROPE + MLA_WIDTH
ROPE_BASE = 10000.0
Q_BLOCK = 128
S5_GROUP = 16
S5_GROUPS = E_BRANCH // S5_GROUP
S5_STATE = 64
S5_CHUNK = 128
DT_MIN = 0.001
DT_MAX = 0.1
CONV_WIDTH = 31
CONV_PAD = CONV_WIDTH // 2
DEEPNORM_ALPHA = (2.0 * DEPTH) ** 0.25
DEEPNORM_BETA = (8.0 * DEPTH) ** -0.25
NORM_EPS = 1e-6


def _layernorm(x, g, b):
    xf = x.astype(jnp.float32)
    mu = jnp.mean(xf, axis=-1, keepdims=True)
    var = jnp.mean(jnp.square(xf - mu), axis=-1, keepdims=True)
    y = (xf - mu) * lax.rsqrt(var + NORM_EPS) * g.astype(jnp.float32) + b.astype(jnp.float32)
    return y.astype(x.dtype)

def _rmsnorm(x, g):
    xf = x.astype(jnp.float32)
    y = xf * lax.rsqrt(jnp.mean(jnp.square(xf), axis=-1, keepdims=True) + NORM_EPS) * g.astype(jnp.float32)
    return y.astype(x.dtype)

def _axial_rope_tables(rows):
    r, col = jnp.meshgrid(jnp.arange(rows, dtype=jnp.float32), jnp.arange(GRID_W, dtype=jnp.float32), indexing='ij')
    r, col = r.reshape(-1), col.reshape(-1)
    quarter = MLA_ROPE // 4
    inv = ROPE_BASE ** (-jnp.arange(quarter, dtype=jnp.float32) / quarter)
    ang_r = r[:, None] * inv
    ang_c = col[:, None] * inv
    ang = jnp.concatenate([ang_r, ang_r, ang_c, ang_c], axis=-1)
    return jnp.cos(ang), jnp.sin(ang)

def _apply_rope(v, cos, sin):
    x1, x2, x3, x4 = jnp.split(v, 4, axis=-1)
    rot = jnp.concatenate([-x2, x1, -x4, x3], axis=-1)
    return v * cos.astype(v.dtype) + rot * sin.astype(v.dtype)

def _mla_split(h, w_in, kv_norm):
    q_dn, kv_dn, k_rope, gate = jnp.split(h @ w_in, MLA_SPLITS, axis=-1)
    return q_dn, _rmsnorm(kv_dn, kv_norm), k_rope, gate

def _mla_queries(q_dn, q_norm, w_uq, w_uk):
    b, n, _ = q_dn.shape
    q = (_rmsnorm(q_dn, q_norm) @ w_uq).reshape(b, n, MLA_HEADS, MLA_NOPE + MLA_ROPE)
    q_abs = jnp.einsum('bnhd,chd->bnhc', q[..., :MLA_NOPE], w_uk)
    return q_abs, q[..., MLA_NOPE:]

def _mla_output(o_lat, gate, w_uv, w_out):
    b, n = o_lat.shape[:2]
    v = jnp.einsum('bnhc,chv->bnhv', o_lat, w_uv).reshape(b, n, MLA_WIDTH)
    return (v * jax.nn.silu(gate)) @ w_out

def _mla_mixer(h_lat, h_ctx, cos, sin, w_in, q_norm, kv_norm, w_uq, w_uk, w_uv, w_out, with_ctx_out):
    b, s, _ = h_lat.shape
    scale = (MLA_NOPE + MLA_ROPE) ** -0.5
    q_dn_l, ckv_l, kr_l, g_l = _mla_split(h_lat, w_in, kv_norm)
    q_dn_c, ckv_c, kr_c, g_c = _mla_split(h_ctx, w_in, kv_norm)
    qa_l, qr_l = _mla_queries(q_dn_l, q_norm, w_uq, w_uk)
    keys_lat = jnp.concatenate([ckv_l, _apply_rope(kr_l, cos, sin)], axis=-1)
    keys_ctx = jnp.concatenate([ckv_c, kr_c], axis=-1)

    def block(args):
        qa, qr, cs, sn = args
        q_pos = jnp.concatenate([qa, _apply_rope(qr, cs[:, None], sn[:, None])], axis=-1)
        q_free = jnp.concatenate([qa, qr], axis=-1)
        s_all = jnp.concatenate([jnp.einsum('bthd,bkd->bhtk', q_pos, keys_lat),
                                 jnp.einsum('bthd,bkd->bhtk', q_free, keys_ctx)], axis=-1)
        p = jax.nn.softmax(s_all.astype(jnp.float32) * scale, axis=-1).astype(ckv_l.dtype)
        return (jnp.einsum('bhtk,bkc->bthc', p[..., :s], ckv_l)
                + jnp.einsum('bhtk,bkc->bthc', p[..., s:], ckv_c))

    nblk = s // Q_BLOCK
    to_blocks = lambda a: a.reshape(b, nblk, Q_BLOCK, *a.shape[2:]).swapaxes(0, 1)
    o = lax.map(block, (to_blocks(qa_l), to_blocks(qr_l),
                        cos.reshape(nblk, Q_BLOCK, MLA_ROPE), sin.reshape(nblk, Q_BLOCK, MLA_ROPE)))
    o = o.swapaxes(0, 1).reshape(b, s, MLA_HEADS, MLA_KV_RANK)
    y_lat = _mla_output(o, g_l, w_uv, w_out)
    if not with_ctx_out:
        return y_lat, None
    qa_c, qr_c = _mla_queries(q_dn_c, q_norm, w_uq, w_uk)
    q_c = jnp.concatenate([qa_c, qr_c], axis=-1)
    p_c = jax.nn.softmax(jnp.einsum('bthd,bkd->bhtk', q_c, keys_ctx).astype(jnp.float32) * scale,
                         axis=-1).astype(ckv_c.dtype)
    o_c = jnp.einsum('bhtk,bkc->bthc', p_c, ckv_c)
    return y_lat, _mla_output(o_c, g_c, w_uv, w_out)

def _ssm_combine(left, right):
    a_l, b_l = left
    a_r, b_r = right
    return a_r * a_l, a_r * b_l + b_r

def _s5_direction(u_ctx, u_lat, lam, dt, bmat, cmat):
    lam_dt = lam * dt[:, None]
    lam_bar = jnp.exp(lam_dt)
    b_bar = ((lam_bar - 1.0) / lam)[..., None] * bmat
    powers = jnp.exp(lam_dt[None] * jnp.arange(1, S5_CHUNK + 1, dtype=jnp.float32)[:, None, None])

    def step(h, u_chunk):
        bu = jnp.einsum('btgs,gps->btgp', u_chunk.astype(jnp.complex64), b_bar)
        a = jnp.broadcast_to(lam_bar, bu.shape)
        _, xs = lax.associative_scan(_ssm_combine, (a, bu), axis=1)
        xs = xs + powers[None] * h[:, None]
        y = jnp.einsum('btgp,gsp->btgs', xs, cmat).real
        return xs[:, -1], y

    def run(u, h0):
        bsz, n = u.shape[:2]
        nch = n // S5_CHUNK
        chunks = u.reshape(bsz, nch, S5_CHUNK, S5_GROUPS, S5_GROUP).swapaxes(0, 1)
        h_fin, ys = lax.scan(step, h0, chunks)
        return h_fin, ys.swapaxes(0, 1).reshape(bsz, n, S5_GROUPS * S5_GROUP)

    h0 = jnp.zeros((u_lat.shape[0], S5_GROUPS, S5_STATE), jnp.complex64)
    h_ctx, y_ctx = run(u_ctx, h0)
    _, y_lat = run(u_lat, h_ctx)
    return y_ctx, y_lat

def _s5_mixer(h_lat, h_ctx, w_in, lam_re, lam_im, log_dt, b_re, b_im, c_re, c_im, d_skip, w_glu, b_glu, w_out,
              with_ctx_out):
    u_l, g_l = jnp.split(h_lat @ w_in, 2, axis=-1)
    u_c, g_c = jnp.split(h_ctx @ w_in, 2, axis=-1)
    ul, uc = u_l.astype(jnp.float32), u_c.astype(jnp.float32)
    dsk = d_skip.astype(jnp.float32)
    y_l, y_c = dsk * ul, dsk * uc
    f32 = lambda a: a.astype(jnp.float32)
    for direction in range(2):
        lam = lax.complex(jnp.minimum(f32(lam_re[direction]), -1e-4), f32(lam_im[direction]))
        dt = jnp.exp(f32(log_dt[direction]))
        bmat = lax.complex(f32(b_re[direction]), f32(b_im[direction]))
        cmat = lax.complex(f32(c_re[direction]), f32(c_im[direction]))
        if direction == 0:
            yc, yl = _s5_direction(uc, ul, lam, dt, bmat, cmat)
        else:
            yc, yl = _s5_direction(jnp.flip(uc, 1), jnp.flip(ul, 1), lam, dt, bmat, cmat)
            yc, yl = jnp.flip(yc, 1), jnp.flip(yl, 1)
        y_l, y_c = y_l + yl, y_c + yc

    def glu_out(y, g):
        y = jax.nn.gelu(y.astype(g.dtype))
        ya, yb = jnp.split(y @ w_glu + b_glu, 2, axis=-1)
        return ((ya * jax.nn.sigmoid(yb)) * jax.nn.silu(g)) @ w_out

    y_ctx = glu_out(y_c, g_c) if with_ctx_out else None
    return glu_out(y_l, g_l), y_ctx

def _conv_mixer(h_lat, h_ctx, w_in, dw, dw_b, ln_g, ln_b, w_out, with_ctx_out):
    def branch(h):
        a, bgate, g = jnp.split(h @ w_in, 3, axis=-1)
        v = a * jax.nn.sigmoid(bgate)
        v = lax.conv_general_dilated(v, dw[:, None, :], window_strides=(1,), padding=[(CONV_PAD, CONV_PAD)],
                                     dimension_numbers=('NWC', 'WIO', 'NWC'),
                                     feature_group_count=E_BRANCH) + dw_b
        v = jax.nn.silu(_layernorm(v, ln_g, ln_b))
        return (v * jax.nn.silu(g)) @ w_out
    y_ctx = branch(h_ctx) if with_ctx_out else None
    return branch(h_lat), y_ctx

def first_inputs(seed: int = 0) -> dict:
    key = jax.random.key(seed)
    ks = iter(jax.random.split(key, 48))
    f = jnp.float32
    nrm = lambda shape, scale: jax.random.normal(next(ks), shape, f) * scale
    n_a, n_b, n_c = [len(range(k, DEPTH, N_MIXERS)) for k in range(N_MIXERS)]
    D, E, G, P, GS = D_MODEL, E_BRANCH, S5_GROUPS, S5_STATE, S5_GROUP
    lam_im = jnp.broadcast_to(math.pi * jnp.arange(P, dtype=f), (n_b, 2, G, P))
    return {
        'x': nrm((BATCH, SEQ, D), 1.0),
        'c': nrm((BATCH, D), 1.0),
        'ctx': nrm((BATCH, CTX_LEN, D), 1.0),
        'c_ctx': nrm((D,), 1.0),
        'w_mod': nrm((DEPTH, D, 3 * D), 0.5 * D ** -0.5),
        'b_mod': nrm((DEPTH, 3 * D), 0.02),
        'ln_g': 1.0 + nrm((DEPTH, D), 0.02),
        'ln_b': nrm((DEPTH, D), 0.02),
        'mla_w_in': nrm((n_a, D, MLA_IN), D ** -0.5),
        'mla_q_norm': 1.0 + nrm((n_a, MLA_Q_RANK), 0.02),
        'mla_kv_norm': 1.0 + nrm((n_a, MLA_KV_RANK), 0.02),
        'mla_w_uq': nrm((n_a, MLA_Q_RANK, MLA_HEADS * (MLA_NOPE + MLA_ROPE)), MLA_Q_RANK ** -0.5),
        'mla_w_uk': nrm((n_a, MLA_KV_RANK, MLA_HEADS, MLA_NOPE), MLA_NOPE ** -0.5),
        'mla_w_uv': nrm((n_a, MLA_KV_RANK, MLA_HEADS, MLA_V), MLA_KV_RANK ** -0.5),
        'mla_w_out': nrm((n_a, MLA_WIDTH, D), DEEPNORM_BETA * MLA_WIDTH ** -0.5),
        's5_w_in': nrm((n_b, D, 2 * E), D ** -0.5),
        's5_lam_re': -0.5 + nrm((n_b, 2, G, P), 0.01),
        's5_lam_im': lam_im,
        's5_log_dt': jax.random.uniform(next(ks), (n_b, 2, G), f, math.log(DT_MIN), math.log(DT_MAX)),
        's5_b_re': nrm((n_b, 2, G, P, GS), (2.0 * GS) ** -0.5),
        's5_b_im': nrm((n_b, 2, G, P, GS), (2.0 * GS) ** -0.5),
        's5_c_re': nrm((n_b, 2, G, GS, P), P ** -0.5),
        's5_c_im': nrm((n_b, 2, G, GS, P), P ** -0.5),
        's5_d': nrm((n_b, E), 0.5),
        's5_w_glu': nrm((n_b, E, 2 * E), E ** -0.5),
        's5_b_glu': nrm((n_b, 2 * E), 0.02),
        's5_w_out': nrm((n_b, E, D), DEEPNORM_BETA * E ** -0.5),
        'cv_w_in': nrm((n_c, D, 3 * E), D ** -0.5),
        'cv_dw': nrm((n_c, CONV_WIDTH, E), CONV_WIDTH ** -0.5),
        'cv_dw_b': nrm((n_c, E), 0.02),
        'cv_ln_g': 1.0 + nrm((n_c, E), 0.02),
        'cv_ln_b': nrm((n_c, E), 0.02),
        'cv_w_out': nrm((n_c, E, D), DEEPNORM_BETA * E ** -0.5),
    }

def first_block(x, c, ctx, c_ctx, w_mod, b_mod, ln_g, ln_b,
              mla_w_in, mla_q_norm, mla_kv_norm, mla_w_uq, mla_w_uk, mla_w_uv, mla_w_out,
              s5_w_in, s5_lam_re, s5_lam_im, s5_log_dt, s5_b_re, s5_b_im, s5_c_re, s5_c_im, s5_d,
              s5_w_glu, s5_b_glu, s5_w_out,
              cv_w_in, cv_dw, cv_dw_b, cv_ln_g, cv_ln_b, cv_w_out):
    n_tokens = x.shape[1]
    ROWS = n_tokens // GRID_W
    cos, sin = _axial_rope_tables(ROWS)
    cond = jax.nn.silu(c)
    cond_ctx = jax.nn.silu(c_ctx)
    for i in range(DEPTH):
        kind, j = i % N_MIXERS, i // N_MIXERS
        with_ctx_out = i < DEPTH - 1
        sh, sc, gt = jnp.split(cond @ w_mod[i] + b_mod[i], 3, axis=-1)
        sh_c, sc_c, gt_c = jnp.split(cond_ctx @ w_mod[i] + b_mod[i], 3, axis=-1)
        h_lat = x * (1.0 + sc[:, None]) + sh[:, None]
        h_ctx = ctx * (1.0 + sc_c) + sh_c
        if kind == 0:
            y_lat, y_ctx = _mla_mixer(h_lat, h_ctx, cos, sin, mla_w_in[j], mla_q_norm[j], mla_kv_norm[j],
                                      mla_w_uq[j], mla_w_uk[j], mla_w_uv[j], mla_w_out[j], with_ctx_out)
        elif kind == 1:
            y_lat, y_ctx = _s5_mixer(h_lat, h_ctx, s5_w_in[j], s5_lam_re[j], s5_lam_im[j], s5_log_dt[j],
                                     s5_b_re[j], s5_b_im[j], s5_c_re[j], s5_c_im[j], s5_d[j],
                                     s5_w_glu[j], s5_b_glu[j], s5_w_out[j], with_ctx_out)
        else:
            y_lat, y_ctx = _conv_mixer(h_lat, h_ctx, cv_w_in[j], cv_dw[j], cv_dw_b[j], cv_ln_g[j], cv_ln_b[j],
                                       cv_w_out[j], with_ctx_out)
        x = _layernorm(DEEPNORM_ALPHA * x + gt[:, None] * y_lat, ln_g[i], ln_b[i])
        if with_ctx_out:
            ctx = _layernorm(DEEPNORM_ALPHA * ctx + gt_c * y_ctx, ln_g[i], ln_b[i])
    return x


DEPTH_2 = 1

CHUNK = 64
LEFT_CHUNKS = 8
HEAD_DIM = 64
N_HEADS_A = 8
N_HEADS_B = 8
WIDTH_A = N_HEADS_A * HEAD_DIM
WIDTH_B = N_HEADS_B * HEAD_DIM
MAX_REL = 128
N_REL = 2 * MAX_REL + 1
QUERY_BLOCK = 128
D_FF = 2816
CONV_WIDTH_2 = 3
IN_WIDTH = 3 * WIDTH_A + 3 * WIDTH_B + 2 * D_MODEL
EPS = 1e-6


def rms_norm(x, gain):
    xf = x.astype(jnp.float32)
    y = xf * lax.rsqrt(jnp.mean(xf * xf, axis=-1, keepdims=True) + EPS)
    return (y * gain.astype(jnp.float32)).astype(x.dtype)

def chunked_attention(q, k, v, q_gain, k_gain, rel_bias):
    b, s, h, dh = q.shape
    nc = s // CHUNK
    band = (LEFT_CHUNKS + 1) * CHUNK
    q = rms_norm(q, q_gain)
    k = rms_norm(k, k_gain)
    qc = q.reshape(b, nc, CHUNK, h, dh)
    pad = ((0, 0), (LEFT_CHUNKS * CHUNK, 0), (0, 0), (0, 0))
    kp = jnp.pad(k, pad).reshape(b, nc + LEFT_CHUNKS, CHUNK, h, dh)
    vp = jnp.pad(v, pad).reshape(b, nc + LEFT_CHUNKS, CHUNK, h, dh)
    kb = jnp.concatenate([kp[:, i:i + nc] for i in range(LEFT_CHUNKS + 1)], axis=2)
    vb = jnp.concatenate([vp[:, i:i + nc] for i in range(LEFT_CHUNKS + 1)], axis=2)
    scores = jnp.einsum('bnqhd,bnkhd->bnhqk', qc, kb).astype(jnp.float32) * (dh ** -0.5)
    r = jnp.arange(CHUNK)[:, None]
    key_off = jnp.arange(band)[None, :] - LEFT_CHUNKS * CHUNK
    rel = r - key_off
    idx = jnp.clip(rel, -MAX_REL, MAX_REL) + MAX_REL
    bias = rel_bias[:, idx].astype(jnp.float32)
    valid = (jnp.arange(nc)[:, None] * CHUNK + key_off) >= 0
    scores = jnp.where(valid[None, :, None, None, :], scores + bias[None, None], -jnp.inf)
    probs = jax.nn.softmax(scores, axis=-1).astype(v.dtype)
    out = jnp.einsum('bnhqk,bnkhd->bnqhd', probs, vb)
    return out.reshape(b, s, h * dh)

def stick_breaking_attention(q, k, v):
    b, s, h, dh = q.shape
    nb = s // QUERY_BLOCK
    kh = k.transpose(0, 2, 1, 3)
    vh = v.transpose(0, 2, 1, 3)
    qblocks = q.transpose(0, 2, 1, 3).reshape(b, h, nb, QUERY_BLOCK, dh).transpose(2, 0, 1, 3, 4)
    key_pos = jnp.arange(s)

    def block(args):
        qb, blk = args
        z = jnp.einsum('bhqd,bhkd->bhqk', qb, kh).astype(jnp.float32) * (dh ** -0.5)
        q_pos = blk * QUERY_BLOCK + jnp.arange(QUERY_BLOCK)
        causal = key_pos[None, :] < q_pos[:, None]
        log_keep = jnp.where(causal, -jax.nn.softplus(z), 0.0)
        log_after = lax.cumsum(log_keep, axis=3, reverse=True) - log_keep
        w = jnp.where(causal, jnp.exp(jax.nn.log_sigmoid(z) + log_after), 0.0)
        return jnp.einsum('bhqk,bhkd->bhqd', w.astype(vh.dtype), vh)

    out = lax.map(block, (qblocks, jnp.arange(nb)))
    return out.transpose(1, 0, 3, 2, 4).reshape(b, s, h * dh)

def conv_glu(x, w_up, conv_w, conv_b, w_down):
    hid = x @ w_up
    hid = lax.conv_general_dilated(
        hid, conv_w[:, None, :], window_strides=(1,),
        padding=((CONV_WIDTH_2 - 1, 0),),
        dimension_numbers=('NWC', 'WIO', 'NWC'),
        feature_group_count=2 * D_FF) + conv_b
    gate, up = hid[..., :D_FF], hid[..., D_FF:]
    return (jax.nn.silu(gate) * up) @ w_down

def second_inputs(seed: int = 0) -> dict:
    key = jax.random.key(seed)
    ks = jax.random.split(key, 16)
    f32 = jnp.float32
    nrm = lambda k, shape, scale: jax.random.normal(k, shape, f32) * scale
    return {
        "x": nrm(ks[0], (BATCH, SEQ, D_MODEL), 1.0),
        "norm1_g": 1.0 + nrm(ks[1], (DEPTH_2, D_MODEL), 0.02),
        "w_in": nrm(ks[2], (DEPTH_2, D_MODEL, IN_WIDTH), D_MODEL ** -0.5),
        "q_norm_g": 1.0 + nrm(ks[3], (DEPTH_2, HEAD_DIM), 0.02),
        "k_norm_g": 1.0 + nrm(ks[4], (DEPTH_2, HEAD_DIM), 0.02),
        "rel_bias": nrm(ks[5], (DEPTH_2, N_HEADS_A, N_REL), 0.2),
        "w_branch_a": nrm(ks[6], (DEPTH_2, WIDTH_A, D_MODEL), WIDTH_A ** -0.5),
        "w_branch_b": nrm(ks[7], (DEPTH_2, WIDTH_B, D_MODEL), WIDTH_B ** -0.5),
        "w_out": nrm(ks[8], (DEPTH_2, D_MODEL, D_MODEL), D_MODEL ** -0.5),
        "norm2_g": 1.0 + nrm(ks[9], (DEPTH_2, D_MODEL), 0.02),
        "w_ffn_up": nrm(ks[10], (DEPTH_2, D_MODEL, 2 * D_FF), D_MODEL ** -0.5),
        "ffn_conv_w": nrm(ks[11], (DEPTH_2, CONV_WIDTH_2, 2 * D_FF), CONV_WIDTH_2 ** -0.5),
        "ffn_conv_b": nrm(ks[12], (DEPTH_2, 2 * D_FF), 0.01),
        "w_ffn_down": nrm(ks[13], (DEPTH_2, D_FF, D_MODEL), D_FF ** -0.5),
    }

def second_block(x, norm1_g, w_in, q_norm_g, k_norm_g, rel_bias, w_branch_a, w_branch_b,
              w_out, norm2_g, w_ffn_up, ffn_conv_w, ffn_conv_b, w_ffn_down):
    b, s, _ = x.shape
    o1 = 3 * WIDTH_A
    o2 = o1 + 3 * WIDTH_B
    for l in range(DEPTH_2):
        hn = rms_norm(x, norm1_g[l])
        proj = hn @ w_in[l]
        qa, ka, va = [proj[..., i * WIDTH_A:(i + 1) * WIDTH_A].reshape(b, s, N_HEADS_A, HEAD_DIM)
                      for i in range(3)]
        qb, kb, vb = [proj[..., o1 + i * WIDTH_B:o1 + (i + 1) * WIDTH_B].reshape(b, s, N_HEADS_B, HEAD_DIM)
                      for i in range(3)]
        gate_a = proj[..., o2:o2 + D_MODEL]
        gate_b = proj[..., o2 + D_MODEL:o2 + 2 * D_MODEL]
        out_a = chunked_attention(qa, ka, va, q_norm_g[l], k_norm_g[l], rel_bias[l])
        out_b = stick_breaking_attention(qb, kb, vb)
        mixed = (jax.nn.sigmoid(gate_a) * (out_a @ w_branch_a[l])
                 + jax.nn.sigmoid(gate_b) * (out_b @ w_branch_b[l]))
        x = x + mixed @ w_out[l]
        x = x + conv_glu(rms_norm(x, norm2_g[l]), w_ffn_up[l], ffn_conv_w[l],
                         ffn_conv_b[l], w_ffn_down[l])
    return x


def setup_inputs(seed=0):
    out = dict(first_inputs(seed))
    for name, value in second_inputs(seed + 1).items():
        if name != "x":
            out[name + "_2"] = value
    return out


def reference(
    x, c, ctx, c_ctx, w_mod, b_mod, ln_g, ln_b, mla_w_in, mla_q_norm, mla_kv_norm, mla_w_uq,
    mla_w_uk, mla_w_uv, mla_w_out, s5_w_in, s5_lam_re, s5_lam_im, s5_log_dt, s5_b_re, s5_b_im,
    s5_c_re, s5_c_im, s5_d, s5_w_glu, s5_b_glu, s5_w_out, cv_w_in, cv_dw, cv_dw_b, cv_ln_g,
    cv_ln_b, cv_w_out, norm1_g_2, w_in_2, q_norm_g_2, k_norm_g_2, rel_bias_2, w_branch_a_2,
    w_branch_b_2, w_out_2, norm2_g_2, w_ffn_up_2, ffn_conv_w_2, ffn_conv_b_2, w_ffn_down_2,
):
    x = first_block(
        x, c, ctx, c_ctx, w_mod, b_mod, ln_g, ln_b, mla_w_in, mla_q_norm, mla_kv_norm, mla_w_uq,
        mla_w_uk, mla_w_uv, mla_w_out, s5_w_in, s5_lam_re, s5_lam_im, s5_log_dt, s5_b_re,
        s5_b_im, s5_c_re, s5_c_im, s5_d, s5_w_glu, s5_b_glu, s5_w_out, cv_w_in, cv_dw, cv_dw_b,
        cv_ln_g, cv_ln_b, cv_w_out,
    )
    return second_block(
        x, norm1_g_2, w_in_2, q_norm_g_2, k_norm_g_2, rel_bias_2, w_branch_a_2, w_branch_b_2,
        w_out_2, norm2_g_2, w_ffn_up_2, ffn_conv_w_2, ffn_conv_b_2, w_ffn_down_2,
    )


_drawn_inputs = setup_inputs


def setup_inputs(seed=0):
    import zlib

    import numpy as np

    out = dict(_drawn_inputs(seed))
    spreads = {}
    factors = {'ctx': 8.0,
     'c_ctx': 6.617,
     'b_mod': 8.0,
     'mla_w_in': 2.807,
     'mla_q_norm': 8.0,
     'mla_kv_norm': 8.0,
     'mla_w_uq': 6.922,
     'mla_w_uk': 7.618,
     'mla_w_uv': 2.925,
     'mla_w_out': 3.103,
     's5_w_in': 3.854,
     's5_lam_re': 64.0,
     's5_lam_im': 64.0,
     's5_log_dt': 64.0,
     's5_b_re': 64.0,
     's5_b_im': 64.0,
     's5_c_re': 64.0,
     's5_c_im': 64.0,
     's5_d': 4.21,
     's5_w_glu': 3.796,
     's5_b_glu': 8.0,
     's5_w_out': 3.754,
     'norm1_g_2': 5.758,
     'q_norm_g_2': 8.0,
     'k_norm_g_2': 8.0,
     'rel_bias_2': 3.764,
     'norm2_g_2': 3.782,
     'ffn_conv_b_2': 7.822}
    for name, (base, spread) in spreads.items():
        noise = np.random.default_rng([zlib.crc32(name.encode()), seed]).standard_normal(out[name].shape)
        drawn = base * np.exp(spread * noise) if base else spread * noise
        out[name] = __import__('jax').numpy.asarray(drawn.astype(out[name].dtype))
    for name, factor in factors.items():
        out[name] = (out[name] * factor).astype(out[name].dtype)
    return out
```

```python
from contextlib import ExitStack

import numpy as np

import concourse.bass as bass
from concourse import mybir

F32 = mybir.dt.float32
I32 = mybir.dt.int32
ALU = mybir.AluOpType
ACT = mybir.ActivationFunctionType
AX = mybir.AxisListType.X

P = 128
D = 1024
KD = D // P
T = 256
NTT = 4
E = 2 * D
KE = E // P
DEPTH = 2
ALPHA = (2.0 * DEPTH) ** 0.25
EPS = 1e-6

H = 16
NOPE, ROPE, QR, KVR = 128, 64, 256, 128
HEAD_IN = QR + KVR + ROPE
MLA_SCALE = (NOPE + ROPE) ** -0.5
GRID_W = 64

GS, NG, NP = 16, 128, 64
L = 8
NC = 2 * T // L
NCL = T // L
GQ = 16
NQ = NG // 2 // GQ
TWO_PI = 2.0 * np.pi
PI_1, PI_2 = 6.28125, float(np.float32(TWO_PI - 6.28125))
PI_3 = float(TWO_PI - 6.28125 - np.float64(np.float32(TWO_PI - 6.28125)))
LN2_1 = 0.693359375
LN2_2 = float(np.log(2.0) - 0.693359375)
ROUND = 12582912.0

NH2, HD = 8, 64
MAX_REL = 128
FF = 2816
KF = FF // P
LOW = -1e30

SLOTS, SLOT = 3, KD * 512

VECTORS = {"cond": 2 * KD, "q_norm": 2, "s5_d": KE, "b_glu": 2 * KE, "norm1": KD, "norm2": KD, "q_gain": 1, "k_gain": 1,
           "conv_b": 2 * KF, "conv_w0": 2 * KF, "conv_w1": 2 * KF, "conv_w2": 2 * KF}


def vector_rows():
    at, n = {}, 0
    for name, rows in VECTORS.items():
        at[name] = n
        n += rows
    return at, n


VROW, NVROW = vector_rows()


SHARED = {"qnT_mm": "transposed", "ckvT_mm": "transposed", "krT_mm": "transposed", "colv_mm": "transposed",
          "lamT_mm": "transposed", "xT_mm": "transposed", "sa_mm": "scores", "s_mm": "scores", "pat_mm": "probs_turned",
          "pt_mm": "probs_turned", "out0_mm": "out_sum", "out1_mm": "out_sum", "out2_mm": "out_sum", "down_mm": "out_sum",
          "out0_k": "out_part", "out1_k": "out_part", "down_k": "out_part", "oa_mm": "attended", "ob_mm": "attended",
          "res0": "residual", "res1": "residual", "res2": "residual", "res3": "residual", "res0_a": "scaled",
          "res1_a": "scaled", "var0": "variance", "var1": "variance", "x1": "normalized", "x2": "normalized",
          "std0_0": "root", "std0_1": "root", "std0_2": "root", "std0_3": "root", "std1_0": "root", "std1_1": "root",
          "qk_rms": "root", "rms": "root", "lat_rms": "root", "qn": "latent", "ckv": "latent", "kr": "latent",
          "kr_pos": "latent", "qrp_a": "rope_part", "qrp_b": "rope_part", "nmax": "row_max", "nmax_a": "row_max",
          "pn": "probs", "pan": "probs", "pt": "probsT", "pat": "probsT", "gate": "gates", "gs": "gates",
          "gates": "gates", "p": "exps", "pa": "exps", "qnT": "latentT", "ckvT": "latentT", "lat_ss": "squares", "lat_sq": "squares", "x_sq": "squares",
          "qk_sq": "squares", "va": "value", "vb": "value", "oa": "attendedT", "ob": "attendedT"}


class Signals:

    def __init__(self, nc, stack, counts):
        self.nc, self.stack, self.known = nc, stack, counts
        self.sems, self.total, self.seen = {}, {}, {}

    def sem(self, name):
        name = SHARED.get(name, name)
        if name not in self.sems:
            self.sems[name] = self.stack.enter_context(self.nc.semaphore(name))
        return self.sems[name]

    def up(self, name, key=None, by=1):
        shared = SHARED.get(name, name)
        self.total[shared] = self.total.get(shared, 0) + by
        self.seen[(name, key)] = self.total[shared]
        return self.sem(name), by

    def at(self, name, key=None):
        return self.sem(name), 1 if self.known is None else self.known[(name, key)]

    def last(self, name):
        return self.sem(name), self.total[name]


def over(ap, *steps):
    return bass.AP(tensor=ap.tensor, offset=ap.offset, ap=[list(ap.ap[0])] + [list(s) for s in steps])


def dview(ap, offset, *steps):
    return bass.AP(tensor=ap.tensor, offset=ap.offset + offset, ap=[list(s) for s in steps])


def build(nc, a, out, counts, places):
    with ExitStack() as stack:
        S = Signals(nc, stack, counts)
        block = stack.enter_context(nc.Block())
        sb = stack.enter_context(nc.sbuf_tensor("memory", [P, 53200], F32))
        banks = [stack.enter_context(nc.psum_tensor(f"bank{i}", [P, 512], F32))[:, :] for i in range(8)]
        u_dram = nc.dram_tensor("u_scratch", [E, 2 * T], F32).ap()
        k_dram = nc.dram_tensor("k_scratch", [NG, GS, 15 * GS], F32).ap()
        y_dram = nc.dram_tensor("y_scratch", [E, T], F32).ap()

        def carve(start):
            at = [start]

            def take(*shape):
                n = int(np.prod(shape))
                assert at[0] + n <= 53200, (at[0] + n, shape)
                v = sb[:, at[0]:at[0] + n]
                at[0] += n
                if len(shape) > 1:
                    names = " ".join("abcde"[:len(shape)])
                    v = v.rearrange(f"p ({names}) -> p {names}", **{"abcde"[i]: shape[i] for i in range(len(shape))})
                return v
            return take, at

        take, at = carve(0)
        x = take(NTT, D)
        ident = take(P)
        colv = take(3, P)
        sel = take(2, P)
        condT = take(2 * KD)
        shsc = take(2 * KD, 2)
        gtb = take(2, D)
        modrow = take(2, 512)
        bmod = take(2, 512)
        small = take(256)
        ring_at = at[0]
        ring = take(SLOTS, SLOT)
        hT = take(KD, 2 * T)
        arena = at[0]

        take, at = carve(arena)
        gT = take(H, 2 * T)
        wukv = take(2, H * P)
        lnbc0 = wukv.rearrange("p a n -> p (a n)")[:, 0:2 * D].rearrange("p (a n) -> p a n", a=2)
        qrfT = take(4, 2 * T)
        qrpT = take(4, T)
        qrf = take(2, 512)
        qrp = take(512)
        qrt = take(512)
        qT = take(2, 512)
        kT = take(2, 512)
        PT = take(2, 3, 512)
        olT = take(512)
        vrows = kT.rearrange("p a n -> p (a n)")[:, 0:3 * P].rearrange("p (a n) -> p a n", a=3)
        qn = take(NTT, QR)
        ckv = take(NTT, KVR)
        ckvT = take(2 * T)
        qnT = take(2, 2 * T)
        kr = take(NTT, 2, ROPE)
        krt = qrp[:, 0:2 * ROPE].rearrange("p (a n) -> p a n", a=2)
        krT = take(2 * T)
        kvg = take(KVR)
        rope = take(2, 2, ROPE)
        sq = qrt
        hT_flat = hT.rearrange("p a n -> p (a n)")
        pl = hT_flat[:, 0:2048].rearrange("p (b t n) -> p b t n", b=2, t=2)
        pc = hT_flat[:, 2048:3072].rearrange("p (b t n) -> p b t n", b=2, t=2)
        st0 = small[:, 0:64]

        take, at = carve(arena)
        gsT = take(KE, T)
        lam = take(2, P)
        ldt = take(2)
        dts = take(16)
        sc_a = take(14, P)
        lamT = take(4, P)
        lamL = take(2, 2, 64)
        lamN = take(2, 2, 64)
        wR = take(2, 2, 64)
        wN = take(2, 2, 64)
        L8R = take(2, 2, 64)
        L8N = take(2, 2, 64)
        ust = take(2, 2 * T)
        braw = take(2, GQ, 2, GS)
        bbar = take(2, GQ, 2, GS)
        bbd = take(2, GQ, 2, 2 * GS)
        cn = take(2, 2, 2, P)
        kt = take(4, 15 * GS)
        tmpd = take(2, 512)
        tmpp = take(2, 512)
        y_sb = take(2, GQ, NCL)
        mbt = take(2, 2, 4, P)
        end_l1 = at[0]
        take, at = carve(ring_at)
        mc = take(2, GQ, 2, 9, GS)
        u_sb = take(2, GQ, NC)
        xs = take(NC, 2, 2, GQ)
        take, at = carve(end_l1)
        mb = take(2, 4, 2, L, GS)
        tt_sb = take(2, GQ, L * GS)
        scan = take(2, 64)
        take, at = carve(end_l1)
        yT = hT_flat.rearrange("p (k t) -> p k t", k=KE)
        uT = take(KE, T)
        lnbc1 = take(2, D)
        take, at = carve(arena + KE * T)
        zT = take(KE, T)
        ya = take(2, 2, T)
        yb = take(2, 2, T)
        assert at[0] <= end_l1

        take, at = carve(arena)
        hn = take(2, D)
        qaT = take(4, T)
        kaT = take(4, T)
        qbT = take(4, T)
        kbT = take(4, T)
        va = take(2, 512)
        vb = take(2, 512)
        ga = take(2, D)
        gb = take(2, D)
        qk_sb = take(2, 512)
        qk_sq = take(2, 512)
        toe = take(NH2, T)
        cst = take(6, P)
        pa = take(2, 384)
        pat = take(2, 384)
        az = take(2, 384)
        lk = take(2, 384)
        oaT = take(4, T)
        obT = take(4, T)
        mixed = take(2, D)
        mT = take(KD, T)
        take, at = carve(arena + 2 * D)
        fT = take(KF, T)
        cg = take(4, 2, T)
        st2 = small[:, 64:128]

        def slot(i, *shape):
            v = ring[:, i % SLOTS, 0:int(np.prod(shape))]
            names = " ".join("abcd"[:len(shape)])
            return v.rearrange(f"p ({names}) -> p {names}", **{"abcd"[j]: shape[j] for j in range(len(shape))})

        def column(name, i=0):
            r = VROW[name] + i
            return colv[:, r // P, r % P:r % P + 1]

        loads, load_no = [], {}

        def load(key, src, shape, freed, parts=None):
            load_no[key] = len(loads)
            loads.append((src, shape, freed, parts))

        def ktiles(w):
            return w.rearrange("(k p) n -> p k n", p=P)

        def mod_loads(l):
            for ct in range(6):
                load(("mod", l, ct), ktiles(a["w_mod"][l])[:, :, ct * 512:(ct + 1) * 512], (KD, 512), ("mod_mm", (l, ct)))

        mod_loads(0)
        w_in0 = ktiles(a["mla_w_in"][0])
        load("head_in", w_in0[:, :, 0:HEAD_IN], (KD, HEAD_IN), ("head_mm", NTT - 1))
        for ct in range(4):
            load(("gate", ct), w_in0[:, :, HEAD_IN + ct * 512:HEAD_IN + (ct + 1) * 512], (KD, 512), ("gate_mm", 4 * ct + 3))
        for hf in range(2):
            load(("uq", hf), ktiles(a["mla_w_uq"][0])[:, :, hf * 1536:(hf + 1) * 1536], (2, 1536), ("q_mm", 8 * hf + 7))
        w_o0 = ktiles(a["mla_w_out"][0])
        for n in range(2):
            for kh in range(2):
                load(("out0", n, kh), w_o0[:, kh * 8:kh * 8 + 8, n * 512:(n + 1) * 512], (KD, 512), ("out0_k", (n, kh)))
        mod_loads(1)
        w_in1 = ktiles(a["s5_w_in"][0])
        for ct in range(8):
            load(("s5in", ct), w_in1[:, :, ct * 512:(ct + 1) * 512], (KD, 512), ("s5in_mm", 4 * ct + 3))
        first_glu = len(loads)
        w_glu = ktiles(a["s5_w_glu"][0])
        for ct in range(4):
            for half in range(2):
                for kh in range(2):
                    c0 = half * E + ct * 512
                    load(("glu", ct, half, kh), w_glu[:, kh * 8:kh * 8 + 8, c0:c0 + 512], (KD, 512),
                         ("glu_k", (ct, half, kh)))
        w_o1 = ktiles(a["s5_w_out"][0])
        for n in range(2):
            for kh in range(2):
                load(("out1", n, kh), w_o1[:, kh * 8:kh * 8 + 8, n * 512:(n + 1) * 512], (KD, 512), ("out1_k", (n, kh)))
        w_in2 = ktiles(a["w_in_2"][0])
        for ct in range(10):
            load(("in2", ct), w_in2[:, :, ct * 512:(ct + 1) * 512], (KD, 512), ("in2_mm", (ct, 1)))
        for b in range(2):
            w = ktiles(a["w_branch_" + "ab"[b] + "_2"][0])
            load(("branch", b), w, (4, D), ("branch_mm", (b, 1, 1)))
        w_o2 = ktiles(a["w_out_2"][0])
        for n in range(2):
            load(("out2", n), w_o2[:, :, n * 512:(n + 1) * 512], (KD, 512), ("out2_mm", (n, 1)))
        w_up = ktiles(a["w_ffn_up_2"][0])
        for f in range(KF // 2):
            parts = [w_up[:, :, half * FF + f * 256:half * FF + (f + 1) * 256] for half in range(2)]
            load(("up", f), None, (2, KD, 256), ("up_mm", (f, 1)), parts)
        w_dn = ktiles(a["w_ffn_down_2"][0])
        for n in range(2):
            for kc in range(3):
                k0, k1 = 8 * kc, min(8 * kc + 8, KF)
                load(("down", n, kc), w_dn[:, k0:k1, n * 512:(n + 1) * 512], (k1 - k0, 512), ("down_k", (n, kc)))

        def weights(eng, key, shape):
            i = load_no[key]
            eng.wait_ge(*S.at(f"slot{i % SLOTS}", i))
            return slot(i, *shape)

        users = []

        def bank(pe, key, freed):
            n = len(users)
            if n >= 8:
                for f in users[n - 8]:
                    pe.wait_ge(*S.at(*f))
            users.append(freed)
            places[key] = n % 8
            return banks[n % 8]

        def at_bank(*key):
            return banks[places.get(key, 0)]

        def modulate_views(l, k, c):
            i = at_bank("xT", l, k)[:, c * T:(c + 1) * T]
            if l == 0:
                return hT[:, k, c * T:(c + 1) * T], i
            return hT[:, k, :].rearrange("p (j s c) -> p s c j", j=L, s=2)[:, 1 - c], i.rearrange("p (c j) -> p c j", j=L)

        @block.tensor
        def _(pe):
            def mm(o, l, r, start, stop, free=False):
                return nc.tensor.matmul(o, l, r, start=start, stop=stop, skip_group_check=free)

            def tr(o, i, n=P):
                return nc.tensor.transpose(o, i, ident[0:n, 0:n])

            pe.wait_ge(*S.at("consts", "first"))
            pe.wait_ge(*S.at("cond_silu"))
            b = bank(pe, ("colv",), [("colv",)])
            for i in range(3):
                n = min(P, NVROW - i * P)
                last = tr(b[:, i * P:i * P + n], vrows[0:n, i, :], n)
            last.then_inc(*S.up("colv_mm"))
            pe.wait_ge(*S.at("condT"))

            def modulation(l):
                for ct in range(6):
                    w = weights(pe, ("mod", l, ct), (KD, 512))
                    b = bank(pe, ("mod", l, ct), [("mod_row", (l, ct))])
                    for k in range(KD):
                        last = mm(b[0:2, :], condT.rearrange("p (c k) -> p c k", c=2)[:, :, k], w[:, k, :], k == 0, k == KD - 1)
                    last.then_inc(*S.up("mod_mm", (l, ct)))
                    pe.wait_ge(*S.at("mod_row", (l, ct)))
                    row = modrow[0:2, ct % 2, :]
                    if ct < 4:
                        b = bank(pe, ("modT", l, ct), [("shsc", (l, ct))])
                        for i in range(4):
                            last = tr(b[:, 2 * i:2 * i + 2], row[:, i * P:(i + 1) * P], 2)
                        last.then_inc(*S.up("modT_mm", (l, ct)))
                    else:
                        for c in range(2 - l):
                            b = bank(pe, ("gtb", l, ct, c), [("gtb", (l, ct, c))])
                            mm(b, sel[0:2, c, :], row, True, True).then_inc(*S.up("gtb_mm", (l, ct, c)))

            def x_transposes(l):
                for k in range(KD):
                    b = bank(pe, ("xT", l, k), [("hT_v" if k % 2 == 0 else "hT_a", (l, k))])
                    for t in range(NTT):
                        pe.wait_ge(*S.at(*(("x_in%d" % t,) if l == 0 else ("x1", t))))
                        last = tr(b[:, t * P:(t + 1) * P], x[:, t, k * P:(k + 1) * P])
                    last.then_inc(*S.up("xT_mm", (l, k)))

            modulation(0)
            x_transposes(0)
            w = weights(pe, "head_in", (KD, HEAD_IN))
            for k in range(KD):
                pe.wait_ge(*S.at("hT_v" if k % 2 == 0 else "hT_a", (0, k)))
            for t in range(NTT):
                b = bank(pe, ("head", t), [("ckv", t), ("qn", t), ("kr", t)])
                for k in range(KD):
                    last = mm(b[:, 0:HEAD_IN], hT[:, k, t * P:(t + 1) * P], w[:, k, :], k == 0, k == KD - 1)
                last.then_inc(*S.up("head_mm", t))
            for ct in range(4):
                w = weights(pe, ("gate", ct), (KD, 512))
                for f in range(4):
                    b = bank(pe, ("gate", 4 * ct + f), [("gate", 4 * ct + f)])
                    for k in range(KD):
                        last = mm(b, w[:, k, f * P:(f + 1) * P], hT[:, k, :], k == 0, k == KD - 1)
                    last.then_inc(*S.up("gate_mm", 4 * ct + f))
            for i in range(2):
                b = bank(pe, ("qnT", i), [("qnT", i)])
                for t in range(NTT):
                    pe.wait_ge(*S.at("qn", t))
                    last = tr(b[:, t * P:(t + 1) * P], qn[:, t, i * P:(i + 1) * P])
                last.then_inc(*S.up("qnT_mm", i))
            b = bank(pe, ("ckvT",), [("ckvT",)])
            for t in range(NTT):
                pe.wait_ge(*S.at("ckv", t))
                last = tr(b[:, t * P:(t + 1) * P], ckv[:, t, :])
            last.then_inc(*S.up("ckvT_mm"))
            b = bank(pe, ("krT",), [("krT",)])
            for t in range(NTT):
                pe.wait_ge(*S.at("kr", t))
                if t < 2:
                    pe.wait_ge(*S.at("kr_pos", t))
                last = tr(b[:, t * P:(t + 1) * P], kr[:, t, :, :].rearrange("p a n -> p (a n)"))
            last.then_inc(*S.up("krT_mm"))
            for i in range(2):
                pe.wait_ge(*S.at("qnT", i))
            pe.wait_ge(*S.at("ckvT"))
            pe.wait_ge(*S.at("krT"))
            pe.wait_ge(*S.at("second"))

            def q_rope(hf):
                w = weights(pe, ("uq", hf), (2, 1536)).rearrange("p k (h n) -> p k h n", n=NOPE + ROPE)
                for t in range(NTT):
                    b = bank(pe, ("qrope", hf, t), [("qrf", (hf, t))] + ([("qrp_a", (hf, t)), ("qrp_b", (hf, t))] if t < 2 else []))
                    for k in range(2):
                        last = mm(b, qnT[:, k, t * P:(t + 1) * P], w[:, k, :, NOPE:], k == 0, k == 1)
                    last.then_inc(*S.up("qrope_mm", (hf, t)))
                    bf = bank(pe, ("qrfT", hf, t), [("qrfT", (hf, t))])
                    pe.wait_ge(*S.at("qrf", (hf, t)))
                    for i in range(4):
                        last = tr(bf[:, i * P:(i + 1) * P], qrf[:, t % 2, i * P:(i + 1) * P])
                    last.then_inc(*S.up("qrfT_mm", (hf, t)))
                    if t < 2:
                        bp = bank(pe, ("qrpT", hf, t), [("qrpT", (hf, t))])
                        pe.wait_ge(*S.at("qrp", (hf, t)))
                        for i in range(4):
                            last = tr(bp[:, i * P:(i + 1) * P], qrp[:, i * P:(i + 1) * P])
                        last.then_inc(*S.up("qrpT_mm", (hf, t)))

            def qk_head(h):
                w = weights(pe, ("uq", h // 8), (2, 1536))
                b = bank(pe, ("q", h), [("qT", h)])
                c = (h % 8) * (NOPE + ROPE)
                for k in range(2):
                    last = mm(b, w[:, k, c:c + NOPE], qnT[:, k, :], k == 0, k == 1)
                last.then_inc(*S.up("q_mm", h))
                b = bank(pe, ("k", h), [("kT", h)])
                mm(b, wukv[:, 0, h * P:(h + 1) * P], ckvT, True, True).then_inc(*S.up("k_mm", h))

            def scores(h):
                hf, r = h // 8, 64 * (h % 2)
                pair = (h % 8) // 2
                pe.wait_ge(*S.at("qT", h))
                pe.wait_ge(*S.at("kT", h))
                for t in range(NTT):
                    pe.wait_ge(*S.at("qrfT", (hf, t)))
                for t in range(2):
                    pe.wait_ge(*S.at("qrpT", (hf, t)))
                q, kk = qT[:, h % 2, :], kT[:, h % 2, :]
                for t in range(2):
                    b = bank(pe, ("s", h, t), [("p", (h, t))])
                    mm(b, q[:, t * P:(t + 1) * P], kk, True, False, True)
                    mm(b[:, 0:T], qrpT[r:r + 64, pair, t * P:(t + 1) * P], krT[r:r + 64, 0:T], False, False, True)
                    last = mm(b[:, T:2 * T], qrfT[r:r + 64, pair, t * P:(t + 1) * P], krT[r:r + 64, T:2 * T], False, True, True)
                    last.then_inc(*S.up("s_mm", (h, t)))
                b = bank(pe, ("s", h, 2), [("p", (h, 3))])
                for t in range(2, 4):
                    o = b[:, (t - 2) * T:(t - 1) * T]
                    mm(o, q[:, t * P:(t + 1) * P], kk[:, T:2 * T], t == 2, False, True)
                    last = mm(o, qrfT[r:r + 64, pair, t * P:(t + 1) * P], krT[r:r + 64, T:2 * T], False, t == 3, True)
                last.then_inc(*S.up("s_mm", (h, 2)))

            def values(h):
                for i in range(2):
                    b = bank(pe, ("pt", h, i), [("pt", (h, i))])
                    for kk in range(2):
                        for t in range(2):
                            pe.wait_ge(*S.at("pn", (h, t)))
                            last = tr(b[:, kk * T + t * P:kk * T + (t + 1) * P], pl[:, h % 2, t, (2 * i + kk) * P:(2 * i + kk + 1) * P])
                    last.then_inc(*S.up("pt_mm", (h, i)))
                b = bank(pe, ("pt", h, 2), [("pt", (h, 2))])
                for kk in range(2):
                    for t in range(2):
                        pe.wait_ge(*S.at("pn", (h, 2 + t)))
                        last = tr(b[:, kk * T + t * P:kk * T + (t + 1) * P], pc[:, h % 2, t, kk * P:(kk + 1) * P])
                last.then_inc(*S.up("pt_mm", (h, 2)))
                b = bank(pe, ("ol", h), [("olT", h)])
                for kk in range(4):
                    pe.wait_ge(*S.at("pt", (h, kk // 2)))
                    mm(b[:, 0:T], ckv[:, kk, :], PT[:, h % 2, kk // 2, (kk % 2) * T:(kk % 2 + 1) * T], kk == 0, False, True)
                pe.wait_ge(*S.at("pt", (h, 2)))
                for kk in range(2):
                    last = mm(b[:, T:2 * T], ckv[:, 2 + kk, :], PT[:, h % 2, 2, kk * T:(kk + 1) * T], False, kk == 1, True)
                last.then_inc(*S.up("ol_mm", h))

            def value_up(h):
                pe.wait_ge(*S.at("olT", h))
                b = bank(pe, ("v", h), [("vg", h)])
                mm(b, wukv[:, 1, h * P:(h + 1) * P], olT, True, True).then_inc(*S.up("v_mm", h))

            for h in range(H + 2):
                if h % 8 == 0 and h < H:
                    if h:
                        pass
                    q_rope(h // 8)
                if h < H:
                    qk_head(h)
                if 1 <= h <= H:
                    values(h - 1)
                if h >= 2:
                    value_up(h - 2)
                if h < H:
                    scores(h)

            for n in range(2):
                bs = []
                for kh in range(2):
                    w = weights(pe, ("out0", n, kh), (KD, 512))
                    for t in range(NTT):
                        if kh == 0:
                            bs.append(bank(pe, ("out0", n, t), [("res0_a", (n, t))]))
                        for k in range(8):
                            pe.wait_ge(*S.at("vg", kh * 8 + k))
                            last = mm(bs[t], gT[:, kh * 8 + k, t * P:(t + 1) * P], w[:, k, :], kh == 0 and k == 0, kh == 1 and k == 7)
                        if kh == 1:
                            last.then_inc(*S.up("out0_k" if t == 3 else "out0_mm", (n, 1) if t == 3 else (n, t)))
                    if kh == 0:
                        last.then_inc(*S.up("out0_k", (n, kh)))

            modulation(1)
            pe.wait_ge(*S.at("lam_ready"))
            b = bank(pe, ("lamT",), [("lamT",)])
            for i in range(4):
                last = tr(b[:, i * P:(i + 1) * P], sc_a[:, 10 + i, :])
            last.then_inc(*S.up("lamT_mm"))
            x_transposes(1)
            for k in range(KD):
                pe.wait_ge(*S.at("hT_v" if k % 2 == 0 else "hT_a", (1, k)))
            for ct in range(8):
                w = weights(pe, ("s5in", ct), (KD, 512))
                for f in range(4):
                    b = bank(pe, ("s5in", 4 * ct + f), [("u_sb" if ct < 4 else "gs", 4 * ct + f)])
                    for k in range(KD):
                        if ct < 4:
                            last = mm(b, w[:, k, f * P:(f + 1) * P], hT[:, k, :], k == 0, k == KD - 1)
                        else:
                            r = hT[:, k, :].rearrange("p (j s c) -> p j s c", j=L, s=2)[:, :, 1, :]
                            last = mm(b[:, 0:T], w[:, k, f * P:(f + 1) * P], r, k == 0, k == KD - 1)
                    last.then_inc(*S.up("s5in_mm", 4 * ct + f))

            for q in range(NQ):
                pe.wait_ge(*S.at("cn", q))
                for ri in range(2):
                    b = bank(pe, ("cT", q, ri), [("c0", (q, ri))])
                    for dr in range(2):
                        for bk in range(2):
                            last = tr(b[:, (2 * dr + bk) * P:(2 * dr + bk + 1) * P], cn[:, ri, dr, bk * P:(bk + 1) * P] if False else cn[:, ri, dr, bk, :])
                    last.then_inc(*S.up("cT_mm", (q, ri)))
                pe.wait_ge(*S.at("mc", (q, 0)))
                pe.wait_ge(*S.at("mc", (q, 1)))
                pe.wait_ge(*S.at("bbd", q))
                for half in range(2):
                    b = bank(pe, ("kern", q, half), [("kt", (q, half))])
                    for gi in range(8):
                        gg = 8 * half + gi
                        o = b[32 * (gg % 4):32 * (gg % 4) + 32, (gi // 4) * 240:(gi // 4 + 1) * 240]
                        for dr, c0, e0 in ((1, 0, 1), (0, 112, 0)):
                            for ri in range(2):
                                last = mm(o[:, c0:c0 + 128], bbd[:, dr, gg, ri, :],
                                          mc[:, dr, gg, ri, e0:e0 + 8, :].rearrange("p j s -> p (j s)"),
                                          dr == 1 and ri == 0, dr == 0 and ri == 1, True)
                    last.then_inc(*S.up("kern_mm", (q, half)))
                pe.wait_ge(*S.at("u_load", q))
                for s4 in range(4):
                    for dr in range(2):
                        for ri in range(2):
                            b = bank(pe, ("mbT", q, s4, dr, ri), [("mbt", (q, s4, dr, ri))])
                            pe.wait_ge(*S.at("mb", (q, s4, dr)))
                            for i in range(4):
                                last = tr(b[:, i * P:(i + 1) * P], mb[:, dr, i, ri, :, :].rearrange("p j s -> p (j s)"))
                            last.then_inc(*S.up("mbT_mm", (q, s4, dr, ri)))
                    for dr in range(2):
                        b = bank(pe, ("st", q, s4, dr), [("xs", (q, s4, dr))])
                        for ri in range(2):
                            pe.wait_ge(*S.at("mbt", (q, s4, dr, ri)))
                            for i in range(4):
                                for par in range(2):
                                    last = mm(b[64 * par:64 * par + 64, (4 * ri + i) * NC:(4 * ri + i + 1) * NC],
                                              mbt[:, dr, ri, i, 64 * par:64 * par + 64], u_sb[:, par, 4 * s4 + i, :],
                                              ri == 0 and i == 0, ri == 1 and i == 3, True)
                        last.then_inc(*S.up("st_mm", (q, s4, dr)))
                pe.wait_ge(*S.at("t_load", q))
                pe.wait_ge(*S.at("scan", (q, NC - 1)))
                for par in range(2):
                    b = bank(pe, ("y", q, par), [("y", (q, par))])
                    for gg in range(GQ):
                        mm(b[:, gg * NCL:(gg + 1) * NCL], tt_sb[:, par, gg, :], u_sb[:, par, gg, NCL:NC], gg == 0, False, True)
                    r = slice(64 * par, 64 * par + 64)
                    for gg in range(GQ):
                        for dr in range(2):
                            for ri in range(2):
                                st = xs[r, NCL - 1:NC - 1, dr, ri, gg] if dr == 0 else xs[r, NC - 2:NCL - 2:-1, dr, ri, gg]
                                e0 = 1 - dr
                                last = mm(b[:, gg * NCL:(gg + 1) * NCL],
                                          mc[r, dr, gg, ri, e0:e0 + 8, :].rearrange("p j s -> p (j s)"), st,
                                          False, gg == GQ - 1 and dr == 1 and ri == 1, True)
                    last.then_inc(*S.up("y_mm", (q, par)))

            for k in range(KE):
                pe.wait_ge(*S.at("gelu", k))
            for ct in range(4):
                for half in range(2):
                    bs = []
                    for kh in range(2):
                        w = weights(pe, ("glu", ct, half, kh), (KD, 512))
                        for f in range(4):
                            if kh == 0 and f % 2 == 0:
                                bs.append(bank(pe, ("glu", ct, half, f // 2), [("glu_a" if half == 0 else "glu_b", (ct, 2 * (f // 2) + 1))]))
                            for k in range(8):
                                last = mm(bs[f // 2][:, (f % 2) * T:(f % 2 + 1) * T], w[:, k, f * P:(f + 1) * P], yT[:, kh * 8 + k, :],
                                          kh == 0 and k == 0 and f % 2 == 0, kh == 1 and k == 7 and f % 2 == 1, True)
                        last.then_inc(*S.up("glu_k", (ct, half, kh)))
            for n in range(2):
                bs = []
                for kh in range(2):
                    w = weights(pe, ("out1", n, kh), (KD, 512))
                    for t in range(2):
                        if kh == 0:
                            bs.append(bank(pe, ("out1", n, t), [("res1_a", (n, t))]))
                        for k in range(8):
                            pe.wait_ge(*S.at("z", kh * 8 + k))
                            last = mm(bs[t], zT[:, kh * 8 + k, t * P:(t + 1) * P], w[:, k, :], kh == 0 and k == 0, kh == 1 and k == 7)
                        if kh == 1 and t == 0:
                            last.then_inc(*S.up("out1_mm", (n, t)))
                    last.then_inc(*S.up("out1_k", (n, kh)))

            def hn_transposes(i):
                for k2 in range(KD // 2):
                    b = bank(pe, ("hnT", i, k2), [("hnT", (i, 2 * k2 + 1))])
                    for k in range(2):
                        for t in range(2):
                            pe.wait_ge(*S.at("hn", (i, t)))
                            last = tr(b[:, k * T + t * P:k * T + (t + 1) * P], hn[:, t, (2 * k2 + k) * P:(2 * k2 + k + 1) * P])
                    last.then_inc(*S.up("hnT_mm", (i, k2)))
                for k in range(KD):
                    pe.wait_ge(*S.at("hnT", (i, k)))

            h2 = hT_flat[:, 0:KD * T].rearrange("p (k t) -> p k t", k=KD)
            hn_transposes(0)
            pe.wait_ge(*S.at("consts2"))

            def project(ct):
                w = weights(pe, ("in2", ct), (KD, 512))
                for t in range(2):
                    freed = {0: "qk_n", 1: "qk_n", 2: "va", 3: "qk_n", 4: "qk_n", 5: "vb"}.get(ct, "gates")
                    b = bank(pe, ("in2", ct, t), [(freed, (ct, t))])
                    for k in range(KD):
                        last = mm(b, h2[:, k, t * P:(t + 1) * P], w[:, k, :], k == 0, k == KD - 1)
                    last.then_inc(*S.up("in2_mm", (ct, t)))

            def qk_transposes(ct):
                for i2 in range(2):
                    b = bank(pe, ("qkT", ct, i2), [("qkT", (ct, i2))])
                    for i in range(2):
                        for t in range(2):
                            pe.wait_ge(*S.at("qk_n", (ct, t)))
                            last = tr(b[:, i * T + t * P:i * T + (t + 1) * P], qk_sb[:, t, (2 * i2 + i) * P:(2 * i2 + i + 1) * P])
                    last.then_inc(*S.up("qkT_mm", (ct, i2)))

            for ct in range(10):
                project(ct)
                if ct in (0, 1, 3, 4):
                    qk_transposes(ct)
            for ct in (0, 1, 3, 4):
                for i in range(2):
                    pe.wait_ge(*S.at("qkT", (ct, i)))

            def score_a(h):
                r, pair = 64 * (h % 2), h // 2
                b = bank(pe, ("sa", h), [("pa", (h, 1))])
                mm(b[:, P:3 * P], cst[:, 0, :], toe[:, h, :], True, False, True)
                mm(b[:, 0:P], cst[:, 0, :], toe[:, h, P:2 * P], False, False, True)
                mm(b[:, 0:P], ident, cst[:, 1, :], False, False, True)
                mm(b[:, 2 * P:3 * P], ident, cst[:, 1, :], False, False, True)
                mm(b[:, 0:P], qaT[r:r + 64, pair, 0:P], kaT[r:r + 64, pair, 0:P], False, False, True)
                last = mm(b[:, P:3 * P], qaT[r:r + 64, pair, P:T], kaT[r:r + 64, pair, :], False, True, True)
                last.then_inc(*S.up("sa_mm", h))

            def pt_a(h):
                b = bank(pe, ("pat", h), [("pat", h)])
                pe.wait_ge(*S.at("pan", (h, 0)))
                pe.wait_ge(*S.at("pan", (h, 1)))
                for i in range(3):
                    last = tr(b[:, i * P:(i + 1) * P], pa[:, h % 2, i * P:(i + 1) * P])
                last.then_inc(*S.up("pat_mm", h))

            attended = {}

            def attend(name, h, v, w, ready):
                r = 64 * (h % 2)
                if h % 2 == 0:
                    attended[name] = bank(pe, (name, h // 2), [(name, h // 2)])
                b = attended[name]
                pe.wait_ge(*S.at(*ready))
                mm(b[r:r + 64, 0:T], v[:, 0, h * HD:(h + 1) * HD], w[:, 0:T], True, False, True)
                last = mm(b[r:r + 64, P:T], v[:, 1, h * HD:(h + 1) * HD], w[:, T:3 * P], False, True, True)
                last.then_inc(*S.up(name + "_mm", h))

            zb = {}

            def score_b(h):
                r, pair = 64 * (h % 2), h // 2
                b = zb[h] = bank(pe, ("z", h), [("wb", h)])
                mm(b[:, 0:T], kbT[r:r + 64, pair, 0:P], qbT[r:r + 64, pair, :], True, False, True)
                last = mm(b[:, T:3 * P], kbT[r:r + 64, pair, P:T], qbT[r:r + 64, pair, P:T], False, False, True)
                last.then_inc(*S.up("z_mm", h))

            def after_b(h):
                b = zb[h]
                pe.wait_ge(*S.at("lk", h))
                w = lk[:, h % 2, :]
                mm(b[:, 0:T], cst[:, 3, :], w[:, 0:T], False, False, True)
                mm(b[:, P:T], cst[:, 4, :], w[:, T:3 * P], False, False, True)
                mm(b[:, T:3 * P], cst[:, 3, :], w[:, T:3 * P], False, False, True)
                mm(b[:, 0:P], ident, cst[:, 5, :], False, False, True)
                last = mm(b[:, T:3 * P], ident, cst[:, 5, :], False, True, True)
                last.then_inc(*S.up("zl_mm", h))

            pe.wait_ge(*S.at("va", (2, 1)))
            pe.wait_ge(*S.at("vb", (5, 1)))
            for h in range(NH2 + 1):
                if h < NH2:
                    score_a(h)
                    score_b(h)
                if h >= 1:
                    pt_a(h - 1)
                    attend("oa", h - 1, va, pat[:, (h - 1) % 2, :], ("pat", h - 1))
                    after_b(h - 1)
                    attend("ob", h - 1, vb, az[:, (h - 1) % 2, :], ("wb", h - 1))

            for k in range(4):
                pe.wait_ge(*S.at("oa", k))
                pe.wait_ge(*S.at("ob", k))
            bs = {}
            for br in range(2):
                w = weights(pe, ("branch", br), (4, D))
                for n in range(2):
                    for t in range(2):
                        b = bank(pe, ("branch", br, n, t), [("mix", (br, n, t))])
                        for k in range(4):
                            last = mm(b, (oaT if br == 0 else obT)[:, k, t * P:(t + 1) * P], w[:, k, n * 512:(n + 1) * 512], k == 0, k == 3)
                        last.then_inc(*S.up("branch_mm", (br, n, t)))
            for k2 in range(KD // 2):
                b = bank(pe, ("mT", k2), [("mT", k2)])
                for k in range(2):
                    kk = 2 * k2 + k
                    for t in range(2):
                        pe.wait_ge(*S.at("mix", (1, kk // 4, t)))
                        last = tr(b[:, k * T + t * P:k * T + (t + 1) * P], mixed[:, t, kk * P:(kk + 1) * P])
                last.then_inc(*S.up("mT_mm", k2))
            for n in range(2):
                w = weights(pe, ("out2", n), (KD, 512))
                for t in range(2):
                    b = bank(pe, ("out2", n, t), [("res2", (n, t))])
                    for k in range(KD):
                        pe.wait_ge(*S.at("mT", k // 2))
                        last = mm(b, mT[:, k, t * P:(t + 1) * P], w[:, k, :], k == 0, k == KD - 1)
                    last.then_inc(*S.up("out2_mm", (n, t)))
            hn_transposes(1)
            for f in range(KF // 2):
                w = weights(pe, ("up", f), (2, KD, 256))
                for half in range(2):
                    b = bank(pe, ("up", f, half), [("conv", (f, half, 1))])
                    for i in range(2):
                        for k in range(KD):
                            last = mm(b[:, i * T:(i + 1) * T], w[:, half, k, i * P:(i + 1) * P], h2[:, k, :],
                                      i == 0 and k == 0, i == 1 and k == KD - 1, True)
                    last.then_inc(*S.up("up_mm", (f, half)))
            for n in range(2):
                bs = []
                for kc in range(3):
                    k0, k1 = 8 * kc, min(8 * kc + 8, KF)
                    w = weights(pe, ("down", n, kc), (k1 - k0, 512))
                    for t in range(2):
                        if kc == 0:
                            bs.append(bank(pe, ("down", n, t), [("res3", (n, t))]))
                        for k in range(k0, k1):
                            pe.wait_ge(*S.at("ffn", k))
                            last = mm(bs[t], fT[:, k, t * P:(t + 1) * P], w[:, k - k0, :], k == 0, k == KF - 1)
                        if kc == 2 and t == 0:
                            last.then_inc(*S.up("down_mm", (n, t)))
                    last.then_inc(*S.up("down_k", (n, kc)))

        @block.scalar
        def _(act):
            A = nc.scalar.activation

            first = [(ident, a["c_ident"][0]), (sel[0:2, :, :], a["c_sel"])]
            rows = [("q_norm", a["mla_q_norm"]), ("s5_d", a["s5_d"]), ("b_glu", a["s5_b_glu"]), ("norm1", a["norm1_g_2"]),
                    ("norm2", a["norm2_g_2"]), ("conv_b", a["ffn_conv_b_2"]),
                    ("conv_w0", a["ffn_conv_w_2"][0, 0:1]), ("conv_w1", a["ffn_conv_w_2"][0, 1:2]), ("conv_w2", a["ffn_conv_w_2"][0, 2:3])]

            def put_rows(row, n, src):
                done = 0
                while done < n:
                    r = row + done
                    m = min(n - done, P - r % P)
                    first.append((vrows[r % P:r % P + m, r // P, :], src[done:done + m, :]))
                    done += m
            for name, v in rows:
                put_rows(VROW[name], VECTORS[name], v[0, :].rearrange("(r n) -> r n", n=P))
            for name, v in (("q_gain", a["q_norm_g_2"]), ("k_gain", a["k_norm_g_2"])):
                r = VROW[name]
                for i in range(2):
                    first.append((vrows[r % P:r % P + 1, r // P, i * HD:(i + 1) * HD], v))
            put_rows(VROW["cond"], KD, a["c"][0, :].rearrange("(r n) -> r n", n=P))
            put_rows(VROW["cond"] + KD, KD, a["c_ctx"].rearrange("(r n) -> r n", n=P))
            for o, i in first:
                act.dma_start(o, i).then_inc(*S.up("consts", "first", by=16))
            for t in range(NTT):
                src = a["x"] if t < 2 else a["ctx"]
                act.dma_start(x[:, t, :], src[0, (t % 2) * P:(t % 2 + 1) * P, :]).then_inc(*S.up("x_in%d" % t, by=16))
            second = [(kvg, dview(a["mla_kv_norm"], 0, (0, P), (1, KVR))), (wukv[:, 0, :], a["mla_w_uk"][0].rearrange("c h d -> c (h d)")),
                      (wukv[:, 1, :], a["mla_w_uv"][0].rearrange("c h d -> c (h d)"))]
            for t in range(2):
                for i in range(2):
                    second.append((rope[:, i, t, :], a["c_rope"][i, t * P:(t + 1) * P, :]))
            for o, i in second:
                act.dma_start(o, i).then_inc(*S.up("second", by=16))
            act.wait_ge(*S.at("consts", "first"))
            A(vrows[0:2 * KD, 0, :], vrows[0:2 * KD, 0, :], ACT.Silu).then_inc(*S.up("cond_silu"))

            def gate_rows(l):
                for ct in range(4, 6):
                    for c in range(2 - l):
                        act.wait_ge(*S.at("gtb_mm", (l, ct, c)))
                        if l == 1:
                            act.wait_ge(*S.at("res0", (1, 3)))
                        A(gtb[:, c, (ct - 4) * 512:(ct - 3) * 512], at_bank("gtb", l, ct, c), ACT.Copy).then_inc(*S.up("gtb", (l, ct, c)))

            def modulated(l):
                for k in range(1, KD, 2):
                    act.wait_ge(*S.at("xT_mm", (l, k)))
                    act.wait_ge(*S.at("shsc", (l, 3)))
                    for c in range(2):
                        o, i = modulate_views(l, k, c)
                        ins = A(o, i, ACT.Identity, bias=shsc[:, k, c:c + 1], scale=shsc[:, KD + k, c:c + 1])
                    ins.then_inc(*S.up("hT_a", (l, k)))

            gate_rows(0)
            modulated(0)
            for t in range(NTT):
                act.wait_ge(*S.at("head_mm", t))
                if t:
                    act.wait_ge(*S.at("lat_ss", t - 1))
                b = at_bank("head", t)
                A(sq[:, 0:QR], b[:, 0:QR], ACT.Square, accum_out=st0[:, t:t + 1]).then_inc(*S.up("lat_sq", t))
                act.wait_ge(*S.at("lat_sq", t))
                A(sq[:, 0:KVR], b[:, QR:QR + KVR], ACT.Square, accum_out=st0[:, 4 + t:5 + t]).then_inc(*S.up("lat_ss", t))
            act.wait_ge(*S.at("lat_ms"))
            A(st0[:, 16:24], st0[:, 8:16], ACT.Sqrt).then_inc(*S.up("lat_rms"))
            for f in range(H):
                act.wait_ge(*S.at("gate_mm", f))
                A(gT[:, f, :], at_bank("gate", f), ACT.Silu).then_inc(*S.up("gate", f))
            for i in range(2):
                act.wait_ge(*S.at("qnT_mm", i))
                act.wait_ge(*S.at("colv"))
                A(qnT[:, i, :], at_bank("qnT", i), ACT.Copy, scale=column("q_norm", i)).then_inc(*S.up("qnT", i))
            act.wait_ge(*S.at("ckvT_mm"))
            A(ckvT, at_bank("ckvT"), ACT.Copy).then_inc(*S.up("ckvT"))

            def q_rope(hf):
                for t in range(NTT):
                    act.wait_ge(*S.at("qrope_mm", (hf, t)))
                    if hf or t >= 2:
                        act.wait_ge(*S.at("qrfT_mm", (hf, t - 2) if t >= 2 else (hf - 1, t + 2)))
                    A(qrf[:, t % 2, :], at_bank("qrope", hf, t), ACT.Copy).then_inc(*S.up("qrf", (hf, t)))
                    act.wait_ge(*S.at("qrfT_mm", (hf, t)))
                    if hf:
                        act.wait_ge(*S.at("s_mm", (7, 2)))
                    A(qrfT[:, :, t * P:(t + 1) * P], at_bank("qrfT", hf, t).rearrange("p (i t) -> p i t", i=4), ACT.Copy).then_inc(*S.up("qrfT", (hf, t)))
                    if t < 2:
                        act.wait_ge(*S.at("qrpT_mm", (hf, t)))
                        A(qrpT[:, :, t * P:(t + 1) * P], at_bank("qrpT", hf, t).rearrange("p (i t) -> p i t", i=4), ACT.Copy).then_inc(*S.up("qrpT", (hf, t)))

            def head(h):
                act.wait_ge(*S.at("q_mm", h))
                if h >= 2:
                    act.wait_ge(*S.at("s_mm", (h - 2, 2)))
                A(qT[:, h % 2, :], at_bank("q", h), ACT.Copy).then_inc(*S.up("qT", h))

            def softmax(h):
                for t in range(NTT):
                    act.wait_ge(*S.at("nmax", h))
                    b = at_bank("s", h, min(t, 2))
                    i = b if t < 2 else b[:, (t - 2) * T:(t - 1) * T]
                    o = pl[:, h % 2, t, :] if t < 2 else pc[:, h % 2, t - 2, :]
                    if h >= 2:
                        act.wait_ge(*S.at("pt_mm", (h - 2, 2)))
                    act.wait_ge(*S.at("gate_mm", H - 1))
                    A(o, i, ACT.Exp, bias=st0[:, 24 + 4 * (h % 2) + t:25 + 4 * (h % 2) + t], scale=MLA_SCALE,
                            accum_out=st0[:, 32 + 4 * (h % 2) + t:33 + 4 * (h % 2) + t]).then_inc(*S.up("p", (h, t)))

            for h in range(H + 1):
                if h < H:
                    if h % 8 == 0:
                        q_rope(h // 8)
                    head(h)
                if h >= 1:
                    g = h - 1
                    act.wait_ge(*S.at("pt_mm", (g, 2)))
                    A(PT[:, g % 2, 2, :], at_bank("pt", g, 2), ACT.Copy).then_inc(*S.up("pt2", g))
                    act.wait_ge(*S.at("ol_mm", g))
                    if g >= 1:
                        act.wait_ge(*S.at("v_mm", g - 1))
                    A(olT, at_bank("ol", g), ACT.Copy).then_inc(*S.up("olT", g))
                if h < H:
                    softmax(h)

            act.wait_ge(*S.at("v_mm", H - 1))
            for i, nm in enumerate(("ln_g", "ln_b")):
                act.dma_start(lnbc0[:, i, :], dview(a[nm], 0, (0, P), (1, D))).then_inc(*S.up("lnbc0", by=16))

            def roots(name, key, o, i):
                act.wait_ge(*S.at(*key))
                A(o, i, ACT.Sqrt).then_inc(*S.up(name))

            for t in range(NTT):
                roots("std0_%d" % t, ("var0", t), small[:, 160 + t:161 + t], small[:, 152 + t:153 + t])
            gate_rows(1)
            act.wait_ge(*S.at("theta"))
            A(sc_a[:, 6, :], sc_a[:, 2, :], ACT.Sin).then_inc(*S.up("sin", 0))
            A(sc_a[:, 7, :], sc_a[:, 2, :], ACT.Sin, scale=0.5).then_inc(*S.up("sin", 1))
            modulated(1)
            for f in range(16):
                act.wait_ge(*S.at("s5in_mm", f))
                if f >= 2:
                    act.wait_ge(*S.at("u_out%d" % (f % 2), f - 2))
                A(ust[:, f % 2, :], at_bank("s5in", f), ACT.Copy).then_inc(*S.up("u_sb", f))
                act.wait_ge(*S.at("u_sb", f))
                act.dma_start(u_dram[f * P:(f + 1) * P, :], ust[:, f % 2, :]).then_inc(*S.up("u_out%d" % (f % 2), f, by=16))
            for f in range(16, 32):
                act.wait_ge(*S.at("s5in_mm", f))
                A(gsT[:, f - 16, :], at_bank("s5in", f)[:, 0:T], ACT.Silu).then_inc(*S.up("gs", f))

            for q in range(NQ):
                for half in range(2):
                    act.wait_ge(*S.at("kern_mm", (q, half)))
                    if q:
                        act.wait_ge(*S.at("k_out%d" % 0, q - 1))
                    A(kt[:, 2 * half:2 * half + 2, :], at_bank("kern", q, half)[:, 0:480].rearrange("p (a n) -> p a n", a=2), ACT.Copy).then_inc(*S.up("kt", (q, half)))
                act.wait_ge(*S.at("kt", (q, 1)))
                for gi in range(4):
                    for par in range(2):
                        g0 = par * 64 + q * GQ + gi
                        r = 32 * gi + 16 * par
                        act.dma_start(k_dram[g0:g0 + 13:4, :, :].rearrange("g s n -> s g n"), kt[r:r + 16, :, :]).then_inc(*S.up("k_out0", q, by=16))
                for s4 in range(4):
                    for dr in range(2):
                        for ri in range(2):
                            act.wait_ge(*S.at("mbT_mm", (q, s4, dr, ri)))
                            prev = (q, s4 - 1) if s4 else (q - 1, 3)
                            if prev[0] >= 0:
                                act.wait_ge(*S.at("st_mm", (*prev, dr)))
                            A(mbt[:, dr, ri, :, :], at_bank("mbT", q, s4, dr, ri).rearrange("p (i n) -> p i n", i=4), ACT.Copy).then_inc(*S.up("mbt", (q, s4, dr, ri)))
                for par in range(2):
                    act.wait_ge(*S.at("y_mm", (q, par)))
                    if q:
                        act.wait_ge(*S.at("y_out", q - 1))
                    A(y_sb[:, par, :, :], at_bank("y", q, par).rearrange("p (g c) -> p g c", g=GQ), ACT.Copy).then_inc(*S.up("y", (q, par)))
                act.wait_ge(*S.at("y", (q, 1)))
                for par in range(2):
                    for j in range(L):
                        f0 = (par * 64 + q * GQ) * GS
                        dst = y_dram[f0:f0 + GQ * GS, j * NCL:(j + 1) * NCL].rearrange("(g s) c -> s g c", s=GS)
                        act.dma_start(dst, y_sb[16 * j:16 * j + 16, par, :, :]).then_inc(*S.up("y_out", q, by=16))

            for k in range(KE):
                act.wait_ge(*S.at("y_d", k))
                A(yT[:, k, :], yT[:, k, :], ACT.Gelu_apprx_tanh).then_inc(*S.up("gelu", k))
            for ct in range(4):
                for f in range(4):
                    act.wait_ge(*S.at("glu_k", (ct, 1, 1)))
                    i = 4 * ct + f
                    if i >= 4:
                        act.wait_ge(*S.at("z", i - 4))
                    A(yb.rearrange("p a b t -> p (a b) t")[:, i % 4, :], at_bank("glu", ct, 1, f // 2)[:, (f % 2) * T:(f % 2 + 1) * T], ACT.Sigmoid,
                            bias=column("b_glu", KE + i)).then_inc(*S.up("glu_b", (ct, f)))
            for i, nm in enumerate(("ln_g", "ln_b")):
                act.wait_ge(*S.at("gelu", KE - 1))
                act.dma_start(lnbc1[:, i, :], dview(a[nm], D, (0, P), (1, D))).then_inc(*S.up("lnbc1", by=16))
            for t in range(2):
                roots("std1_%d" % t, ("var1", t), small[:, 160 + t:161 + t], small[:, 152 + t:153 + t])

            def rms(i):
                for t in range(2):
                    act.wait_ge(*S.at("x_rms", (i, t)))
                    A(hn[:, t, :], x[:, t, :], ACT.Square, accum_out=st2[:, t:t + 1]).then_inc(*S.up("x_sq", (i, t)))
                    act.wait_ge(*S.at("x_sq", (i, t)))
                    A(st2[:, 2 + t:3 + t], st2[:, t:t + 1], ACT.Sqrt, scale=1.0 / D, bias=small[:, 200:201]).then_inc(*S.up("rms", (i, t)))

            act.wait_ge(*S.at("eps"))
            rms(0)
            for k in range(KD):
                act.wait_ge(*S.at("hnT_mm", (0, k // 2)))
                A(h2v(hT_flat)[:, k, :], at_bank("hnT", 0, k // 2)[:, (k % 2) * T:(k % 2 + 1) * T], ACT.Copy, scale=column("norm1", k)).then_inc(*S.up("hnT", (0, k)))
            act.wait_ge(*S.at("hnT", (0, 0)))
            act.dma_start(cst, a["c_masks"].rearrange("m p n -> p m n")).then_inc(*S.up("consts2", by=16))
            act.dma_start(toe, dview(a["c_rel"], 0, (1, P), (384, NH2), (1, T))).then_inc(*S.up("consts2", by=16))
            for ct in range(10):
                for t in range(2):
                    act.wait_ge(*S.at("in2_mm", (ct, t)))
                    b = at_bank("in2", ct, t)
                    if ct in (0, 1):
                        if ct:
                            act.wait_ge(*S.at("qk_ss", (ct - 1, t)))
                        A(qk_sq[:, t, :], b, ACT.Square).then_inc(*S.up("qk_sq", (ct, t)))
                        act.wait_ge(*S.at("qk_ss", (ct, t)))
                        A(st2[:, 24 + 8 * t:32 + 8 * t], st2[:, 8 + 8 * t:16 + 8 * t], ACT.Sqrt, scale=1.0 / HD, bias=small[:, 200:201]).then_inc(*S.up("qk_rms", (ct, t)))
                    elif ct == 2:
                        A(va[:, t, :], b, ACT.Copy).then_inc(*S.up("va", (ct, t)))
                    elif ct == 5:
                        A(vb[:, t, :], b, ACT.Copy).then_inc(*S.up("vb", (ct, t)))
                    elif ct >= 6:
                        g = ga if ct < 8 else gb
                        A(g[:, t, (ct % 2) * 512:(ct % 2 + 1) * 512], b, ACT.Sigmoid).then_inc(*S.up("gates", (ct, t)))
                if ct in (0, 1, 3, 4):
                    o = {0: qaT, 1: kaT, 3: qbT, 4: kbT}[ct]
                    for i2 in range(2):
                        act.wait_ge(*S.at("qkT_mm", (ct, i2)))
                        i = at_bank("qkT", ct, i2).rearrange("p (i t) -> p i t", i=2)
                        sc = {0: small[:, 201:202], 1: column("k_gain"), 3: HD ** -0.5, 4: 1.0}[ct]
                        A(o[:, 2 * i2:2 * i2 + 2, :], i, ACT.Copy, scale=sc).then_inc(*S.up("qkT", (ct, i2)))

            for h in range(NH2 + 1):
                if h < NH2:
                    act.wait_ge(*S.at("nmax_a", h))
                    if h >= 2:
                        act.wait_ge(*S.at("pat_mm", h - 2))
                    b = at_bank("sa", h)
                    for t, (c0, c1) in enumerate(((0, P), (P, 3 * P))):
                        i = 40 + 2 * (h % 2) + t
                        A(pa[:, h % 2, c0:c1], b[:, c0:c1], ACT.Exp, bias=st2[:, i:i + 1], accum_out=st2[:, i + 4:i + 5]).then_inc(*S.up("pa", (h, t)))
                    act.wait_ge(*S.at("z_mm", h))
                    if h >= 2:
                        act.wait_ge(*S.at("ob_mm", h - 2))
                    A(az[:, h % 2, :], at_bank("z", h)[:, 0:384], ACT.Abs).then_inc(*S.up("az", h))
                    act.wait_ge(*S.at("az", h))
                    A(az[:, h % 2, :], az[:, h % 2, :], ACT.Exp, scale=-1.0).then_inc(*S.up("ez", h))
                    act.wait_ge(*S.at("ez", h))
                    A(az[:, h % 2, :], az[:, h % 2, :], ACT.Ln, bias=1.0).then_inc(*S.up("lz", h))
                if h >= 1:
                    g = h - 1
                    act.wait_ge(*S.at("zl_mm", g))
                    act.wait_ge(*S.at("sp", g))
                    A(az[:, g % 2, :], at_bank("z", g)[:, 0:384], ACT.Exp).then_inc(*S.up("wb", g))
                    if g % 2:
                        for name, o in (("oa", oaT), ("ob", obT)):
                            act.wait_ge(*S.at(name + "_mm", g))
                            A(o[:, g // 2, :], at_bank(name, g // 2)[:, 0:T], ACT.Copy).then_inc(*S.up(name, g // 2))
            for k2 in range(KD // 2):
                act.wait_ge(*S.at("mT_mm", k2))
                A(mT[:, 2 * k2:2 * k2 + 2, :], at_bank("mT", k2).rearrange("p (k t) -> p k t", k=2), ACT.Copy).then_inc(*S.up("mT", k2))
            rms(1)
            for k in range(KD):
                act.wait_ge(*S.at("hnT_mm", (1, k // 2)))
                A(h2v(hT_flat)[:, k, :], at_bank("hnT", 1, k // 2)[:, (k % 2) * T:(k % 2 + 1) * T], ACT.Copy, scale=column("norm2", k)).then_inc(*S.up("hnT", (1, k)))
            for f in range(KF // 2):
                for half in range(2):
                    for i in range(2):
                        fb = half * KF + 2 * f + i
                        n = (2 * f + i) % 4
                        act.wait_ge(*S.at("up_mm", (f, half)))
                        if f >= 2:
                            act.wait_ge(*S.at("ffn", 2 * (f - 2) + i))
                        A(cg[:, n, half, :], at_bank("up", f, half)[:, i * T:(i + 1) * T], ACT.Identity,
                                scale=column("conv_w2", fb), bias=column("conv_b", fb)).then_inc(*S.up("tap2", (f, half, i)))
                for i in range(2):
                    n = (2 * f + i) % 4
                    act.wait_ge(*S.at("conv", (f, 0, i)))
                    A(cg[:, n, 0, :], cg[:, n, 0, :], ACT.Silu).then_inc(*S.up("up_silu", (f, i)))
            for t in range(2):
                act.wait_ge(*S.at("res3", (1, t)))
                act.dma_start(out[0, t * P:(t + 1) * P, :], x[:, t, :]).then_inc(*S.up("stored", t, by=16))
            for t in range(2):
                act.wait_ge(*S.at("stored", t))

        @block.vector
        def _(dve):
            V = nc.vector
            ts, tt, stt = V.tensor_scalar, V.tensor_tensor, V.scalar_tensor_tensor

            def link(ins):
                ins.then_inc(*S.up("vec_link"))
                dve.wait_ge(*S.last("vec_link"))

            link(V.memset(small, EPS))
            dve.wait_ge(*S.at("consts", "first"))
            V.memset(small[:, 200:201], EPS).then_inc(*S.up("eps"))
            dve.wait_ge(*S.at("colv_mm"))
            link(V.tensor_copy(colv.rearrange("p a n -> p (a n)")[:, 0:NVROW], at_bank("colv")[:, 0:NVROW]))
            r = VROW["cond"]
            V.tensor_copy(condT, colv[:, r // P, r % P:r % P + 2 * KD]).then_inc(*S.up("condT"))
            ts(small[:, 201:202], column("q_gain"), HD ** -0.5, None, ALU.mult).then_inc(*S.up("colv"))

            def modulation(l):
                for ct in range(6):
                    dve.wait_ge(*S.at("mod_mm", (l, ct)))
                    dve.wait_ge(*S.at("bmod%d" % (ct % 2), (l, ct)))
                    if ct >= 2 or l:
                        pl_, pt_ = (l, ct - 2) if ct >= 2 else (l - 1, ct + 4)
                        if pt_ < 4:
                            dve.wait_ge(*S.at("modT_mm", (pl_, pt_)))
                        else:
                            dve.wait_ge(*S.at("gtb_mm", (pl_, pt_, 1 - pl_)))
                    tt(modrow[0:2, ct % 2, :], at_bank("mod", l, ct)[0:2, :], bmod[0:2, ct % 2, :], ALU.add).then_inc(*S.up("mod_row", (l, ct)))
                    if ct < 4:
                        dve.wait_ge(*S.at("modT_mm", (l, ct)))
                        i = at_bank("modT", l, ct)[:, 0:8].rearrange("p (a b) -> p a b", b=2)
                        ts(shsc[:, 4 * ct:4 * ct + 4, :], i, 1.0 if ct >= 2 else 0.0, None, ALU.add).then_inc(*S.up("shsc", (l, ct)))

            def modulated(l):
                dve.wait_ge(*S.at("shsc", (l, 3)))
                for k in range(0, KD, 2):
                    dve.wait_ge(*S.at("xT_mm", (l, k)))
                    for c in range(2):
                        o, i = modulate_views(l, k, c)
                        ins = ts(o, i, shsc[:, KD + k, c:c + 1], shsc[:, k, c:c + 1], ALU.mult, ALU.add)
                    ins.then_inc(*S.up("hT_v", (l, k)))

            modulation(0)
            modulated(0)
            for t in range(NTT):
                dve.wait_ge(*S.at("lat_ss", t))
            link(ts(st0[:, 8:12], st0[:, 0:4], 1.0 / QR, EPS, ALU.mult, ALU.add))
            ts(st0[:, 12:16], st0[:, 4:8], 1.0 / KVR, EPS, ALU.mult, ALU.add).then_inc(*S.up("lat_ms"))
            dve.wait_ge(*S.at("lat_rms"))
            link(V.reciprocal(st0[:, 40:48], st0[:, 16:24]))
            dve.wait_ge(*S.at("second"))
            for t in range(NTT):
                b = at_bank("head", t)
                ts(qn[:, t, :], b[:, 0:QR], st0[:, 40 + t:41 + t], None, ALU.mult).then_inc(*S.up("qn", t))
                stt(ckv[:, t, :], b[:, QR:QR + KVR], st0[:, 44 + t:45 + t], kvg, ALU.mult, ALU.mult).then_inc(*S.up("ckv", t))
                k_r = b[:, QR + KVR:HEAD_IN]
                if t < 2:
                    link(tt(krt[:, 0, :], k_r, rope[:, 0, t, :], ALU.mult))
                    sw = k_r.rearrange("p (a b n) -> p a b n", a=2, b=2)[:, :, ::-1, :]
                    link(tt(krt[:, 1, :].rearrange("p (a b n) -> p a b n", a=2, b=2), sw,
                            rope[:, 1, t, :].rearrange("p (a b n) -> p a b n", a=2, b=2), ALU.mult))
                    tt(kr[:, t, 0, :], krt[:, 0, :], krt[:, 1, :], ALU.add).then_inc(*S.up("kr", t))
                    tt(kr[:, t, 1, :], krt[:, 0, :], krt[:, 1, :], ALU.add).then_inc(*S.up("kr_pos", t))
                    dve.wait_ge(*S.at("kr_pos", t))
                else:
                    link(V.tensor_copy(kr[:, t, 0, :], k_r))
                    V.tensor_copy(kr[:, t, 1, :], k_r).then_inc(*S.up("kr", t))
            dve.wait_ge(*S.at("krT_mm"))
            V.tensor_copy(krT, at_bank("krT")).then_inc(*S.up("krT"))

            def q_rope(hf):
                for t in range(2):
                    dve.wait_ge(*S.at("qrf", (hf, t)))
                    if hf or t:
                        dve.wait_ge(*S.at("qrpT_mm", (hf, t - 1) if t else (hf - 1, 1)))
                    b = at_bank("qrope", hf, t)
                    cos = rope[:, 0, t, :]
                    sin = rope[:, 1, t, :]
                    v = b.rearrange("p (h n) -> p h n", h=8)
                    tt(qrp.rearrange("p (h n) -> p h n", h=8), v, over(cos, (0, 8), (1, ROPE)), ALU.mult).then_inc(*S.up("qrp_a", (hf, t)))
                    for i in range(2):
                        sw = b.rearrange("p (h a b n) -> p h a b n", h=8, a=2, b=2)[:, :, i, ::-1, :]
                        o = qrt.rearrange("p (h a b n) -> p h a b n", h=8, a=2, b=2)[:, :, i]
                        ins = tt(o, sw, over(sin[:, 32 * i:32 * i + 1], (0, 8), (16, 2), (1, 16)), ALU.mult)
                        if i == 0:
                            link(ins)
                    ins.then_inc(*S.up("qrp_b", (hf, t)))
                    dve.wait_ge(*S.at("qrp_a", (hf, t)))
                    dve.wait_ge(*S.at("qrp_b", (hf, t)))
                    tt(qrp, qrp, qrt, ALU.add).then_inc(*S.up("qrp", (hf, t)))

            def head(h):
                dve.wait_ge(*S.at("k_mm", h))
                if h >= 2:
                    dve.wait_ge(*S.at("s_mm", (h - 2, 2)))
                V.tensor_copy(kT[:, h % 2, :], at_bank("k", h)).then_inc(*S.up("kT", h))

            def maxima(h):
                c = 4 * (h % 2)
                if h >= 2:
                    dve.wait_ge(*S.at("p", (h - 2, 3)))
                for t in range(3):
                    dve.wait_ge(*S.at("s_mm", (h, t)))
                    b = at_bank("s", h, t)
                    i = b if t < 2 else b.rearrange("p (t n) -> p t n", t=2)
                    ins = V.tensor_reduce(st0[:, 48 + c + t:49 + c + t + (t == 2)], i, AX, ALU.max)
                    ins.then_inc(*S.up("vec_link"))
                dve.wait_ge(*S.last("vec_link"))
                ts(st0[:, 24 + c:28 + c], st0[:, 48 + c:52 + c], -MLA_SCALE, None, ALU.mult).then_inc(*S.up("nmax", h))

            def norm(h):
                c = 4 * (h % 2)
                for t in range(NTT):
                    dve.wait_ge(*S.at("p", (h, t)))
                link(V.reciprocal(st0[:, 56 + c:60 + c], st0[:, 32 + c:36 + c]))
                for t in range(NTT):
                    o = pl[:, h % 2, t, :] if t < 2 else pc[:, h % 2, t - 2, :]
                    ts(o, o, st0[:, 56 + c + t:57 + c + t], None, ALU.mult).then_inc(*S.up("pn", (h, t)))

            def values(h):
                for i in range(2):
                    dve.wait_ge(*S.at("pt_mm", (h, i)))
                    if h >= 2:
                        dve.wait_ge(*S.at("ol_mm", h - 2))
                    V.tensor_copy(PT[:, h % 2, i, :], at_bank("pt", h, i)).then_inc(*S.up("pt", (h, i)))
                dve.wait_ge(*S.at("pt2", h))
                V.tensor_copy(small[0:1, 250:251], small[0:1, 200:201]).then_inc(*S.up("pt", (h, 2)))

            def gated(h):
                dve.wait_ge(*S.at("v_mm", h))
                dve.wait_ge(*S.at("gate", h))
                tt(gT[:, h, :], at_bank("v", h), gT[:, h, :], ALU.mult).then_inc(*S.up("vg", h))

            for h in range(H + 2):
                if h < H:
                    if h % 8 == 0:
                        q_rope(h // 8)
                    head(h)
                if 1 <= h <= H:
                    values(h - 1)
                if h >= 2:
                    gated(h - 2)
                if h < H:
                    maxima(h)
                    norm(h)

            def residual(l, n, t):
                o = "out%d" % l
                if (l == 0 and t == 3) or (l == 1 and t == 1):
                    dve.wait_ge(*S.at(o + "_k", (n, 1)))
                else:
                    dve.wait_ge(*S.at(o + "_mm", (n, t)))
                cols = slice(n * 512, (n + 1) * 512)
                y = at_bank(o, n, t)
                dve.wait_ge(*S.at("gtb", (l, 5, 0 if (t < 2) else 1)))
                tmp = (qrf[:, t % 2, :] if l == 0 else hT_flat[:, (t % 2) * 512:(t % 2 + 1) * 512])
                tt(tmp, y, gtb[:, t // 2, cols], ALU.mult).then_inc(*S.up("res%d_a" % l, (n, t)))
                dve.wait_ge(*S.at("res%d_a" % l, (n, t)))
                stt(x[:, t, cols], x[:, t, cols], ALPHA, tmp, ALU.mult, ALU.add).then_inc(*S.up("res%d" % l, (n, t)))

            def layernorm(l, nt, lnbc):
                for t in range(nt):
                    dve.wait_ge(*S.at("res%d" % l, (1, t)))
                    for i in range(2):
                        ins = V.bn_stats(small[:, 208 + 6 * i:214 + 6 * i], x[:, t, i * 512:(i + 1) * 512])
                        link(ins)
                    link(V.bn_aggr(small[:, 128 + 2 * t:130 + 2 * t], small[:, 208:220]))
                    ts(small[:, 152 + t:153 + t], small[:, 129 + 2 * t:130 + 2 * t], EPS, None, ALU.add).then_inc(*S.up("var%d" % l, t))
                dve.wait_ge(*S.at("lnbc%d" % l))
                for t in range(nt):
                    dve.wait_ge(*S.at("std%d_%d" % (l, t)))
                    link(V.reciprocal(small[:, 168 + t:169 + t], small[:, 160 + t:161 + t]))
                    link(ts(x[:, t, :], x[:, t, :], small[:, 128 + 2 * t:129 + 2 * t], small[:, 168 + t:169 + t], ALU.subtract, ALU.mult))
                    link(tt(x[:, t, :], x[:, t, :], lnbc[:, 0, :], ALU.mult))
                    tt(x[:, t, :], x[:, t, :], lnbc[:, 1, :], ALU.add).then_inc(*S.up("x%d" % (l + 1), t))

            for n in range(2):
                for t in range(NTT):
                    residual(0, n, t)
            layernorm(0, NTT, lnbc0)
            modulation(1)

            dve.wait_ge(*S.at("lam_in"))
            z = lambda i: sc_a[:, i, :]
            d0 = lambda i: dts[:, 2 * i:2 * i + 2]
            link(ts(d0(0), ldt, -150.0, 80.0, ALU.max, ALU.min))
            link(ts(d0(1), d0(0), float(1.0 / np.log(2.0)), ROUND, ALU.mult, ALU.add))
            link(ts(d0(1), d0(1), ROUND, None, ALU.subtract))
            link(stt(d0(2), d0(1), -LN2_1, d0(0), ALU.mult, ALU.add))
            link(stt(d0(2), d0(1), -LN2_2, d0(2), ALU.mult, ALU.add))
            coef = [1.0 / float(np.prod(np.arange(1, n + 1))) for n in range(1, 10)]
            link(ts(d0(3), d0(2), coef[8], None, ALU.mult))
            for n in range(7, -1, -1):
                link(stt(d0(3), d0(3), coef[n], d0(2), ALU.add, ALU.mult))
            link(ts(d0(3), d0(3), 1.0, None, ALU.add))
            link(ts(d0(1), d0(1), 127.0, 0.0, ALU.add, ALU.max))
            ki = d0(4).bitcast(I32)
            link(V.tensor_copy(ki, d0(1)))
            link(ts(ki, ki, 23, None, ALU.logical_shift_left))
            link(tt(d0(5), d0(3), d0(4), ALU.mult))
            link(ts(z(0), lam[:, 0, :], -1e-4, None, ALU.min))
            for par in range(2):
                c = slice(64 * par, 64 * par + 64)
                link(ts(z(1)[:, c], z(0)[:, c], dts[:, 10 + par:11 + par], None, ALU.mult))
                link(ts(z(2)[:, c], lam[:, 1, c], dts[:, 10 + par:11 + par], None, ALU.mult))
            link(ts(z(3), z(2), float(1.0 / TWO_PI), ROUND, ALU.mult, ALU.add))
            link(ts(z(3), z(3), ROUND, None, ALU.subtract))
            for c in (PI_1, PI_2, PI_3):
                link(stt(z(2), z(3), -c, z(2), ALU.mult, ALU.add))
            ts(z(2), z(2), float(np.float32(3.1415925)), float(-np.float32(3.1415925)), ALU.min, ALU.max).then_inc(*S.up("theta"))
            link(ts(z(1), z(1), -88.0, 1.0 / 256, ALU.max, ALU.mult))
            link(ts(z(4), z(1), coef[6], None, ALU.mult))
            for n in range(5, -1, -1):
                link(stt(z(4), z(4), coef[n], z(1), ALU.add, ALU.mult))
            for n in range(8):
                link(stt(z(4), z(4), 2.0, z(4), ALU.add, ALU.mult))
            dve.wait_ge(*S.at("sin", 0))
            dve.wait_ge(*S.at("sin", 1))
            link(tt(z(7), z(7), z(7), ALU.mult))
            link(ts(z(5), z(7), -2.0, 1.0, ALU.mult, ALU.add))
            link(tt(z(5), z(5), z(4), ALU.mult))
            link(stt(z(5), z(7), -2.0, z(5), ALU.mult, ALU.add))
            link(stt(z(11), z(4), 1.0, z(6), ALU.add, ALU.mult))
            link(ts(z(10), z(5), 1.0, None, ALU.add))
            link(tt(z(8), z(0), z(0), ALU.mult))
            link(tt(z(9), lam[:, 1, :], lam[:, 1, :], ALU.mult))
            link(tt(z(8), z(8), z(9), ALU.add))
            link(V.reciprocal(z(8), z(8)))
            link(tt(z(12), z(5), z(0), ALU.mult))
            link(tt(z(9), z(11), lam[:, 1, :], ALU.mult))
            link(tt(z(12), z(12), z(9), ALU.add))
            link(tt(z(12), z(12), z(8), ALU.mult))
            link(tt(z(13), z(11), z(0), ALU.mult))
            link(tt(z(9), z(5), lam[:, 1, :], ALU.mult))
            link(tt(z(13), z(13), z(9), ALU.subtract))
            tt(z(13), z(13), z(8), ALU.mult).then_inc(*S.up("lam_ready"))
            dve.wait_ge(*S.at("lamT_mm"))
            V.tensor_copy(lamT.rearrange("p a n -> p (a n)"), at_bank("lamT")).then_inc(*S.up("lamT"))
            dve.wait_ge(*S.at("lamT"))

            def pairs(oR, oN, re, im):
                v = lambda i: i.rearrange("p (d g) -> p d g", d=2)
                for i in range(2):
                    link(V.tensor_copy(oR[:, :, i, :], v(re)))
                link(ts(oN[:, :, 0, :], v(im), -1.0, None, ALU.mult))
                link(V.tensor_copy(oN[:, :, 1, :], v(im)))

            pairs(lamL, lamN, lamT[:, 0, :], lamT[:, 1, :])
            pairs(wR, wN, lamT[:, 2, :], lamT[:, 3, :])
            for _ in range(3):
                link(tt(z(0), lamT[:, 0, :], lamT[:, 0, :], ALU.mult))
                link(tt(z(1), lamT[:, 1, :], lamT[:, 1, :], ALU.mult))
                link(tt(z(2), lamT[:, 0, :], lamT[:, 1, :], ALU.mult))
                link(tt(lamT[:, 0, :], z(0), z(1), ALU.subtract))
                link(ts(lamT[:, 1, :], z(2), 2.0, None, ALU.mult))
            pairs(L8R, L8N, lamT[:, 0, :], lamT[:, 1, :])
            V.tensor_copy(small[0:1, 251:252], small[0:1, 200:201]).then_inc(*S.up("lam_tables"))
            modulated(1)

            for q in range(NQ):
                gs = slice(q * GQ, (q + 1) * GQ)
                for ri in range(2):
                    dve.wait_ge(*S.at("cT_mm", (q, ri)))
                    if q == 0:
                        dve.wait_ge(*S.at("s5in_mm", 31))
                    b = at_bank("cT", q, ri).rearrange("p (d g s) -> p d g s", d=2, s=GS)
                    for dr in range(2):
                        e = 0 if dr == 0 else 8
                        ins = ts(mc[:, dr, :, ri, e, :], b[:, dr], -1.0 if ri else 1.0, None, ALU.mult)
                        if dr == 0:
                            link(ins)
                    ins.then_inc(*S.up("c0", (q, ri)))
                    dve.wait_ge(*S.at("c0", (q, ri)))
                for n in range(8):
                    for dr in range(2):
                        e0, e1 = (n, n + 1) if dr == 0 else (8 - n, 7 - n)
                        src = mc[:, dr, :, :, e0, :]
                        t0 = tmpd[:, 0, :].rearrange("p (g r s) -> p g r s", g=GQ, r=2)
                        t1 = tmpd[:, 1, :].rearrange("p (g r s) -> p g r s", g=GQ, r=2)
                        lr = over(lamL[:, dr, 0, gs], (1, GQ), (64, 2), (0, GS))
                        ln = over(lamN[:, dr, 1, gs], (1, GQ), (-64, 2), (0, GS))
                        link(tt(t0, src, lr, ALU.mult))
                        link(tt(t1, src[:, :, ::-1, :], ln, ALU.mult))
                        ins = tt(mc[:, dr, :, :, e1, :], t0, t1, ALU.add)
                        if n == 7:
                            ins.then_inc(*S.up("mc", (q, dr)))
                            dve.wait_ge(*S.at("mc", (q, dr)))
                        else:
                            link(ins)
                for s4 in range(4):
                    g4 = slice(4 * s4, 4 * s4 + 4)
                    for dr in range(2):
                        dve.wait_ge(*S.at("st_mm", (q, s4, dr)))
                        b = at_bank("st", q, s4, dr).rearrange("p (r g c) -> p r g c", r=2, g=4)
                        o = xs[:, :, dr, :, g4].rearrange("p k r g -> p r g k")
                        if dr == 0:
                            ins = V.tensor_copy(o, b)
                        else:
                            link(V.tensor_copy(o[:, :, :, 0:NCL], b[:, :, :, NCL - 1::-1]))
                            ins = V.tensor_copy(o[:, :, :, NCL:NC], b[:, :, :, NC - 1:NCL - 1:-1])
                        ins.then_inc(*S.up("xs", (q, s4, dr)))
                dve.wait_ge(*S.at("xs", (q, 3, 0)))
                dve.wait_ge(*S.at("xs", (q, 3, 1)))
                for k in range(1, NC):
                    t0 = scan[:, 0, :].rearrange("p (d r g) -> p d r g", d=2, r=2)
                    t1 = scan[:, 1, :].rearrange("p (d r g) -> p d r g", d=2, r=2)
                    tt(t0, xs[:, k - 1], L8R[:, :, :, gs], ALU.mult).then_inc(*S.up("scan_r", (q, k)))
                    link(tt(t1, xs[:, k - 1, :, ::-1, :], L8N[:, :, :, gs], ALU.mult))
                    link(tt(t0, t0, t1, ALU.add))
                    tt(xs[:, k], xs[:, k], t0, ALU.add).then_inc(*S.up("scan", (q, k)))
                    dve.wait_ge(*S.at("scan", (q, k)))

            dve.wait_ge(*S.at("yT_load"))
            for k in range(KE):
                stt(yT[:, k, :], uT[:, k, :], column("s5_d", k), yT[:, k, :], ALU.mult, ALU.add).then_inc(*S.up("y_d", k))
            for ct in range(4):
                for f in range(4):
                    i = 4 * ct + f
                    dve.wait_ge(*S.at("glu_k", (ct, 0, 1)))
                    if i >= 4:
                        dve.wait_ge(*S.at("z", i - 4))
                    ts(ya.rearrange("p a b t -> p (a b) t")[:, i % 4, :], at_bank("glu", ct, 0, f // 2)[:, (f % 2) * T:(f % 2 + 1) * T],
                             column("b_glu", i), None, ALU.add).then_inc(*S.up("glu_a", (ct, f)))
                for f in range(4):
                    i = 4 * ct + f
                    dve.wait_ge(*S.at("glu_b", (ct, f)))
                    dve.wait_ge(*S.at("glu_a", (ct, f)))
                    m = ya.rearrange("p a b t -> p (a b) t")[:, i % 4, :]
                    link(tt(m, m, yb.rearrange("p a b t -> p (a b) t")[:, i % 4, :], ALU.mult))
                    jc = lambda v: v.rearrange("p (j c) -> p j c", j=L)
                    tt(zT[:, i, :].rearrange("p (c j) -> p j c", j=L), jc(m), jc(gsT[:, i, :]), ALU.mult).then_inc(*S.up("z", i))
            for n in range(2):
                for t in range(2):
                    residual(1, n, t)
            layernorm(1, 2, lnbc1)

            def rms(i):
                for t in range(2):
                    if i == 0:
                        V.tensor_copy(small[0:1, 252 + t:253 + t], small[0:1, 200:201]).then_inc(*S.up("x_rms", (i, t)))
                for t in range(2):
                    dve.wait_ge(*S.at("rms", (i, t)))
                    link(V.reciprocal(st2[:, 4 + t:5 + t], st2[:, 2 + t:3 + t]))
                    ts(hn[:, t, :], x[:, t, :], st2[:, 4 + t:5 + t], None, ALU.mult).then_inc(*S.up("hn", (i, t)))

            dve.wait_ge(*S.at("x2", 1))
            rms(0)
            for ct in range(6):
                if ct in (2, 5):
                    continue
                for t in range(2):
                    b = at_bank("in2", ct, t)
                    if ct > 0:
                        prev = {1: 0, 3: 1, 4: 3}[ct]
                        dve.wait_ge(*S.at("qkT_mm", (prev, 1)))
                    if ct < 2:
                        dve.wait_ge(*S.at("qk_sq", (ct, t)))
                        V.tensor_reduce(st2[:, 8 + 8 * t:16 + 8 * t], qk_sq[:, t, :].rearrange("p (h d) -> p h d", h=8), AX, ALU.add).then_inc(*S.up("qk_ss", (ct, t)))
                        dve.wait_ge(*S.at("qk_rms", (ct, t)))
                        rr = small[:, 176 + 8 * t:184 + 8 * t]
                        link(V.reciprocal(rr, st2[:, 24 + 8 * t:32 + 8 * t]))
                        tt(qk_sb[:, t, :].rearrange("p (h d) -> p h d", h=8), b.rearrange("p (h d) -> p h d", h=8),
                                 over(rr, (1, 8), (0, HD)), ALU.mult).then_inc(*S.up("qk_n", (ct, t)))
                    else:
                        dve.wait_ge(*S.at("in2_mm", (ct, t)))
                        V.tensor_copy(qk_sb[:, t, :], b).then_inc(*S.up("qk_n", (ct, t)))

            for h in range(NH2 + 1):
                if h < NH2:
                    c = 2 * (h % 2)
                    dve.wait_ge(*S.at("sa_mm", h))
                    if h >= 2:
                        dve.wait_ge(*S.at("pa", (h - 2, 1)))
                    b = at_bank("sa", h)
                    V.tensor_reduce(st2[:, 48 + c:49 + c], b[:, 0:P], AX, ALU.max).then_inc(*S.up("vec_link"))
                    link(V.tensor_reduce(st2[:, 49 + c:50 + c], b[:, P:3 * P], AX, ALU.max))
                    ts(st2[:, 40 + c:42 + c], st2[:, 48 + c:50 + c], -1.0, None, ALU.mult).then_inc(*S.up("nmax_a", h))
                    dve.wait_ge(*S.at("z_mm", h))
                    zz = at_bank("z", h)[:, 0:384]
                    dve.wait_ge(*S.at("lz", h))
                    if h >= 2:
                        dve.wait_ge(*S.at("zl_mm", h - 2))
                    o = lk[:, h % 2, :]
                    stt(o, zz, 0.0, az[:, h % 2, :], ALU.max, ALU.add).then_inc(*S.up("sp", h))
                    dve.wait_ge(*S.at("sp", h))
                    dg = over(o[:, 0:1], (T, 2), (1, P))
                    tt(dg, dg, over(cst[:, 2, 0:1], (0, 2), (1, P)), ALU.mult).then_inc(*S.up("lk", h))
                    for t in range(2):
                        dve.wait_ge(*S.at("pa", (h, t)))
                    link(V.reciprocal(st2[:, 52 + c:54 + c], st2[:, 44 + c:46 + c]))
                    for t, (c0, c1) in enumerate(((0, P), (P, 3 * P))):
                        ts(pa[:, h % 2, c0:c1], pa[:, h % 2, c0:c1], st2[:, 52 + c + t:53 + c + t], None, ALU.mult).then_inc(*S.up("pan", (h, t)))
                if h >= 1:
                    g = h - 1
                    dve.wait_ge(*S.at("pat_mm", g))
                    if g >= 2:
                        dve.wait_ge(*S.at("oa_mm", g - 2))
                    V.tensor_copy(pat[:, g % 2, :], at_bank("pat", g)[:, 0:384]).then_inc(*S.up("pat", g))

            for br in range(2):
                for n in range(2):
                    for t in range(2):
                        dve.wait_ge(*S.at("branch_mm", (br, n, t)))
                        dve.wait_ge(*S.at("gates", ((6 if br == 0 else 8) + n, t)))
                        cols = slice(n * 512, (n + 1) * 512)
                        b = at_bank("branch", br, n, t)
                        if br == 0:
                            tt(mixed[:, t, cols], b, ga[:, t, cols], ALU.mult).then_inc(*S.up("mix", (br, n, t)))
                        else:
                            link(tt(gb[:, t, cols], b, gb[:, t, cols], ALU.mult))
                            tt(mixed[:, t, cols], mixed[:, t, cols], gb[:, t, cols], ALU.add).then_inc(*S.up("mix", (br, n, t)))
            for n in range(2):
                for t in range(2):
                    dve.wait_ge(*S.at("out2_mm", (n, t)))
                    cols = slice(n * 512, (n + 1) * 512)
                    tt(x[:, t, cols], at_bank("out2", n, t), x[:, t, cols], ALU.add).then_inc(*S.up("res2", (n, t)))
            dve.wait_ge(*S.at("res2", (1, 1)))
            for t in range(2):
                V.tensor_copy(small[0:1, 252 + t:253 + t], small[0:1, 200:201]).then_inc(*S.up("x_rms", (1, t)))
            rms(1)
            for f in range(KF // 2):
                for half in range(2):
                    for i in range(2):
                        fb = half * KF + 2 * f + i
                        n = (2 * f + i) % 4
                        b = at_bank("up", f, half)[:, i * T:(i + 1) * T]
                        o = cg[:, n, half, :]
                        dve.wait_ge(*S.at("tap2", (f, half, 1)))
                        link(stt(o[:, 1:T], b[:, 0:T - 1], column("conv_w1", fb), o[:, 1:T], ALU.mult, ALU.add))
                        stt(o[:, 2:T], b[:, 0:T - 2], column("conv_w0", fb), o[:, 2:T], ALU.mult, ALU.add).then_inc(*S.up("conv", (f, half, i)))
                for i in range(2):
                    n = (2 * f + i) % 4
                    dve.wait_ge(*S.at("up_silu", (f, i)))
                    dve.wait_ge(*S.at("conv", (f, 1, i)))
                    tt(fT[:, 2 * f + i, :], cg[:, n, 0, :], cg[:, n, 1, :], ALU.mult).then_inc(*S.up("ffn", 2 * f + i))
            for n in range(2):
                for t in range(2):
                    if t == 0:
                        dve.wait_ge(*S.at("down_mm", (n, t)))
                    else:
                        dve.wait_ge(*S.at("down_k", (n, 2)))
                    cols = slice(n * 512, (n + 1) * 512)
                    tt(x[:, t, cols], at_bank("down", n, t), x[:, t, cols], ALU.add).then_inc(*S.up("res3", (n, t)))

        @block.gpsimd
        def _(pool):
            G = nc.gpsimd
            pool.wait_ge(*S.at("lam_tables"))
            pool.wait_ge(*S.at("x1", 3))
            G.memset(bbd.rearrange("p a b c d -> p (a b c d)"), 0.0).then_inc(*S.up("bbd_zero"))
            pool.wait_ge(*S.at("bbd_zero"))

            def link(ins):
                ins.then_inc(*S.up("pool_link"))
                pool.wait_ge(*S.last("pool_link"))

            def times(o, src, r, n):
                ng = src.shape[1]
                t0 = tmpp[:, 0, 0:ng * 32].rearrange("p (g r s) -> p g r s", g=ng, r=2)
                t1 = tmpp[:, 1, 0:ng * 32].rearrange("p (g r s) -> p g r s", g=ng, r=2)
                link(G.tensor_tensor(t0, src, over(r, (1, ng), (64, 2), (0, GS)), ALU.mult))
                link(G.tensor_tensor(t1, src[:, :, ::-1, :], over(n, (1, ng), (64, 2), (0, GS)), ALU.mult))
                return G.tensor_tensor(o, t0, t1, ALU.add)

            for q in range(NQ):
                pool.wait_ge(*S.at("b_load", q))
                for dr in range(2):
                    g0 = q * GQ
                    link(times(bbar[:, dr], braw[:, dr], wR[:, dr, 0, g0:g0 + 1], wN[:, dr, 0, g0:g0 + 1]))
                if q:
                    pool.wait_ge(*S.at("kern_mm", (q - 1, 1)))
                for par in range(2):
                    r = slice(64 * par, 64 * par + 64)
                    for dr in range(2):
                        ins = G.tensor_copy(bbd[r, dr, :, :, 16 * par:16 * par + 16], bbar[r, dr])
                        if (par, dr) != (1, 1):
                            link(ins)
                ins.then_inc(*S.up("bbd", q))
                pool.wait_ge(*S.at("bbd", q))
                for s4 in range(4):
                    for dr in range(2):
                        if s4 or q:
                            prev = (q, s4 - 1) if s4 else (q - 1, 3)
                            pool.wait_ge(*S.at("mbT_mm", (*prev, dr, 1)))
                        at_ = lambda n: 7 - n if dr == 0 else n
                        link(G.tensor_copy(mb[:, dr, :, :, at_(0), :], bbar[:, dr, 4 * s4:4 * s4 + 4]))
                        g0 = q * GQ + 4 * s4
                        for n in range(7):
                            ins = times(mb[:, dr, :, :, at_(n + 1), :], mb[:, dr, :, :, at_(n), :], lamL[:, dr, 0, g0:g0 + 1], lamN[:, dr, 0, g0:g0 + 1])
                            if n < 6:
                                link(ins)
                        ins.then_inc(*S.up("mb", (q, s4, dr)))
                        pool.wait_ge(*S.at("mb", (q, s4, dr)))

        @block.sync
        def _(sp):
            def ring_load(i):
                src, shape, freed, parts = loads[i]
                if i >= SLOTS:
                    sp.wait_ge(*S.at(*loads[i - SLOTS][2]))
                o = slot(i, *shape)
                if parts is None:
                    sp.dma_start(o, src).then_inc(*S.up(f"slot{i % SLOTS}", i, by=16))
                else:
                    for n, part in enumerate(parts):
                        sp.dma_start(o[:, n], part).then_inc(*S.up(f"slot{i % SLOTS}", i, by=16))

            def bias(l, ct):
                if ct >= 2 or l:
                    sp.wait_ge(*S.at("mod_row", (l, ct - 2) if ct >= 2 else (l - 1, ct + 4)))
                src = dview(a["b_mod"], l * 3 * D + ct * 512, (0, 2), (1, 512))
                sp.dma_start(bmod[0:2, ct % 2, :], src).then_inc(*S.up("bmod%d" % (ct % 2), (l, ct), by=16))

            for i in range(first_glu):
                for l in range(2):
                    for ct in range(6):
                        if load_no[("mod", l, ct)] == i:
                            bias(l, ct)
                ring_load(i)
                if i == load_no[("mod", 1, 0)]:
                    sp.wait_ge(*S.at("vg", H - 1))
                    sp.wait_ge(*S.at("out0_k", (1, 1)))
                    for ri, nm in enumerate(("s5_lam_re", "s5_lam_im")):
                        for dr in range(2):
                            for par in range(2):
                                sp.dma_start(lam[64 * dr:64 * dr + 64, ri, 64 * par:64 * par + 64],
                                                   a[nm][0, dr, 64 * par:64 * par + 64, :]).then_inc(*S.up("lam_in", by=16))
                    for dr in range(2):
                        for par in range(2):
                            sp.dma_start(ldt[64 * dr:64 * dr + 64, par:par + 1],
                                               dview(a["s5_log_dt"], dr * NG + 64 * par, (1, 64), (1, 1))).then_inc(*S.up("lam_in", by=16))

            def core_loads(q):
                if q:
                    sp.wait_ge(*S.at("bbd", q - 1))
                for ri, nm in enumerate(("s5_b_re", "s5_b_im")):
                    for dr in range(2):
                        for par in range(2):
                            g0 = par * 64 + q * GQ
                            sp.dma_start(braw[64 * par:64 * par + 64, dr, :, ri, :],
                                               a[nm][0, dr, g0:g0 + GQ, :, :].rearrange("g p s -> p g s")).then_inc(*S.up("b_load", q, by=16))
                if q:
                    sp.wait_ge(*S.at("cT_mm", (q - 1, 1)))
                for ri, nm in enumerate(("s5_c_re", "s5_c_im")):
                    for dr in range(2):
                        for par in range(2):
                            r0 = (par * 64 + q * GQ) * GS
                            src = a[nm][0, dr].rearrange("g s p -> (g s) p")[r0:r0 + GQ * GS, :].rearrange("(b r) p -> r b p", b=2)
                            sp.dma_start(cn[:, ri, dr, :, 64 * par:64 * par + 64], src).then_inc(*S.up("cn", q, by=16))
                if q == 0:
                    for f in range(16):
                        sp.wait_ge(*S.at("u_out%d" % (f % 2), f))
                    sp.wait_ge(*S.at("s5in_mm", 31))
                else:
                    sp.wait_ge(*S.at("y_mm", (q - 1, 1)))
                for par in range(2):
                    for j in range(L):
                        f0 = (par * 64 + q * GQ) * GS
                        src = u_dram[f0:f0 + GQ * GS, j * NC:(j + 1) * NC].rearrange("(g s) c -> s g c", s=GS)
                        sp.dma_start(u_sb[16 * j:16 * j + 16, par, :, :], src).then_inc(*S.up("u_load", q, by=16))
                sp.wait_ge(*S.at("k_out0", q))
                for par in range(2):
                    for j in range(L):
                        g0 = par * 64 + q * GQ
                        src = k_dram[g0:g0 + GQ, :, (7 - j) * GS:(15 - j) * GS].rearrange("g s n -> s g n")
                        sp.dma_start(tt_sb[16 * j:16 * j + 16, par, :, :], src).then_inc(*S.up("t_load", q, by=16))

            sp.wait_ge(*S.at("res0", (1, 3)))
            for q in range(NQ):
                core_loads(q)
            sp.wait_ge(*S.at("y_mm", (NQ - 1, 1)))
            for i in range(SLOTS):
                ring_load(first_glu + i)
            for q in range(NQ):
                sp.wait_ge(*S.at("y_out", q))
            sp.dma_start(yT, y_dram.rearrange("(k p) t -> p k t", p=P)).then_inc(*S.up("yT_load", by=16))
            sp.dma_start(uT.rearrange("p k (j c) -> p k j c", j=L),
                               u_dram.rearrange("(k p) (j s c) -> p k j s c", p=P, j=L, s=2)[:, :, :, 1, :]).then_inc(*S.up("yT_load", by=16)) if False else None
            for k in range(KE):
                sp.dma_start(uT[:, k, :].rearrange("p (j c) -> p j c", j=L),
                                   u_dram[k * P:(k + 1) * P, :].rearrange("p (j s c) -> p j s c", j=L, s=2)[:, :, 1, :]).then_inc(*S.up("yT_load", by=16))
            for i in range(first_glu + SLOTS, len(loads)):
                ring_load(i)

        return S.seen


def h2v(flat):
    return flat[:, 0:KD * T].rearrange("p (k t) -> p k t", k=KD)


def tables():
    i = np.arange(P)
    masks = np.zeros((6, P, P), np.float32)
    masks[0] = i[:, None] + i[None, :] == P - 1
    masks[1] = np.where((i[:, None] < 64) & (i[None, :] >= 64), LOW, 0.0)
    masks[2] = i[:, None] < i[None, :]
    masks[3] = -(i[:, None] >= i[None, :]).astype(np.float32)
    masks[4] = -1.0
    masks[5] = np.where(i[:, None] >= i[None, :], LOW, 0.0)
    sel = np.zeros((2, 2, P), np.float32)
    sel[0, 0] = sel[1, 1] = 1.0
    t = np.arange(T)
    quarter = ROPE // 4
    inv = np.float32(10000.0) ** (-np.arange(quarter, dtype=np.float32) / np.float32(quarter))
    ang_r = (t // GRID_W).astype(np.float32)[:, None] * inv
    ang_c = (t % GRID_W).astype(np.float32)[:, None] * inv
    ang = np.concatenate([ang_r, ang_r, ang_c, ang_c], axis=-1).astype(np.float32)
    sign = np.repeat(np.array([-1.0, 1.0, -1.0, 1.0], np.float32), quarter)
    rope = np.stack([np.cos(ang), np.sin(ang) * sign]).astype(np.float32)
    return {"c_ident": np.eye(P, dtype=np.float32)[None], "c_masks": masks, "c_sel": sel, "c_rope": rope}


_INS = ["x", "c", "ctx", "c_ctx", "w_mod", "b_mod", "ln_g", "ln_b", "mla_w_in", "mla_q_norm", "mla_kv_norm", "mla_w_uq",
        "mla_w_uk", "mla_w_uv", "mla_w_out", "s5_w_in", "s5_lam_re", "s5_lam_im", "s5_log_dt", "s5_b_re", "s5_b_im",
        "s5_c_re", "s5_c_im", "s5_d", "s5_w_glu", "s5_b_glu", "s5_w_out", "norm1_g_2", "w_in_2", "q_norm_g_2",
        "k_norm_g_2", "w_branch_a_2", "w_branch_b_2", "w_out_2", "norm2_g_2", "w_ffn_up_2", "ffn_conv_w_2",
        "ffn_conv_b_2", "w_ffn_down_2"]


def kernel(**inputs):
    import concourse.bacc as _bacc
    from concourse.bass_utils import run_bass_kernel_spmd as _run

    arrays = {n: np.ascontiguousarray(inputs[n]) for n in _INS}
    arrays.update(tables())
    rel = np.asarray(inputs["rel_bias_2"])[0]
    arrays["c_rel"] = np.ascontiguousarray(rel[:, np.clip(255 - np.arange(384), -MAX_REL, MAX_REL) + MAX_REL])

    counts, places = None, {}
    for _ in range(2):
        nc = _bacc.Bacc("TRN2", target_bir_lowering=False, num_devices=1)
        aps = {n: nc.dram_tensor("in_" + n, v.shape, F32, kind="ExternalInput").ap() for n, v in arrays.items()}
        o = nc.dram_tensor("out", (1, T, D), F32, kind="ExternalOutput").ap()
        counts = build(nc, aps, o, counts, places)
    r = _run(nc, [{"in_" + n: v for n, v in arrays.items()}], core_ids=[0])
    return r.results[0]["out"]
```

```python
from contextlib import ExitStack

import numpy as np

import concourse.bass as bass
from concourse import mybir

F32 = mybir.dt.float32
I32 = mybir.dt.int32
ALU = mybir.AluOpType
ACT = mybir.ActivationFunctionType
AX = mybir.AxisListType.X

P = 128
D = 1024
KD = D // P
T = 256
NTT = 4
E = 2 * D
KE = E // P
DEPTH = 2
ALPHA = (2.0 * DEPTH) ** 0.25
EPS = 1e-6

H = 16
NOPE, ROPE, QR, KVR = 128, 64, 256, 128
HEAD_IN = QR + KVR + ROPE
MLA_SCALE = (NOPE + ROPE) ** -0.5
GRID_W = 64

GS, NG, NP = 16, 128, 64
L = 8
NC = 2 * T // L
NCL = T // L
GQ = 8
NQ = NG // 2 // GQ
TWO_PI = 2.0 * np.pi
PI_1, PI_2 = 6.28125, float(np.float32(TWO_PI - 6.28125))
PI_3 = float(TWO_PI - 6.28125 - np.float64(np.float32(TWO_PI - 6.28125)))
LN2_1 = 0.693359375
LN2_2 = float(np.log(2.0) - 0.693359375)
ROUND = 12582912.0

NH2, HD = 8, 64
MAX_REL = 128
FF = 2816
KF = FF // P
LOW = -1e30

SLOTS, SLOT = 3, KD * 512

VECTORS = {"cond": 2 * KD, "q_norm": 2, "s5_d": KE, "b_glu": 2 * KE, "norm1": KD, "norm2": KD, "q_gain": 1, "k_gain": 1,
           "conv_b": 2 * KF, "conv_w0": 2 * KF, "conv_w1": 2 * KF, "conv_w2": 2 * KF}


def vector_rows():
    at, n = {}, 0
    for name, rows in VECTORS.items():
        at[name] = n
        n += rows
    return at, n


VROW, NVROW = vector_rows()


SHARED = {"qnT_mm": "transposed", "ckvT_mm": "transposed", "krT_mm": "transposed", "colv_mm": "transposed",
          "lamT_mm": "transposed", "xT_mm": "transposed", "sa_mm": "scores", "s_mm": "scores", "pat_mm": "probs_turned",
          "pt_mm": "probs_turned", "out0_mm": "out_sum", "out1_mm": "out_sum", "out2_mm": "out_sum", "down_mm": "out_sum",
          "out0_k": "out_part", "out1_k": "out_part", "down_k": "out_part", "oa_mm": "attended", "ob_mm": "attended",
          "res0": "residual", "res1": "residual", "res2": "residual", "res3": "residual", "res0_a": "scaled",
          "res1_a": "scaled", "var0": "variance", "var1": "variance", "x1": "normalized", "x2": "normalized",
          "std0_0": "root", "std0_1": "root", "std0_2": "root", "std0_3": "root", "std1_0": "root", "std1_1": "root",
          "qk_rms": "root", "rms": "root", "lat_rms": "root", "qn": "latent", "ckv": "latent", "kr": "latent",
          "kr_pos": "latent", "qrp_a": "rope_part", "qrp_b": "rope_part", "nmax": "row_max", "nmax_a": "row_max",
          "pn": "probs", "pan": "probs", "pt": "probsT", "pat": "probsT", "gate": "gates", "gs": "gates",
          "gates": "gates", "p": "exps", "pa": "exps", "qnT": "latentT", "ckvT": "latentT", "lat_ss": "squares", "lat_sq": "squares", "x_sq": "squares",
          "qk_sq": "squares", "va": "value", "vb": "value", "oa": "attendedT", "ob": "attendedT"}


class Signals:

    def __init__(self, nc, stack, counts):
        self.nc, self.stack, self.known = nc, stack, counts
        self.sems, self.total, self.seen = {}, {}, {}

    def sem(self, name):
        name = SHARED.get(name, name)
        if name not in self.sems:
            self.sems[name] = self.stack.enter_context(self.nc.semaphore(name))
        return self.sems[name]

    def up(self, name, key=None, by=1):
        shared = SHARED.get(name, name)
        self.total[shared] = self.total.get(shared, 0) + by
        self.seen[(name, key)] = self.total[shared]
        return self.sem(name), by

    def at(self, name, key=None):
        return self.sem(name), 1 if self.known is None else self.known[(name, key)]

    def last(self, name):
        return self.sem(name), self.total[name]


def over(ap, *steps):
    return bass.AP(tensor=ap.tensor, offset=ap.offset, ap=[list(ap.ap[0])] + [list(s) for s in steps])


def dview(ap, offset, *steps):
    return bass.AP(tensor=ap.tensor, offset=ap.offset + offset, ap=[list(s) for s in steps])


def build(nc, a, out, counts, places):
    with ExitStack() as stack:
        S = Signals(nc, stack, counts)
        block = stack.enter_context(nc.Block())
        sb = stack.enter_context(nc.sbuf_tensor("memory", [P, 53200], F32))
        banks = [stack.enter_context(nc.psum_tensor(f"bank{i}", [P, 512], F32))[:, :] for i in range(8)]
        u_dram = nc.dram_tensor("u_scratch", [E, 2 * T], F32).ap()
        k_dram = nc.dram_tensor("k_scratch", [NG, GS, 15 * GS], F32).ap()
        y_dram = nc.dram_tensor("y_scratch", [E, T], F32).ap()

        def carve(start):
            at = [start]

            def take(*shape):
                n = int(np.prod(shape))
                assert at[0] + n <= 53200, (at[0] + n, shape)
                v = sb[:, at[0]:at[0] + n]
                at[0] += n
                if len(shape) > 1:
                    names = " ".join("abcde"[:len(shape)])
                    v = v.rearrange(f"p ({names}) -> p {names}", **{"abcde"[i]: shape[i] for i in range(len(shape))})
                return v
            return take, at

        take, at = carve(0)
        x = take(NTT, D)
        ident = take(P)
        colv = take(3, P)
        sel = take(2, P)
        condT = take(2 * KD)
        shsc = take(2 * KD, 2)
        gtb = take(2, D)
        modrow = take(2, 512)
        bmod = take(2, 512)
        small = take(256)
        ring_at = at[0]
        ring = take(SLOTS, SLOT)
        hT = take(KD, 2 * T)
        arena = at[0]

        take, at = carve(arena)
        gT = take(H, 2 * T)
        wukv = take(2, H * P)
        lnbc0 = wukv.rearrange("p a n -> p (a n)")[:, 0:2 * D].rearrange("p (a n) -> p a n", a=2)
        qrfT = take(4, 2 * T)
        qrpT = take(4, T)
        qrf = take(2, 512)
        qrp = take(512)
        qrt = take(512)
        qT = take(2, 512)
        kT = take(2, 512)
        PT = take(2, 3, 512)
        olT = take(512)
        vrows = kT.rearrange("p a n -> p (a n)")[:, 0:3 * P].rearrange("p (a n) -> p a n", a=3)
        qn = take(NTT, QR)
        ckv = take(NTT, KVR)
        ckvT = take(2 * T)
        qnT = take(2, 2 * T)
        kr = take(NTT, 2, ROPE)
        krt = qrp[:, 0:2 * ROPE].rearrange("p (a n) -> p a n", a=2)
        krT = take(2 * T)
        kvg = take(KVR)
        rope = take(2, 2, ROPE)
        sq = qrt
        hT_flat = hT.rearrange("p a n -> p (a n)")
        pl = hT_flat[:, 0:2048].rearrange("p (b t n) -> p b t n", b=2, t=2)
        pc = hT_flat[:, 2048:3072].rearrange("p (b t n) -> p b t n", b=2, t=2)
        st0 = small[:, 0:64]

        take, at = carve(arena)
        gsT = take(KE, T)
        lam = take(2, P)
        ldt = take(2)
        dts = take(16)
        lamT = take(4, P)
        lamL = take(2, 2, 64)
        lamN = take(2, 2, 64)
        wR = take(2, 2, 64)
        wN = take(2, 2, 64)
        powR = take(8, P)
        powN = x[:, 2:4, :].rearrange("p t n -> p (t n)").rearrange("p (j q r n) -> p j q r n", j=8, q=NQ, r=2)
        ust = take(2, 2 * T)
        braw = take(2, 2 * GQ * 2 * GS)
        bbar = take(2, GQ, 2, GS)
        bbd = take(2, 2 * GQ * 4 * GS)
        cn = take(2, 4 * P)
        kt = take(2, 15 * GS)
        tmpd = take(2, 2, 2 * GQ * GS)
        tmpp = take(2, 2, 2 * GQ * GS)
        y_sb = take(2, 2 * GQ * NCL)
        mbt = take(2, 2, 4, P)
        tt_sb = take(2, 2 * GQ * P)
        scan = ust.rearrange("p a n -> p (a n)").rearrange("p (i d n) -> p i d n", i=2, d=2)
        sc_at = at[0]
        mb = take(2, GQ, 2, L, GS)
        end_l1 = at[0]
        take, at = carve(sc_at)
        sc_a = take(14, P)
        take, at = carve(ring_at)
        mc = take(2, 2 * GQ * 2 * 9 * GS)
        u_sb = take(2, 2 * GQ * NC)
        xs = take(2, NC * 4 * GQ)
        assert at[0] <= arena

        def turn(v, q, pattern, **sizes):
            return v[:, q % 2].rearrange(f"p ({pattern}) -> p {pattern}", **sizes)

        braw_ = lambda q: turn(braw, q, "d g r s", d=2, g=GQ, r=2)
        bbd_ = lambda q: turn(bbd, q, "d g r n", d=2, g=GQ, r=2)
        cn_ = lambda q: turn(cn, q, "r d n", r=2, d=2)
        y_ = lambda q: turn(y_sb, q, "h g c", h=2, g=GQ)
        tt_ = lambda q: turn(tt_sb, q, "h g n", h=2, g=GQ)
        mc_ = lambda q: turn(mc, q, "d g r e s", d=2, g=GQ, r=2, e=9)
        u_ = lambda q: turn(u_sb, q, "h g c", h=2, g=GQ)
        xs_ = lambda q: turn(xs, q, "k r d g", k=NC, d=2, r=2)
        take, at = carve(arena + KE * T + KE * T + 8 * T)
        yT = hT_flat.rearrange("p (k t) -> p k t", k=KE)
        uT = take(KE, T)
        lnbc1 = take(2, D)
        take, at = carve(arena + KE * T)
        zT = take(KE, T)
        ya = take(2, 2, T)
        yb = take(2, 2, T)
        assert at[0] == arena + KE * T + KE * T + 8 * T

        take, at = carve(arena)
        hn = take(2, D)
        qaT = take(4, T)
        kaT = take(4, T)
        qbT = take(4, T)
        kbT = take(4, T)
        va = take(2, 512)
        vb = take(2, 512)
        ga = take(2, D)
        gb = take(2, D)
        qk_sb = take(2, 512)
        qk_sq = take(2, 512)
        toe = take(NH2, T)
        cst = take(6, P)
        pa = take(2, 384)
        pat = take(2, 384)
        az = take(2, 384)
        lk = take(2, 384)
        oaT = take(4, T)
        obT = take(4, T)
        mixed = take(2, D)
        mT = take(KD, T)
        take, at = carve(arena + 2 * D)
        fT = take(KF, T)
        cg = take(4, 2, T)
        st2 = small[:, 64:128]

        def slot(i, *shape):
            v = ring[:, i % SLOTS, 0:int(np.prod(shape))]
            names = " ".join("abcd"[:len(shape)])
            return v.rearrange(f"p ({names}) -> p {names}", **{"abcd"[j]: shape[j] for j in range(len(shape))})

        def column(name, i=0):
            r = VROW[name] + i
            return colv[:, r // P, r % P:r % P + 1]

        loads, load_no = [], {}

        def load(key, src, shape, freed, parts=None):
            load_no[key] = len(loads)
            loads.append((src, shape, freed, parts))

        def ktiles(w):
            return w.rearrange("(k p) n -> p k n", p=P)

        def mod_loads(l):
            for ct in range(6):
                load(("mod", l, ct), ktiles(a["w_mod"][l])[:, :, ct * 512:(ct + 1) * 512], (KD, 512), ("mod_mm", (l, ct)))

        mod_loads(0)
        w_in0 = ktiles(a["mla_w_in"][0])
        load("head_in", w_in0[:, :, 0:HEAD_IN], (KD, HEAD_IN), ("head_mm", NTT - 1))
        for ct in range(4):
            load(("gate", ct), w_in0[:, :, HEAD_IN + ct * 512:HEAD_IN + (ct + 1) * 512], (KD, 512), ("gate_mm", 4 * ct + 3))
        for hf in range(2):
            load(("uq", hf), ktiles(a["mla_w_uq"][0])[:, :, hf * 1536:(hf + 1) * 1536], (2, 1536), ("q_mm", 8 * hf + 7))
        w_o0 = ktiles(a["mla_w_out"][0])
        for n in range(2):
            for kh in range(2):
                load(("out0", n, kh), w_o0[:, kh * 8:kh * 8 + 8, n * 512:(n + 1) * 512], (KD, 512), ("out0_k", (n, kh)))
        mod_loads(1)
        w_in1 = ktiles(a["s5_w_in"][0])
        for ct in range(8):
            load(("s5in", ct), w_in1[:, :, ct * 512:(ct + 1) * 512], (KD, 512), ("s5in_mm", 4 * ct + 3))
        first_glu = len(loads)
        w_glu = ktiles(a["s5_w_glu"][0])
        for ct in range(4):
            for half in range(2):
                for kh in range(2):
                    c0 = half * E + ct * 512
                    load(("glu", ct, half, kh), w_glu[:, kh * 8:kh * 8 + 8, c0:c0 + 512], (KD, 512),
                         ("glu_k", (ct, half, kh)))
        w_o1 = ktiles(a["s5_w_out"][0])
        for n in range(2):
            for kh in range(2):
                load(("out1", n, kh), w_o1[:, kh * 8:kh * 8 + 8, n * 512:(n + 1) * 512], (KD, 512), ("out1_k", (n, kh)))
        w_in2 = ktiles(a["w_in_2"][0])
        for ct in range(10):
            load(("in2", ct), w_in2[:, :, ct * 512:(ct + 1) * 512], (KD, 512), ("in2_mm", (ct, 1)))
        for b in range(2):
            w = ktiles(a["w_branch_" + "ab"[b] + "_2"][0])
            load(("branch", b), w, (4, D), ("branch_mm", (b, 1, 1)))
        w_o2 = ktiles(a["w_out_2"][0])
        for n in range(2):
            load(("out2", n), w_o2[:, :, n * 512:(n + 1) * 512], (KD, 512), ("out2_mm", (n, 1)))
        w_up = ktiles(a["w_ffn_up_2"][0])
        for f in range(KF // 2):
            parts = [w_up[:, :, half * FF + f * 256:half * FF + (f + 1) * 256] for half in range(2)]
            load(("up", f), None, (2, KD, 256), ("up_mm", (f, 1)), parts)
        w_dn = ktiles(a["w_ffn_down_2"][0])
        for n in range(2):
            for kc in range(3):
                k0, k1 = 8 * kc, min(8 * kc + 8, KF)
                load(("down", n, kc), w_dn[:, k0:k1, n * 512:(n + 1) * 512], (k1 - k0, 512), ("down_k", (n, kc)))

        def weights(eng, key, shape):
            i = load_no[key]
            eng.wait_ge(*S.at(f"slot{i % SLOTS}", i))
            return slot(i, *shape)

        users = []

        def bank(pe, key, freed):
            n = len(users)
            if n >= 8:
                for f in users[n - 8]:
                    pe.wait_ge(*S.at(*f))
            users.append(freed)
            places[key] = n % 8
            return banks[n % 8]

        def at_bank(*key):
            return banks[places.get(key, 0)]

        def modulate_views(l, k, c):
            i = at_bank("xT", l, k)[:, c * T:(c + 1) * T]
            if l == 0:
                return hT[:, k, c * T:(c + 1) * T], i
            return hT[:, k, :].rearrange("p (j s c) -> p s c j", j=L, s=2)[:, 1 - c], i.rearrange("p (c j) -> p c j", j=L)

        @block.tensor
        def _(pe):
            def mm(o, l, r, start, stop, free=False):
                return nc.tensor.matmul(o, l, r, start=start, stop=stop, skip_group_check=free)

            def tr(o, i, n=P):
                return nc.tensor.transpose(o, i, ident[0:n, 0:n])

            pe.wait_ge(*S.at("consts", "first"))
            pe.wait_ge(*S.at("cond_silu"))
            b = bank(pe, ("colv",), [("colv",)])
            for i in range(3):
                n = min(P, NVROW - i * P)
                last = tr(b[:, i * P:i * P + n], vrows[0:n, i, :], n)
            last.then_inc(*S.up("colv_mm"))
            pe.wait_ge(*S.at("condT"))

            def modulation(l):
                for ct in range(6):
                    w = weights(pe, ("mod", l, ct), (KD, 512))
                    b = bank(pe, ("mod", l, ct), [("mod_row", (l, ct))])
                    for k in range(KD):
                        last = mm(b[0:2, :], condT.rearrange("p (c k) -> p c k", c=2)[:, :, k], w[:, k, :], k == 0, k == KD - 1)
                    last.then_inc(*S.up("mod_mm", (l, ct)))
                    pe.wait_ge(*S.at("mod_row", (l, ct)))
                    row = modrow[0:2, ct % 2, :]
                    if ct < 4:
                        b = bank(pe, ("modT", l, ct), [("shsc", (l, ct))])
                        for i in range(4):
                            last = tr(b[:, 2 * i:2 * i + 2], row[:, i * P:(i + 1) * P], 2)
                        last.then_inc(*S.up("modT_mm", (l, ct)))
                    else:
                        for c in range(2 - l):
                            b = bank(pe, ("gtb", l, ct, c), [("gtb", (l, ct, c))])
                            mm(b, sel[0:2, c, :], row, True, True).then_inc(*S.up("gtb_mm", (l, ct, c)))

            def x_transposes(l):
                for k in range(KD):
                    b = bank(pe, ("xT", l, k), [("hT_v" if k % 2 == 0 else "hT_a", (l, k))])
                    for t in range(NTT):
                        pe.wait_ge(*S.at(*(("x_in%d" % t,) if l == 0 else ("x1", t))))
                        last = tr(b[:, t * P:(t + 1) * P], x[:, t, k * P:(k + 1) * P])
                    last.then_inc(*S.up("xT_mm", (l, k)))

            modulation(0)
            x_transposes(0)
            w = weights(pe, "head_in", (KD, HEAD_IN))
            for k in range(KD):
                pe.wait_ge(*S.at("hT_v" if k % 2 == 0 else "hT_a", (0, k)))
            for t in range(NTT):
                b = bank(pe, ("head", t), [("ckv", t), ("qn", t), ("kr", t)])
                for k in range(KD):
                    last = mm(b[:, 0:HEAD_IN], hT[:, k, t * P:(t + 1) * P], w[:, k, :], k == 0, k == KD - 1)
                last.then_inc(*S.up("head_mm", t))
            for ct in range(4):
                w = weights(pe, ("gate", ct), (KD, 512))
                for f in range(4):
                    b = bank(pe, ("gate", 4 * ct + f), [("gate", 4 * ct + f)])
                    for k in range(KD):
                        last = mm(b, w[:, k, f * P:(f + 1) * P], hT[:, k, :], k == 0, k == KD - 1)
                    last.then_inc(*S.up("gate_mm", 4 * ct + f))
            for i in range(2):
                b = bank(pe, ("qnT", i), [("qnT", i)])
                for t in range(NTT):
                    pe.wait_ge(*S.at("qn", t))
                    last = tr(b[:, t * P:(t + 1) * P], qn[:, t, i * P:(i + 1) * P])
                last.then_inc(*S.up("qnT_mm", i))
            b = bank(pe, ("ckvT",), [("ckvT",)])
            for t in range(NTT):
                pe.wait_ge(*S.at("ckv", t))
                last = tr(b[:, t * P:(t + 1) * P], ckv[:, t, :])
            last.then_inc(*S.up("ckvT_mm"))
            b = bank(pe, ("krT",), [("krT",)])
            for t in range(NTT):
                pe.wait_ge(*S.at("kr", t))
                if t < 2:
                    pe.wait_ge(*S.at("kr_pos", t))
                last = tr(b[:, t * P:(t + 1) * P], kr[:, t, :, :].rearrange("p a n -> p (a n)"))
            last.then_inc(*S.up("krT_mm"))
            for i in range(2):
                pe.wait_ge(*S.at("qnT", i))
            pe.wait_ge(*S.at("ckvT"))
            pe.wait_ge(*S.at("krT"))
            pe.wait_ge(*S.at("second"))

            def q_rope(hf):
                w = weights(pe, ("uq", hf), (2, 1536)).rearrange("p k (h n) -> p k h n", n=NOPE + ROPE)
                for t in range(NTT):
                    b = bank(pe, ("qrope", hf, t), [("qrf", (hf, t))] + ([("qrp_a", (hf, t)), ("qrp_b", (hf, t))] if t < 2 else []))
                    for k in range(2):
                        last = mm(b, qnT[:, k, t * P:(t + 1) * P], w[:, k, :, NOPE:], k == 0, k == 1)
                    last.then_inc(*S.up("qrope_mm", (hf, t)))
                    bf = bank(pe, ("qrfT", hf, t), [("qrfT", (hf, t))])
                    pe.wait_ge(*S.at("qrf", (hf, t)))
                    for i in range(4):
                        last = tr(bf[:, i * P:(i + 1) * P], qrf[:, t % 2, i * P:(i + 1) * P])
                    last.then_inc(*S.up("qrfT_mm", (hf, t)))
                    if t < 2:
                        bp = bank(pe, ("qrpT", hf, t), [("qrpT", (hf, t))])
                        pe.wait_ge(*S.at("qrp", (hf, t)))
                        for i in range(4):
                            last = tr(bp[:, i * P:(i + 1) * P], qrp[:, i * P:(i + 1) * P])
                        last.then_inc(*S.up("qrpT_mm", (hf, t)))

            def qk_head(h):
                w = weights(pe, ("uq", h // 8), (2, 1536))
                b = bank(pe, ("q", h), [("qT", h)])
                c = (h % 8) * (NOPE + ROPE)
                for k in range(2):
                    last = mm(b, w[:, k, c:c + NOPE], qnT[:, k, :], k == 0, k == 1)
                last.then_inc(*S.up("q_mm", h))
                b = bank(pe, ("k", h), [("kT", h)])
                mm(b, wukv[:, 0, h * P:(h + 1) * P], ckvT, True, True).then_inc(*S.up("k_mm", h))

            def scores(h):
                hf, r = h // 8, 64 * (h % 2)
                pair = (h % 8) // 2
                pe.wait_ge(*S.at("qT", h))
                pe.wait_ge(*S.at("kT", h))
                for t in range(NTT):
                    pe.wait_ge(*S.at("qrfT", (hf, t)))
                for t in range(2):
                    pe.wait_ge(*S.at("qrpT", (hf, t)))
                q, kk = qT[:, h % 2, :], kT[:, h % 2, :]
                for t in range(2):
                    b = bank(pe, ("s", h, t), [("p", (h, t))])
                    mm(b, q[:, t * P:(t + 1) * P], kk, True, False, True)
                    mm(b[:, 0:T], qrpT[r:r + 64, pair, t * P:(t + 1) * P], krT[r:r + 64, 0:T], False, False, True)
                    last = mm(b[:, T:2 * T], qrfT[r:r + 64, pair, t * P:(t + 1) * P], krT[r:r + 64, T:2 * T], False, True, True)
                    last.then_inc(*S.up("s_mm", (h, t)))
                b = bank(pe, ("s", h, 2), [("p", (h, 3))])
                for t in range(2, 4):
                    o = b[:, (t - 2) * T:(t - 1) * T]
                    mm(o, q[:, t * P:(t + 1) * P], kk[:, T:2 * T], t == 2, False, True)
                    last = mm(o, qrfT[r:r + 64, pair, t * P:(t + 1) * P], krT[r:r + 64, T:2 * T], False, t == 3, True)
                last.then_inc(*S.up("s_mm", (h, 2)))

            def values(h):
                for i in range(2):
                    b = bank(pe, ("pt", h, i), [("pt", (h, i))])
                    for kk in range(2):
                        for t in range(2):
                            pe.wait_ge(*S.at("pn", (h, t)))
                            last = tr(b[:, kk * T + t * P:kk * T + (t + 1) * P], pl[:, h % 2, t, (2 * i + kk) * P:(2 * i + kk + 1) * P])
                    last.then_inc(*S.up("pt_mm", (h, i)))
                b = bank(pe, ("pt", h, 2), [("pt", (h, 2))])
                for kk in range(2):
                    for t in range(2):
                        pe.wait_ge(*S.at("pn", (h, 2 + t)))
                        last = tr(b[:, kk * T + t * P:kk * T + (t + 1) * P], pc[:, h % 2, t, kk * P:(kk + 1) * P])
                last.then_inc(*S.up("pt_mm", (h, 2)))
                b = bank(pe, ("ol", h), [("olT", h)])
                for kk in range(4):
                    pe.wait_ge(*S.at("pt", (h, kk // 2)))
                    mm(b[:, 0:T], ckv[:, kk, :], PT[:, h % 2, kk // 2, (kk % 2) * T:(kk % 2 + 1) * T], kk == 0, False, True)
                pe.wait_ge(*S.at("pt", (h, 2)))
                for kk in range(2):
                    last = mm(b[:, T:2 * T], ckv[:, 2 + kk, :], PT[:, h % 2, 2, kk * T:(kk + 1) * T], False, kk == 1, True)
                last.then_inc(*S.up("ol_mm", h))

            def value_up(h):
                pe.wait_ge(*S.at("olT", h))
                b = bank(pe, ("v", h), [("vg", h)])
                mm(b, wukv[:, 1, h * P:(h + 1) * P], olT, True, True).then_inc(*S.up("v_mm", h))

            for h in range(H + 2):
                if h % 8 == 0 and h < H:
                    if h:
                        pass
                    q_rope(h // 8)
                if h < H:
                    qk_head(h)
                if 1 <= h <= H:
                    values(h - 1)
                if h >= 2:
                    value_up(h - 2)
                if h < H:
                    scores(h)

            for n in range(2):
                bs = []
                for kh in range(2):
                    w = weights(pe, ("out0", n, kh), (KD, 512))
                    for t in range(NTT):
                        if kh == 0:
                            bs.append(bank(pe, ("out0", n, t), [("res0_a", (n, t))]))
                        for k in range(8):
                            pe.wait_ge(*S.at("vg", kh * 8 + k))
                            last = mm(bs[t], gT[:, kh * 8 + k, t * P:(t + 1) * P], w[:, k, :], kh == 0 and k == 0, kh == 1 and k == 7)
                        if kh == 1:
                            last.then_inc(*S.up("out0_k" if t == 3 else "out0_mm", (n, 1) if t == 3 else (n, t)))
                    if kh == 0:
                        last.then_inc(*S.up("out0_k", (n, kh)))

            modulation(1)
            x_transposes(1)
            for k in range(KD):
                pe.wait_ge(*S.at("hT_v" if k % 2 == 0 else "hT_a", (1, k)))
            for ct in range(8):
                if ct == 4:
                    pe.wait_ge(*S.at("lam_ready"))
                    b = bank(pe, ("lamT",), [("lamT",)])
                    for i in range(4):
                        last = tr(b[:, i * P:(i + 1) * P], sc_a[:, 10 + i, :])
                    last.then_inc(*S.up("lamT_mm"))
                w = weights(pe, ("s5in", ct), (KD, 512))
                for f in range(4):
                    b = bank(pe, ("s5in", 4 * ct + f), [("u_sb" if ct < 4 else "gs", 4 * ct + f)])
                    for k in range(KD):
                        if ct < 4:
                            last = mm(b, w[:, k, f * P:(f + 1) * P], hT[:, k, :], k == 0, k == KD - 1)
                        else:
                            r = hT[:, k, :].rearrange("p (j s c) -> p j s c", j=L, s=2)[:, :, 1, :]
                            last = mm(b[:, 0:T], w[:, k, f * P:(f + 1) * P], r, k == 0, k == KD - 1)
                    last.then_inc(*S.up("s5in_mm", 4 * ct + f))

            def c_turned(q):
                pe.wait_ge(*S.at("cn%d" % (q % 2), q))
                b = bank(pe, ("cT", q), [("c0", q)])
                for ri in range(2):
                    for dr in range(2):
                        last = tr(b[:, (2 * ri + dr) * P:(2 * ri + dr + 1) * P], cn_(q)[:, ri, dr, :])
                last.then_inc(*S.up("cT_mm", q))

            def kernels(q):
                pe.wait_ge(*S.at("mc", (q, 1)))
                pe.wait_ge(*S.at("bbd", q))
                b = bank(pe, ("kern", q), [("kt", q)])
                for gg in range(GQ):
                    o = b[32 * (gg % 4):32 * (gg % 4) + 32, (gg // 4) * 240:(gg // 4 + 1) * 240]
                    for dr, c0, e0 in ((1, 0, 1), (0, 112, 0)):
                        for ri in range(2):
                            last = mm(o[:, c0:c0 + 128], bbd_(q)[:, dr, gg, ri, :],
                                      mc_(q)[:, dr, gg, ri, e0:e0 + 8, :].rearrange("p j s -> p (j s)"),
                                      dr == 1 and ri == 0, dr == 0 and ri == 1, True)
                last.then_inc(*S.up("kern_mm", q))

            def additions(q):
                pe.wait_ge(*S.at("u_load%d" % (q % 2), q))
                for s4 in range(GQ // 4):
                    for dr in range(2):
                        for ri in range(2):
                            b = bank(pe, ("mbT", q, s4, dr, ri), [("mbt", (q, s4, dr, ri))])
                            pe.wait_ge(*S.at("mb", (q, dr)))
                            for i in range(4):
                                last = tr(b[:, i * P:(i + 1) * P], mb[:, dr, 4 * s4 + i, ri, :, :].rearrange("p j s -> p (j s)"))
                            last.then_inc(*S.up("mbT_mm", (q, s4, dr, ri)))
                    for dr in range(2):
                        b = bank(pe, ("st", q, s4, dr), [("xs", (q, s4, dr))])
                        for ri in range(2):
                            pe.wait_ge(*S.at("mbt", (q, s4, dr, ri)))
                            for i in range(4):
                                for par in range(2):
                                    last = mm(b[64 * par:64 * par + 64, (4 * ri + i) * NC:(4 * ri + i + 1) * NC],
                                              mbt[:, dr, ri, i, 64 * par:64 * par + 64], u_(q)[:, par, 4 * s4 + i, :],
                                              ri == 0 and i == 0, ri == 1 and i == 3, True)
                        last.then_inc(*S.up("st_mm", (q, s4, dr)))

            def outputs(q):
                pe.wait_ge(*S.at("t_load%d" % (q % 2), q))
                pe.wait_ge(*S.at("states", (q, 20)))
                for par in range(2):
                    b = bank(pe, ("y", q, par), [("y", (q, par))])
                    for gg in range(GQ):
                        mm(b[:, gg * NCL:(gg + 1) * NCL], tt_(q)[:, par, gg, :], u_(q)[:, par, gg, NCL:NC], gg == 0, False, True)
                    r = slice(64 * par, 64 * par + 64)
                    for gg in range(GQ):
                        for dr in range(2):
                            for ri in range(2):
                                st = xs_(q)[r, NCL - 1:NC - 1, ri, dr, gg] if dr == 0 else xs_(q)[r, NC - 2:NCL - 2:-1, ri, dr, gg]
                                e0 = 1 - dr
                                last = mm(b[:, gg * NCL:(gg + 1) * NCL],
                                          mc_(q)[r, dr, gg, ri, e0:e0 + 8, :].rearrange("p j s -> p (j s)"), st,
                                          False, gg == GQ - 1 and dr == 1 and ri == 1, True)
                    last.then_inc(*S.up("y_mm", (q, par)))

            c_turned(0)
            c_turned(1)
            additions(0)
            kernels(0)
            for q in range(NQ):
                if q + 1 < NQ:
                    additions(q + 1)
                    kernels(q + 1)
                outputs(q)
                if q + 2 < NQ:
                    c_turned(q + 2)

            for ct in range(4):
                for half in range(2):
                    bs = []
                    for kh in range(2):
                        w = weights(pe, ("glu", ct, half, kh), (KD, 512))
                        for f in range(4):
                            if kh == 0 and f % 2 == 0:
                                bs.append(bank(pe, ("glu", ct, half, f // 2), [("glu_a" if half == 0 else "glu_b", (ct, 2 * (f // 2) + 1))]))
                            for k in range(8):
                                if ct == 0 and half == 0 and f == 0:
                                    pe.wait_ge(*S.at("gelu", kh * 8 + k))
                                last = mm(bs[f // 2][:, (f % 2) * T:(f % 2 + 1) * T], w[:, k, f * P:(f + 1) * P], yT[:, kh * 8 + k, :],
                                          kh == 0 and k == 0 and f % 2 == 0, kh == 1 and k == 7 and f % 2 == 1, True)
                        last.then_inc(*S.up("glu_k", (ct, half, kh)))
            for n in range(2):
                bs = []
                for kh in range(2):
                    w = weights(pe, ("out1", n, kh), (KD, 512))
                    for t in range(2):
                        if kh == 0:
                            bs.append(bank(pe, ("out1", n, t), [("res1_a", (n, t))]))
                        for k in range(8):
                            pe.wait_ge(*S.at("z", kh * 8 + k))
                            last = mm(bs[t], zT[:, kh * 8 + k, t * P:(t + 1) * P], w[:, k, :], kh == 0 and k == 0, kh == 1 and k == 7)
                        if kh == 1 and t == 0:
                            last.then_inc(*S.up("out1_mm", (n, t)))
                    last.then_inc(*S.up("out1_k", (n, kh)))

            def hn_transposes(i):
                for k2 in range(KD // 2):
                    b = bank(pe, ("hnT", i, k2), [("hnT", (i, 2 * k2 + 1))])
                    for k in range(2):
                        for t in range(2):
                            pe.wait_ge(*S.at("hn", (i, t)))
                            last = tr(b[:, k * T + t * P:k * T + (t + 1) * P], hn[:, t, (2 * k2 + k) * P:(2 * k2 + k + 1) * P])
                    last.then_inc(*S.up("hnT_mm", (i, k2)))
                for k in range(KD):
                    pe.wait_ge(*S.at("hnT", (i, k)))

            h2 = hT_flat[:, 0:KD * T].rearrange("p (k t) -> p k t", k=KD)
            hn_transposes(0)
            pe.wait_ge(*S.at("consts2"))

            def project(ct):
                w = weights(pe, ("in2", ct), (KD, 512))
                for t in range(2):
                    freed = {0: "qk_n", 1: "qk_n", 2: "va", 3: "qk_n", 4: "qk_n", 5: "vb"}.get(ct, "gates")
                    b = bank(pe, ("in2", ct, t), [(freed, (ct, t))])
                    for k in range(KD):
                        last = mm(b, h2[:, k, t * P:(t + 1) * P], w[:, k, :], k == 0, k == KD - 1)
                    last.then_inc(*S.up("in2_mm", (ct, t)))

            def qk_transposes(ct):
                for i2 in range(2):
                    b = bank(pe, ("qkT", ct, i2), [("qkT", (ct, i2))])
                    for i in range(2):
                        for t in range(2):
                            pe.wait_ge(*S.at("qk_n", (ct, t)))
                            last = tr(b[:, i * T + t * P:i * T + (t + 1) * P], qk_sb[:, t, (2 * i2 + i) * P:(2 * i2 + i + 1) * P])
                    last.then_inc(*S.up("qkT_mm", (ct, i2)))

            for ct in range(10):
                project(ct)
                if ct in (0, 1, 3, 4):
                    qk_transposes(ct)
            for ct in (0, 1, 3, 4):
                for i in range(2):
                    pe.wait_ge(*S.at("qkT", (ct, i)))

            def score_a(h):
                r, pair = 64 * (h % 2), h // 2
                b = bank(pe, ("sa", h), [("pa", (h, 1))])
                mm(b[:, P:3 * P], cst[:, 0, :], toe[:, h, :], True, False, True)
                mm(b[:, 0:P], cst[:, 0, :], toe[:, h, P:2 * P], False, False, True)
                mm(b[:, 0:P], ident, cst[:, 1, :], False, False, True)
                mm(b[:, 2 * P:3 * P], ident, cst[:, 1, :], False, False, True)
                mm(b[:, 0:P], qaT[r:r + 64, pair, 0:P], kaT[r:r + 64, pair, 0:P], False, False, True)
                last = mm(b[:, P:3 * P], qaT[r:r + 64, pair, P:T], kaT[r:r + 64, pair, :], False, True, True)
                last.then_inc(*S.up("sa_mm", h))

            def pt_a(h):
                b = bank(pe, ("pat", h), [("pat", h)])
                pe.wait_ge(*S.at("pan", (h, 0)))
                pe.wait_ge(*S.at("pan", (h, 1)))
                for i in range(3):
                    last = tr(b[:, i * P:(i + 1) * P], pa[:, h % 2, i * P:(i + 1) * P])
                last.then_inc(*S.up("pat_mm", h))

            attended = {}

            def attend(name, h, v, w, ready):
                r = 64 * (h % 2)
                if h % 2 == 0:
                    attended[name] = bank(pe, (name, h // 2), [(name, h // 2)])
                b = attended[name]
                pe.wait_ge(*S.at(*ready))
                mm(b[r:r + 64, 0:T], v[:, 0, h * HD:(h + 1) * HD], w[:, 0:T], True, False, True)
                last = mm(b[r:r + 64, P:T], v[:, 1, h * HD:(h + 1) * HD], w[:, T:3 * P], False, True, True)
                last.then_inc(*S.up(name + "_mm", h))

            zb = {}

            def score_b(h):
                r, pair = 64 * (h % 2), h // 2
                b = zb[h] = bank(pe, ("z", h), [("wb", h)])
                mm(b[:, 0:T], kbT[r:r + 64, pair, 0:P], qbT[r:r + 64, pair, :], True, False, True)
                last = mm(b[:, T:3 * P], kbT[r:r + 64, pair, P:T], qbT[r:r + 64, pair, P:T], False, False, True)
                last.then_inc(*S.up("z_mm", h))

            def after_b(h):
                b = zb[h]
                pe.wait_ge(*S.at("lk", h))
                w = lk[:, h % 2, :]
                mm(b[:, 0:T], cst[:, 3, :], w[:, 0:T], False, False, True)
                mm(b[:, P:T], cst[:, 4, :], w[:, T:3 * P], False, False, True)
                mm(b[:, T:3 * P], cst[:, 3, :], w[:, T:3 * P], False, False, True)
                mm(b[:, 0:P], ident, cst[:, 5, :], False, False, True)
                last = mm(b[:, T:3 * P], ident, cst[:, 5, :], False, True, True)
                last.then_inc(*S.up("zl_mm", h))

            pe.wait_ge(*S.at("va", (2, 1)))
            pe.wait_ge(*S.at("vb", (5, 1)))
            for h in range(NH2 + 1):
                if h < NH2:
                    score_a(h)
                    score_b(h)
                if h >= 1:
                    pt_a(h - 1)
                    attend("oa", h - 1, va, pat[:, (h - 1) % 2, :], ("pat", h - 1))
                    after_b(h - 1)
                    attend("ob", h - 1, vb, az[:, (h - 1) % 2, :], ("wb", h - 1))

            for k in range(4):
                pe.wait_ge(*S.at("oa", k))
                pe.wait_ge(*S.at("ob", k))
            bs = {}
            for br in range(2):
                w = weights(pe, ("branch", br), (4, D))
                for n in range(2):
                    for t in range(2):
                        b = bank(pe, ("branch", br, n, t), [("mix", (br, n, t))])
                        for k in range(4):
                            last = mm(b, (oaT if br == 0 else obT)[:, k, t * P:(t + 1) * P], w[:, k, n * 512:(n + 1) * 512], k == 0, k == 3)
                        last.then_inc(*S.up("branch_mm", (br, n, t)))
            for k2 in range(KD // 2):
                b = bank(pe, ("mT", k2), [("mT", k2)])
                for k in range(2):
                    kk = 2 * k2 + k
                    for t in range(2):
                        pe.wait_ge(*S.at("mix", (1, kk // 4, t)))
                        last = tr(b[:, k * T + t * P:k * T + (t + 1) * P], mixed[:, t, kk * P:(kk + 1) * P])
                last.then_inc(*S.up("mT_mm", k2))
            for n in range(2):
                w = weights(pe, ("out2", n), (KD, 512))
                for t in range(2):
                    b = bank(pe, ("out2", n, t), [("res2", (n, t))])
                    for k in range(KD):
                        pe.wait_ge(*S.at("mT", k // 2))
                        last = mm(b, mT[:, k, t * P:(t + 1) * P], w[:, k, :], k == 0, k == KD - 1)
                    last.then_inc(*S.up("out2_mm", (n, t)))
            hn_transposes(1)
            for f in range(KF // 2):
                w = weights(pe, ("up", f), (2, KD, 256))
                for half in range(2):
                    b = bank(pe, ("up", f, half), [("conv", (f, half, 1))])
                    for i in range(2):
                        for k in range(KD):
                            last = mm(b[:, i * T:(i + 1) * T], w[:, half, k, i * P:(i + 1) * P], h2[:, k, :],
                                      i == 0 and k == 0, i == 1 and k == KD - 1, True)
                    last.then_inc(*S.up("up_mm", (f, half)))
            for n in range(2):
                bs = []
                for kc in range(3):
                    k0, k1 = 8 * kc, min(8 * kc + 8, KF)
                    w = weights(pe, ("down", n, kc), (k1 - k0, 512))
                    for t in range(2):
                        if kc == 0:
                            bs.append(bank(pe, ("down", n, t), [("res3", (n, t))]))
                        for k in range(k0, k1):
                            pe.wait_ge(*S.at("ffn", k))
                            last = mm(bs[t], fT[:, k, t * P:(t + 1) * P], w[:, k - k0, :], k == 0, k == KF - 1)
                        if kc == 2 and t == 0:
                            last.then_inc(*S.up("down_mm", (n, t)))
                    last.then_inc(*S.up("down_k", (n, kc)))

        @block.scalar
        def _(act):
            A = nc.scalar.activation

            first = [(ident, a["c_ident"][0]), (sel[0:2, :, :], a["c_sel"])]
            rows = [("q_norm", a["mla_q_norm"]), ("s5_d", a["s5_d"]), ("b_glu", a["s5_b_glu"]), ("norm1", a["norm1_g_2"]),
                    ("norm2", a["norm2_g_2"]), ("conv_b", a["ffn_conv_b_2"]),
                    ("conv_w0", a["ffn_conv_w_2"][0, 0:1]), ("conv_w1", a["ffn_conv_w_2"][0, 1:2]), ("conv_w2", a["ffn_conv_w_2"][0, 2:3])]

            def put_rows(row, n, src):
                done = 0
                while done < n:
                    r = row + done
                    m = min(n - done, P - r % P)
                    first.append((vrows[r % P:r % P + m, r // P, :], src[done:done + m, :]))
                    done += m
            for name, v in rows:
                put_rows(VROW[name], VECTORS[name], v[0, :].rearrange("(r n) -> r n", n=P))
            for name, v in (("q_gain", a["q_norm_g_2"]), ("k_gain", a["k_norm_g_2"])):
                r = VROW[name]
                for i in range(2):
                    first.append((vrows[r % P:r % P + 1, r // P, i * HD:(i + 1) * HD], v))
            put_rows(VROW["cond"], KD, a["c"][0, :].rearrange("(r n) -> r n", n=P))
            put_rows(VROW["cond"] + KD, KD, a["c_ctx"].rearrange("(r n) -> r n", n=P))
            for o, i in first:
                act.dma_start(o, i).then_inc(*S.up("consts", "first", by=16))
            for t in range(NTT):
                src = a["x"] if t < 2 else a["ctx"]
                act.dma_start(x[:, t, :], src[0, (t % 2) * P:(t % 2 + 1) * P, :]).then_inc(*S.up("x_in%d" % t, by=16))
            second = [(kvg, dview(a["mla_kv_norm"], 0, (0, P), (1, KVR))), (wukv[:, 0, :], a["mla_w_uk"][0].rearrange("c h d -> c (h d)")),
                      (wukv[:, 1, :], a["mla_w_uv"][0].rearrange("c h d -> c (h d)"))]
            for t in range(2):
                for i in range(2):
                    second.append((rope[:, i, t, :], a["c_rope"][i, t * P:(t + 1) * P, :]))
            for o, i in second:
                act.dma_start(o, i).then_inc(*S.up("second", by=16))
            act.wait_ge(*S.at("consts", "first"))
            A(vrows[0:2 * KD, 0, :], vrows[0:2 * KD, 0, :], ACT.Silu).then_inc(*S.up("cond_silu"))

            def gate_rows(l):
                for ct in range(4, 6):
                    for c in range(2 - l):
                        act.wait_ge(*S.at("gtb_mm", (l, ct, c)))
                        if l == 1:
                            act.wait_ge(*S.at("res0", (1, 3)))
                        A(gtb[:, c, (ct - 4) * 512:(ct - 3) * 512], at_bank("gtb", l, ct, c), ACT.Copy).then_inc(*S.up("gtb", (l, ct, c)))

            def modulated(l):
                for k in range(1, KD, 2):
                    act.wait_ge(*S.at("xT_mm", (l, k)))
                    act.wait_ge(*S.at("shsc", (l, 3)))
                    for c in range(2):
                        o, i = modulate_views(l, k, c)
                        ins = A(o, i, ACT.Identity, bias=shsc[:, k, c:c + 1], scale=shsc[:, KD + k, c:c + 1])
                    ins.then_inc(*S.up("hT_a", (l, k)))

            gate_rows(0)
            modulated(0)
            for t in range(NTT):
                act.wait_ge(*S.at("head_mm", t))
                if t:
                    act.wait_ge(*S.at("lat_ss", t - 1))
                b = at_bank("head", t)
                A(sq[:, 0:QR], b[:, 0:QR], ACT.Square, accum_out=st0[:, t:t + 1]).then_inc(*S.up("lat_sq", t))
                act.wait_ge(*S.at("lat_sq", t))
                A(sq[:, 0:KVR], b[:, QR:QR + KVR], ACT.Square, accum_out=st0[:, 4 + t:5 + t]).then_inc(*S.up("lat_ss", t))
            act.wait_ge(*S.at("lat_ms"))
            A(st0[:, 16:24], st0[:, 8:16], ACT.Sqrt).then_inc(*S.up("lat_rms"))
            for f in range(H):
                act.wait_ge(*S.at("gate_mm", f))
                A(gT[:, f, :], at_bank("gate", f), ACT.Silu).then_inc(*S.up("gate", f))
            for i in range(2):
                act.wait_ge(*S.at("qnT_mm", i))
                act.wait_ge(*S.at("colv"))
                A(qnT[:, i, :], at_bank("qnT", i), ACT.Copy, scale=column("q_norm", i)).then_inc(*S.up("qnT", i))
            act.wait_ge(*S.at("ckvT_mm"))
            A(ckvT, at_bank("ckvT"), ACT.Copy).then_inc(*S.up("ckvT"))

            def q_rope(hf):
                for t in range(NTT):
                    act.wait_ge(*S.at("qrope_mm", (hf, t)))
                    if hf or t >= 2:
                        act.wait_ge(*S.at("qrfT_mm", (hf, t - 2) if t >= 2 else (hf - 1, t + 2)))
                    A(qrf[:, t % 2, :], at_bank("qrope", hf, t), ACT.Copy).then_inc(*S.up("qrf", (hf, t)))
                    act.wait_ge(*S.at("qrfT_mm", (hf, t)))
                    if hf:
                        act.wait_ge(*S.at("s_mm", (7, 2)))
                    A(qrfT[:, :, t * P:(t + 1) * P], at_bank("qrfT", hf, t).rearrange("p (i t) -> p i t", i=4), ACT.Copy).then_inc(*S.up("qrfT", (hf, t)))
                    if t < 2:
                        act.wait_ge(*S.at("qrpT_mm", (hf, t)))
                        A(qrpT[:, :, t * P:(t + 1) * P], at_bank("qrpT", hf, t).rearrange("p (i t) -> p i t", i=4), ACT.Copy).then_inc(*S.up("qrpT", (hf, t)))

            def head(h):
                act.wait_ge(*S.at("q_mm", h))
                if h >= 2:
                    act.wait_ge(*S.at("s_mm", (h - 2, 2)))
                A(qT[:, h % 2, :], at_bank("q", h), ACT.Copy).then_inc(*S.up("qT", h))

            def softmax(h):
                for t in range(NTT):
                    act.wait_ge(*S.at("nmax", h))
                    b = at_bank("s", h, min(t, 2))
                    i = b if t < 2 else b[:, (t - 2) * T:(t - 1) * T]
                    o = pl[:, h % 2, t, :] if t < 2 else pc[:, h % 2, t - 2, :]
                    if h >= 2:
                        act.wait_ge(*S.at("pt_mm", (h - 2, 2)))
                    act.wait_ge(*S.at("gate_mm", H - 1))
                    A(o, i, ACT.Exp, bias=st0[:, 24 + 4 * (h % 2) + t:25 + 4 * (h % 2) + t], scale=MLA_SCALE,
                            accum_out=st0[:, 32 + 4 * (h % 2) + t:33 + 4 * (h % 2) + t]).then_inc(*S.up("p", (h, t)))

            for h in range(H + 1):
                if h < H:
                    if h % 8 == 0:
                        q_rope(h // 8)
                    head(h)
                if h >= 1:
                    g = h - 1
                    act.wait_ge(*S.at("pt_mm", (g, 2)))
                    A(PT[:, g % 2, 2, :], at_bank("pt", g, 2), ACT.Copy).then_inc(*S.up("pt2", g))
                    act.wait_ge(*S.at("ol_mm", g))
                    if g >= 1:
                        act.wait_ge(*S.at("v_mm", g - 1))
                    A(olT, at_bank("ol", g), ACT.Copy).then_inc(*S.up("olT", g))
                if h < H:
                    softmax(h)

            act.wait_ge(*S.at("v_mm", H - 1))
            for i, nm in enumerate(("ln_g", "ln_b")):
                act.dma_start(lnbc0[:, i, :], dview(a[nm], 0, (0, P), (1, D))).then_inc(*S.up("lnbc0", by=16))

            def roots(name, key, o, i):
                act.wait_ge(*S.at(*key))
                A(o, i, ACT.Sqrt).then_inc(*S.up(name))

            for t in range(NTT):
                roots("std0_%d" % t, ("var0", t), small[:, 160 + t:161 + t], small[:, 152 + t:153 + t])
            gate_rows(1)
            modulated(1)
            act.wait_ge(*S.at("theta"))
            A(sc_a[:, 6, :], sc_a[:, 2, :], ACT.Sin).then_inc(*S.up("sin", 0))
            A(sc_a[:, 7, :], sc_a[:, 2, :], ACT.Sin, scale=0.5).then_inc(*S.up("sin", 1))
            for f in range(16):
                act.wait_ge(*S.at("s5in_mm", f))
                if f >= 2:
                    act.wait_ge(*S.at("u_out%d" % (f % 2), f - 2))
                A(ust[:, f % 2, :], at_bank("s5in", f), ACT.Copy).then_inc(*S.up("u_sb", f))
                act.wait_ge(*S.at("u_sb", f))
                act.dma_start(u_dram[f * P:(f + 1) * P, :], ust[:, f % 2, :]).then_inc(*S.up("u_out%d" % (f % 2), f, by=16))
            for f in range(16, 32):
                act.wait_ge(*S.at("s5in_mm", f))
                A(gsT[:, f - 16, :], at_bank("s5in", f)[:, 0:T], ACT.Silu).then_inc(*S.up("gs", f))

            def c_conjugated(q):
                act.wait_ge(*S.at("cT_mm", q))
                if q < 2:
                    act.wait_ge(*S.at("s5in_mm", 31))
                else:
                    act.wait_ge(*S.at("y_mm", (q - 2, 1)))
                b = at_bank("cT", q).rearrange("p (r d g s) -> p r d g s", r=2, d=2, s=GS)
                for ri in range(2):
                    for dr in range(2):
                        ins = A(mc_(q)[:, dr, :, ri, 8 * dr, :], b[:, ri, dr], ACT.Copy, scale=-1.0 if ri else 1.0)
                ins.then_inc(*S.up("c0", q))

            def kernels(q):
                act.wait_ge(*S.at("kern_mm", q))
                if q:
                    act.wait_ge(*S.at("k_out", q - 1))
                A(kt, at_bank("kern", q)[:, 0:480].rearrange("p (a n) -> p a n", a=2), ACT.Copy).then_inc(*S.up("kt", q))
                act.wait_ge(*S.at("kt", q))
                for gi in range(4):
                    for par in range(2):
                        g0 = par * 64 + q * GQ + gi
                        r = 32 * gi + 16 * par
                        act.dma_start(k_dram[g0:g0 + 5:4, :, :].rearrange("g s n -> s g n"), kt[r:r + 16, :, :]).then_inc(*S.up("k_out", q, by=16))

            def additions(q):
                for s4 in range(GQ // 4):
                    for dr in range(2):
                        for ri in range(2):
                            act.wait_ge(*S.at("mbT_mm", (q, s4, dr, ri)))
                            if s4 or q:
                                act.wait_ge(*S.at("st_mm", (q, s4 - 1, dr) if s4 else (q - 1, GQ // 4 - 1, dr)))
                            A(mbt[:, dr, ri, :, :], at_bank("mbT", q, s4, dr, ri).rearrange("p (i n) -> p i n", i=4), ACT.Copy).then_inc(*S.up("mbt", (q, s4, dr, ri)))
                    for dr in range(2):
                        act.wait_ge(*S.at("st_mm", (q, s4, dr)))
                        if q >= 2:
                            act.wait_ge(*S.at("y_mm", (q - 2, 1)))
                        b = at_bank("st", q, s4, dr).rearrange("p (r g c) -> p r g c", r=2, g=4)
                        o = xs_(q)[:, :, :, dr, 4 * s4:4 * s4 + 4].rearrange("p k r g -> p r g k")
                        if dr == 0:
                            ins = A(o, b, ACT.Copy)
                        else:
                            A(o[:, :, :, 0:NCL], b[:, :, :, NCL - 1::-1], ACT.Copy)
                            ins = A(o[:, :, :, NCL:NC], b[:, :, :, NC - 1:NCL - 1:-1], ACT.Copy)
                        ins.then_inc(*S.up("xs", (q, s4, dr)))

            def outputs(q):
                for par in range(2):
                    act.wait_ge(*S.at("y_mm", (q, par)))
                    if q >= 2:
                        act.wait_ge(*S.at("y_out%d" % (q % 2), q - 2))
                    A(y_(q)[:, par, :, :], at_bank("y", q, par)[:, 0:GQ * NCL].rearrange("p (g c) -> p g c", g=GQ), ACT.Copy).then_inc(*S.up("y", (q, par)))
                act.wait_ge(*S.at("y", (q, 1)))
                for j in range(L):
                    for par in range(2):
                        f0 = (par * 64 + q * GQ) * GS
                        dst = dview(y_dram, f0 * T + j * NCL, (T, GS), (GS * T, GQ), (1, NCL))
                        act.dma_start(dst, y_(q)[16 * j:16 * j + 16, par, :, :]).then_inc(*S.up("y_out%d" % (q % 2), q, by=16))

            c_conjugated(0)
            c_conjugated(1)
            additions(0)
            kernels(0)
            for q in range(NQ):
                if q + 1 < NQ:
                    additions(q + 1)
                    kernels(q + 1)
                outputs(q)
                if q + 2 < NQ:
                    c_conjugated(q + 2)

            for k in range(KE):
                act.wait_ge(*S.at("y_d", k))
                A(yT[:, k, :], yT[:, k, :], ACT.Gelu_apprx_tanh).then_inc(*S.up("gelu", k))
            for ct in range(4):
                for f in range(4):
                    act.wait_ge(*S.at("glu_k", (ct, 1, 1)))
                    i = 4 * ct + f
                    if i >= 4:
                        act.wait_ge(*S.at("z", i - 4))
                    A(yb.rearrange("p a b t -> p (a b) t")[:, i % 4, :], at_bank("glu", ct, 1, f // 2)[:, (f % 2) * T:(f % 2 + 1) * T], ACT.Sigmoid,
                            bias=column("b_glu", KE + i)).then_inc(*S.up("glu_b", (ct, f)))
            for i, nm in enumerate(("ln_g", "ln_b")):
                act.wait_ge(*S.at("gelu", KE - 1))
                act.dma_start(lnbc1[:, i, :], dview(a[nm], D, (0, P), (1, D))).then_inc(*S.up("lnbc1", by=16))
            for t in range(2):
                roots("std1_%d" % t, ("var1", t), small[:, 160 + t:161 + t], small[:, 152 + t:153 + t])

            def rms(i):
                for t in range(2):
                    act.wait_ge(*S.at("x_rms", (i, t)))
                    A(hn[:, t, :], x[:, t, :], ACT.Square, accum_out=st2[:, t:t + 1]).then_inc(*S.up("x_sq", (i, t)))
                    act.wait_ge(*S.at("x_sq", (i, t)))
                    A(st2[:, 2 + t:3 + t], st2[:, t:t + 1], ACT.Sqrt, scale=1.0 / D, bias=small[:, 200:201]).then_inc(*S.up("rms", (i, t)))

            act.wait_ge(*S.at("eps"))
            rms(0)
            for k in range(KD):
                act.wait_ge(*S.at("hnT_mm", (0, k // 2)))
                A(h2v(hT_flat)[:, k, :], at_bank("hnT", 0, k // 2)[:, (k % 2) * T:(k % 2 + 1) * T], ACT.Copy, scale=column("norm1", k)).then_inc(*S.up("hnT", (0, k)))
            act.wait_ge(*S.at("hnT", (0, 0)))
            act.dma_start(cst, a["c_masks"].rearrange("m p n -> p m n")).then_inc(*S.up("consts2", by=16))
            act.dma_start(toe, dview(a["c_rel"], 0, (1, P), (384, NH2), (1, T))).then_inc(*S.up("consts2", by=16))
            for ct in range(10):
                for t in range(2):
                    act.wait_ge(*S.at("in2_mm", (ct, t)))
                    b = at_bank("in2", ct, t)
                    if ct in (0, 1):
                        if ct:
                            act.wait_ge(*S.at("qk_ss", (ct - 1, t)))
                        A(qk_sq[:, t, :], b, ACT.Square).then_inc(*S.up("qk_sq", (ct, t)))
                        act.wait_ge(*S.at("qk_ss", (ct, t)))
                        A(st2[:, 24 + 8 * t:32 + 8 * t], st2[:, 8 + 8 * t:16 + 8 * t], ACT.Sqrt, scale=1.0 / HD, bias=small[:, 200:201]).then_inc(*S.up("qk_rms", (ct, t)))
                    elif ct == 2:
                        A(va[:, t, :], b, ACT.Copy).then_inc(*S.up("va", (ct, t)))
                    elif ct == 5:
                        A(vb[:, t, :], b, ACT.Copy).then_inc(*S.up("vb", (ct, t)))
                    elif ct >= 6:
                        g = ga if ct < 8 else gb
                        A(g[:, t, (ct % 2) * 512:(ct % 2 + 1) * 512], b, ACT.Sigmoid).then_inc(*S.up("gates", (ct, t)))
                if ct in (0, 1, 3, 4):
                    o = {0: qaT, 1: kaT, 3: qbT, 4: kbT}[ct]
                    for i2 in range(2):
                        act.wait_ge(*S.at("qkT_mm", (ct, i2)))
                        i = at_bank("qkT", ct, i2).rearrange("p (i t) -> p i t", i=2)
                        sc = {0: small[:, 201:202], 1: column("k_gain"), 3: HD ** -0.5, 4: 1.0}[ct]
                        A(o[:, 2 * i2:2 * i2 + 2, :], i, ACT.Copy, scale=sc).then_inc(*S.up("qkT", (ct, i2)))

            for h in range(NH2 + 1):
                if h < NH2:
                    act.wait_ge(*S.at("nmax_a", h))
                    if h >= 2:
                        act.wait_ge(*S.at("pat_mm", h - 2))
                    b = at_bank("sa", h)
                    for t, (c0, c1) in enumerate(((0, P), (P, 3 * P))):
                        i = 40 + 2 * (h % 2) + t
                        A(pa[:, h % 2, c0:c1], b[:, c0:c1], ACT.Exp, bias=st2[:, i:i + 1], accum_out=st2[:, i + 4:i + 5]).then_inc(*S.up("pa", (h, t)))
                    act.wait_ge(*S.at("z_mm", h))
                    if h >= 2:
                        act.wait_ge(*S.at("ob_mm", h - 2))
                    A(az[:, h % 2, :], at_bank("z", h)[:, 0:384], ACT.Abs).then_inc(*S.up("az", h))
                    act.wait_ge(*S.at("az", h))
                    A(az[:, h % 2, :], az[:, h % 2, :], ACT.Exp, scale=-1.0).then_inc(*S.up("ez", h))
                    act.wait_ge(*S.at("ez", h))
                    A(az[:, h % 2, :], az[:, h % 2, :], ACT.Ln, bias=1.0).then_inc(*S.up("lz", h))
                if h >= 1:
                    g = h - 1
                    act.wait_ge(*S.at("zl_mm", g))
                    act.wait_ge(*S.at("sp", g))
                    A(az[:, g % 2, :], at_bank("z", g)[:, 0:384], ACT.Exp).then_inc(*S.up("wb", g))
                    if g % 2:
                        for name, o in (("oa", oaT), ("ob", obT)):
                            act.wait_ge(*S.at(name + "_mm", g))
                            A(o[:, g // 2, :], at_bank(name, g // 2)[:, 0:T], ACT.Copy).then_inc(*S.up(name, g // 2))
            for k2 in range(KD // 2):
                act.wait_ge(*S.at("mT_mm", k2))
                A(mT[:, 2 * k2:2 * k2 + 2, :], at_bank("mT", k2).rearrange("p (k t) -> p k t", k=2), ACT.Copy).then_inc(*S.up("mT", k2))
            rms(1)
            for k in range(KD):
                act.wait_ge(*S.at("hnT_mm", (1, k // 2)))
                A(h2v(hT_flat)[:, k, :], at_bank("hnT", 1, k // 2)[:, (k % 2) * T:(k % 2 + 1) * T], ACT.Copy, scale=column("norm2", k)).then_inc(*S.up("hnT", (1, k)))
            for f in range(KF // 2):
                for half in range(2):
                    for i in range(2):
                        fb = half * KF + 2 * f + i
                        n = (2 * f + i) % 4
                        act.wait_ge(*S.at("up_mm", (f, half)))
                        if f >= 2:
                            act.wait_ge(*S.at("ffn", 2 * (f - 2) + i))
                        A(cg[:, n, half, :], at_bank("up", f, half)[:, i * T:(i + 1) * T], ACT.Identity,
                                scale=column("conv_w2", fb), bias=column("conv_b", fb)).then_inc(*S.up("tap2", (f, half, i)))
                for i in range(2):
                    n = (2 * f + i) % 4
                    act.wait_ge(*S.at("conv", (f, 0, i)))
                    A(cg[:, n, 0, :], cg[:, n, 0, :], ACT.Silu).then_inc(*S.up("up_silu", (f, i)))
            for t in range(2):
                act.wait_ge(*S.at("res3", (1, t)))
                act.dma_start(out[0, t * P:(t + 1) * P, :], x[:, t, :]).then_inc(*S.up("stored", t, by=16))
            for t in range(2):
                act.wait_ge(*S.at("stored", t))

        @block.vector
        def _(dve):
            V = nc.vector
            ts, tt, stt = V.tensor_scalar, V.tensor_tensor, V.scalar_tensor_tensor

            def link(ins):
                ins.then_inc(*S.up("vec_link"))
                dve.wait_ge(*S.last("vec_link"))

            link(V.memset(small, EPS))
            dve.wait_ge(*S.at("consts", "first"))
            V.memset(small[:, 200:201], EPS).then_inc(*S.up("eps"))
            dve.wait_ge(*S.at("colv_mm"))
            link(V.tensor_copy(colv.rearrange("p a n -> p (a n)")[:, 0:NVROW], at_bank("colv")[:, 0:NVROW]))
            r = VROW["cond"]
            V.tensor_copy(condT, colv[:, r // P, r % P:r % P + 2 * KD]).then_inc(*S.up("condT"))
            ts(small[:, 201:202], column("q_gain"), HD ** -0.5, None, ALU.mult).then_inc(*S.up("colv"))

            def modulation(l, cts=range(6)):
                for ct in cts:
                    dve.wait_ge(*S.at("mod_mm", (l, ct)))
                    dve.wait_ge(*S.at("bmod%d" % (ct % 2), (l, ct)))
                    if ct >= 2 or l:
                        pl_, pt_ = (l, ct - 2) if ct >= 2 else (l - 1, ct + 4)
                        if pt_ < 4:
                            dve.wait_ge(*S.at("modT_mm", (pl_, pt_)))
                        else:
                            dve.wait_ge(*S.at("gtb_mm", (pl_, pt_, 1 - pl_)))
                    tt(modrow[0:2, ct % 2, :], at_bank("mod", l, ct)[0:2, :], bmod[0:2, ct % 2, :], ALU.add).then_inc(*S.up("mod_row", (l, ct)))
                    if ct < 4:
                        dve.wait_ge(*S.at("modT_mm", (l, ct)))
                        i = at_bank("modT", l, ct)[:, 0:8].rearrange("p (a b) -> p a b", b=2)
                        ts(shsc[:, 4 * ct:4 * ct + 4, :], i, 1.0 if ct >= 2 else 0.0, None, ALU.add).then_inc(*S.up("shsc", (l, ct)))

            def modulated(l):
                dve.wait_ge(*S.at("shsc", (l, 3)))
                for k in range(0, KD, 2):
                    dve.wait_ge(*S.at("xT_mm", (l, k)))
                    for c in range(2):
                        o, i = modulate_views(l, k, c)
                        ins = ts(o, i, shsc[:, KD + k, c:c + 1], shsc[:, k, c:c + 1], ALU.mult, ALU.add)
                    ins.then_inc(*S.up("hT_v", (l, k)))

            modulation(0)
            modulated(0)
            for t in range(NTT):
                dve.wait_ge(*S.at("lat_ss", t))
            link(ts(st0[:, 8:12], st0[:, 0:4], 1.0 / QR, EPS, ALU.mult, ALU.add))
            ts(st0[:, 12:16], st0[:, 4:8], 1.0 / KVR, EPS, ALU.mult, ALU.add).then_inc(*S.up("lat_ms"))
            dve.wait_ge(*S.at("lat_rms"))
            link(V.reciprocal(st0[:, 40:48], st0[:, 16:24]))
            dve.wait_ge(*S.at("second"))
            for t in range(NTT):
                b = at_bank("head", t)
                ts(qn[:, t, :], b[:, 0:QR], st0[:, 40 + t:41 + t], None, ALU.mult).then_inc(*S.up("qn", t))
                stt(ckv[:, t, :], b[:, QR:QR + KVR], st0[:, 44 + t:45 + t], kvg, ALU.mult, ALU.mult).then_inc(*S.up("ckv", t))
                k_r = b[:, QR + KVR:HEAD_IN]
                if t < 2:
                    link(tt(krt[:, 0, :], k_r, rope[:, 0, t, :], ALU.mult))
                    sw = k_r.rearrange("p (a b n) -> p a b n", a=2, b=2)[:, :, ::-1, :]
                    link(tt(krt[:, 1, :].rearrange("p (a b n) -> p a b n", a=2, b=2), sw,
                            rope[:, 1, t, :].rearrange("p (a b n) -> p a b n", a=2, b=2), ALU.mult))
                    tt(kr[:, t, 0, :], krt[:, 0, :], krt[:, 1, :], ALU.add).then_inc(*S.up("kr", t))
                    tt(kr[:, t, 1, :], krt[:, 0, :], krt[:, 1, :], ALU.add).then_inc(*S.up("kr_pos", t))
                    dve.wait_ge(*S.at("kr_pos", t))
                else:
                    link(V.tensor_copy(kr[:, t, 0, :], k_r))
                    V.tensor_copy(kr[:, t, 1, :], k_r).then_inc(*S.up("kr", t))
            dve.wait_ge(*S.at("krT_mm"))
            V.tensor_copy(krT, at_bank("krT")).then_inc(*S.up("krT"))

            def q_rope(hf):
                for t in range(2):
                    dve.wait_ge(*S.at("qrf", (hf, t)))
                    if hf or t:
                        dve.wait_ge(*S.at("qrpT_mm", (hf, t - 1) if t else (hf - 1, 1)))
                    b = at_bank("qrope", hf, t)
                    cos = rope[:, 0, t, :]
                    sin = rope[:, 1, t, :]
                    v = b.rearrange("p (h n) -> p h n", h=8)
                    tt(qrp.rearrange("p (h n) -> p h n", h=8), v, over(cos, (0, 8), (1, ROPE)), ALU.mult).then_inc(*S.up("qrp_a", (hf, t)))
                    for i in range(2):
                        sw = b.rearrange("p (h a b n) -> p h a b n", h=8, a=2, b=2)[:, :, i, ::-1, :]
                        o = qrt.rearrange("p (h a b n) -> p h a b n", h=8, a=2, b=2)[:, :, i]
                        ins = tt(o, sw, over(sin[:, 32 * i:32 * i + 1], (0, 8), (16, 2), (1, 16)), ALU.mult)
                        if i == 0:
                            link(ins)
                    ins.then_inc(*S.up("qrp_b", (hf, t)))
                    dve.wait_ge(*S.at("qrp_a", (hf, t)))
                    dve.wait_ge(*S.at("qrp_b", (hf, t)))
                    tt(qrp, qrp, qrt, ALU.add).then_inc(*S.up("qrp", (hf, t)))

            def head(h):
                dve.wait_ge(*S.at("k_mm", h))
                if h >= 2:
                    dve.wait_ge(*S.at("s_mm", (h - 2, 2)))
                V.tensor_copy(kT[:, h % 2, :], at_bank("k", h)).then_inc(*S.up("kT", h))

            def maxima(h):
                c = 4 * (h % 2)
                if h >= 2:
                    dve.wait_ge(*S.at("p", (h - 2, 3)))
                for t in range(3):
                    dve.wait_ge(*S.at("s_mm", (h, t)))
                    b = at_bank("s", h, t)
                    i = b if t < 2 else b.rearrange("p (t n) -> p t n", t=2)
                    ins = V.tensor_reduce(st0[:, 48 + c + t:49 + c + t + (t == 2)], i, AX, ALU.max)
                    ins.then_inc(*S.up("vec_link"))
                dve.wait_ge(*S.last("vec_link"))
                ts(st0[:, 24 + c:28 + c], st0[:, 48 + c:52 + c], -MLA_SCALE, None, ALU.mult).then_inc(*S.up("nmax", h))

            def norm(h):
                c = 4 * (h % 2)
                for t in range(NTT):
                    dve.wait_ge(*S.at("p", (h, t)))
                link(V.reciprocal(st0[:, 56 + c:60 + c], st0[:, 32 + c:36 + c]))
                for t in range(NTT):
                    o = pl[:, h % 2, t, :] if t < 2 else pc[:, h % 2, t - 2, :]
                    ts(o, o, st0[:, 56 + c + t:57 + c + t], None, ALU.mult).then_inc(*S.up("pn", (h, t)))

            def values(h):
                for i in range(2):
                    dve.wait_ge(*S.at("pt_mm", (h, i)))
                    if h >= 2:
                        dve.wait_ge(*S.at("ol_mm", h - 2))
                    V.tensor_copy(PT[:, h % 2, i, :], at_bank("pt", h, i)).then_inc(*S.up("pt", (h, i)))
                dve.wait_ge(*S.at("pt2", h))
                V.tensor_copy(small[0:1, 250:251], small[0:1, 200:201]).then_inc(*S.up("pt", (h, 2)))

            def gated(h):
                dve.wait_ge(*S.at("v_mm", h))
                dve.wait_ge(*S.at("gate", h))
                tt(gT[:, h, :], at_bank("v", h), gT[:, h, :], ALU.mult).then_inc(*S.up("vg", h))

            for h in range(H + 2):
                if h < H:
                    if h % 8 == 0:
                        q_rope(h // 8)
                    head(h)
                if 1 <= h <= H:
                    values(h - 1)
                if h >= 2:
                    gated(h - 2)
                if h < H:
                    maxima(h)
                    norm(h)

            def residual(l, n, t):
                o = "out%d" % l
                if (l == 0 and t == 3) or (l == 1 and t == 1):
                    dve.wait_ge(*S.at(o + "_k", (n, 1)))
                else:
                    dve.wait_ge(*S.at(o + "_mm", (n, t)))
                cols = slice(n * 512, (n + 1) * 512)
                y = at_bank(o, n, t)
                dve.wait_ge(*S.at("gtb", (l, 5, 0 if (t < 2) else 1)))
                tmp = (qrf[:, t % 2, :] if l == 0 else hT_flat[:, (t % 2) * 512:(t % 2 + 1) * 512])
                tt(tmp, y, gtb[:, t // 2, cols], ALU.mult).then_inc(*S.up("res%d_a" % l, (n, t)))
                dve.wait_ge(*S.at("res%d_a" % l, (n, t)))
                stt(x[:, t, cols], x[:, t, cols], ALPHA, tmp, ALU.mult, ALU.add).then_inc(*S.up("res%d" % l, (n, t)))

            def layernorm(l, nt, lnbc):
                for t in range(nt):
                    dve.wait_ge(*S.at("res%d" % l, (1, t)))
                    for i in range(2):
                        ins = V.bn_stats(small[:, 208 + 6 * i:214 + 6 * i], x[:, t, i * 512:(i + 1) * 512])
                        link(ins)
                    link(V.bn_aggr(small[:, 128 + 2 * t:130 + 2 * t], small[:, 208:220]))
                    ts(small[:, 152 + t:153 + t], small[:, 129 + 2 * t:130 + 2 * t], EPS, None, ALU.add).then_inc(*S.up("var%d" % l, t))
                dve.wait_ge(*S.at("lnbc%d" % l))
                for t in range(nt):
                    dve.wait_ge(*S.at("std%d_%d" % (l, t)))
                    link(V.reciprocal(small[:, 168 + t:169 + t], small[:, 160 + t:161 + t]))
                    link(ts(x[:, t, :], x[:, t, :], small[:, 128 + 2 * t:129 + 2 * t], small[:, 168 + t:169 + t], ALU.subtract, ALU.mult))
                    link(tt(x[:, t, :], x[:, t, :], lnbc[:, 0, :], ALU.mult))
                    tt(x[:, t, :], x[:, t, :], lnbc[:, 1, :], ALU.add).then_inc(*S.up("x%d" % (l + 1), t))
                    if l == 0:
                        modulation(1, [t])

            for n in range(2):
                for t in range(NTT):
                    residual(0, n, t)
            layernorm(0, NTT, lnbc0)
            modulation(1, (4, 5))
            modulated(1)

            dve.wait_ge(*S.at("lam_in"))
            z = lambda i: sc_a[:, i, :]
            d0 = lambda i: dts[:, 2 * i:2 * i + 2]
            link(ts(d0(0), ldt, -150.0, 80.0, ALU.max, ALU.min))
            link(ts(d0(1), d0(0), float(1.0 / np.log(2.0)), ROUND, ALU.mult, ALU.add))
            link(ts(d0(1), d0(1), ROUND, None, ALU.subtract))
            link(stt(d0(2), d0(1), -LN2_1, d0(0), ALU.mult, ALU.add))
            link(stt(d0(2), d0(1), -LN2_2, d0(2), ALU.mult, ALU.add))
            coef = [1.0 / float(np.prod(np.arange(1, n + 1))) for n in range(1, 10)]
            link(ts(d0(3), d0(2), coef[8], None, ALU.mult))
            for n in range(7, -1, -1):
                link(stt(d0(3), d0(3), coef[n], d0(2), ALU.add, ALU.mult))
            link(ts(d0(3), d0(3), 1.0, None, ALU.add))
            link(ts(d0(1), d0(1), 127.0, 0.0, ALU.add, ALU.max))
            ki = d0(4).bitcast(I32)
            link(V.tensor_copy(ki, d0(1)))
            link(ts(ki, ki, 23, None, ALU.logical_shift_left))
            link(tt(d0(5), d0(3), d0(4), ALU.mult))
            link(ts(z(0), lam[:, 0, :], -1e-4, None, ALU.min))
            for par in range(2):
                c = slice(64 * par, 64 * par + 64)
                link(ts(z(1)[:, c], z(0)[:, c], dts[:, 10 + par:11 + par], None, ALU.mult))
                link(ts(z(2)[:, c], lam[:, 1, c], dts[:, 10 + par:11 + par], None, ALU.mult))
            link(ts(z(3), z(2), float(1.0 / TWO_PI), ROUND, ALU.mult, ALU.add))
            link(ts(z(3), z(3), ROUND, None, ALU.subtract))
            for c in (PI_1, PI_2, PI_3):
                link(stt(z(2), z(3), -c, z(2), ALU.mult, ALU.add))
            ts(z(2), z(2), float(np.float32(3.1415925)), float(-np.float32(3.1415925)), ALU.min, ALU.max).then_inc(*S.up("theta"))
            link(ts(z(1), z(1), -88.0, 1.0 / 256, ALU.max, ALU.mult))
            link(ts(z(4), z(1), coef[6], None, ALU.mult))
            for n in range(5, -1, -1):
                link(stt(z(4), z(4), coef[n], z(1), ALU.add, ALU.mult))
            for n in range(8):
                link(stt(z(4), z(4), 2.0, z(4), ALU.add, ALU.mult))
            dve.wait_ge(*S.at("sin", 0))
            dve.wait_ge(*S.at("sin", 1))
            link(tt(z(7), z(7), z(7), ALU.mult))
            link(ts(z(5), z(7), -2.0, 1.0, ALU.mult, ALU.add))
            link(tt(z(5), z(5), z(4), ALU.mult))
            link(stt(z(5), z(7), -2.0, z(5), ALU.mult, ALU.add))
            link(stt(z(11), z(4), 1.0, z(6), ALU.add, ALU.mult))
            link(ts(z(10), z(5), 1.0, None, ALU.add))
            link(tt(z(8), z(0), z(0), ALU.mult))
            link(tt(z(9), lam[:, 1, :], lam[:, 1, :], ALU.mult))
            link(tt(z(8), z(8), z(9), ALU.add))
            link(V.reciprocal(z(8), z(8)))
            link(tt(z(12), z(5), z(0), ALU.mult))
            link(tt(z(9), z(11), lam[:, 1, :], ALU.mult))
            link(tt(z(12), z(12), z(9), ALU.add))
            link(tt(z(12), z(12), z(8), ALU.mult))
            link(tt(z(13), z(11), z(0), ALU.mult))
            link(tt(z(9), z(5), lam[:, 1, :], ALU.mult))
            link(tt(z(13), z(13), z(9), ALU.subtract))
            tt(z(13), z(13), z(8), ALU.mult).then_inc(*S.up("lam_ready"))
            dve.wait_ge(*S.at("lamT_mm"))
            V.tensor_copy(lamT.rearrange("p a n -> p (a n)"), at_bank("lamT")).then_inc(*S.up("lamT"))
            dve.wait_ge(*S.at("lamT"))

            def pairs(oR, oN, re, im):
                v = lambda i: i.rearrange("p (d g) -> p d g", d=2)
                for i in range(2):
                    link(V.tensor_copy(oR[:, :, i, :], v(re)))
                link(ts(oN[:, :, 0, :], v(im), -1.0, None, ALU.mult))
                link(V.tensor_copy(oN[:, :, 1, :], v(im)))

            pairs(lamL, lamN, lamT[:, 0, :], lamT[:, 1, :])
            pairs(wR, wN, lamT[:, 2, :], lamT[:, 3, :])
            for _ in range(3):
                link(tt(z(0), lamT[:, 0, :], lamT[:, 0, :], ALU.mult))
                link(tt(z(1), lamT[:, 1, :], lamT[:, 1, :], ALU.mult))
                link(tt(z(2), lamT[:, 0, :], lamT[:, 1, :], ALU.mult))
                link(tt(lamT[:, 0, :], z(0), z(1), ALU.subtract))
                link(ts(lamT[:, 1, :], z(2), 2.0, None, ALU.mult))
            dve.wait_ge(*S.at("hT_v", (1, KD - 2)))
            dve.wait_ge(*S.at("hT_a", (1, KD - 1)))
            by_block = lambda v: v.rearrange("p (d q g) -> p d q g", d=2, q=NQ)
            flat = lambda v: v.rearrange("p (q n) -> p q n", q=NQ)
            for d in range(2):
                link(V.tensor_copy(powR[:, 0, :].rearrange("p (q d g) -> p d q g", d=2, q=NQ)[:, d], by_block(lamT[:, 0, :])[:, d]))
                link(V.tensor_copy(powN[:, 0, :, 1, :].rearrange("p q (d g) -> p d q g", d=2)[:, d], by_block(lamT[:, 1, :])[:, d]))
            re, im = (lambda j: flat(powR[:, j, :])), (lambda j: powN[:, j, :, 1, :])
            for j in range(8):
                if j:
                    link(tt(flat(z(0)), re(j - 1), re(0), ALU.mult))
                    link(tt(flat(z(1)), im(j - 1), im(0), ALU.mult))
                    link(tt(flat(z(2)), re(j - 1), im(0), ALU.mult))
                    link(tt(flat(z(3)), im(j - 1), re(0), ALU.mult))
                    link(tt(re(j), flat(z(0)), flat(z(1)), ALU.subtract))
                    link(tt(im(j), flat(z(2)), flat(z(3)), ALU.add))
                link(ts(powN[:, j, :, 0, :], im(j), -1.0, None, ALU.mult))
            V.tensor_copy(small[0:1, 251:252], small[0:1, 200:201]).then_inc(*S.up("lam_tables"))

            def power_steps(q):
                dve.wait_ge(*S.at("c0", q))
                gs = slice(q * GQ, (q + 1) * GQ)
                tmp = lambda dr, i: tmpd[:, dr, i, :].rearrange("p (g r s) -> p g r s", g=GQ, r=2)
                for n in range(8):
                    e = lambda dr, i: (n + i) if dr == 0 else (8 - n - i)
                    for dr in range(2):
                        if n:
                            dve.wait_ge(*S.at("mc_power", (q, n - 1, dr)))
                        elif q:
                            dve.wait_ge(*S.at("mc", (q - 1, dr)))
                        lr = over(lamL[:, dr, 0, gs], (1, GQ), (64, 2), (0, GS))
                        tt(tmp(dr, 0), mc_(q)[:, dr, :, :, e(dr, 0), :], lr, ALU.mult).then_inc(*S.up("mc_re", (q, n, dr)))
                        yield
                        ln = over(lamN[:, dr, 1, gs], (1, GQ), (-64, 2), (0, GS))
                        tt(tmp(dr, 1), mc_(q)[:, dr, :, ::-1, e(dr, 0), :], ln, ALU.mult).then_inc(*S.up("mc_im", (q, n, dr)))
                        yield
                    for dr in range(2):
                        dve.wait_ge(*S.at("mc_re", (q, n, dr)))
                        dve.wait_ge(*S.at("mc_im", (q, n, dr)))
                        ins = tt(mc_(q)[:, dr, :, :, e(dr, 1), :], tmp(dr, 0), tmp(dr, 1), ALU.add)
                        ins.then_inc(*(S.up("mc", (q, dr)) if n == 7 else S.up("mc_power", (q, n, dr))))
                        yield

            def state_steps(q, steps, count):
                v = xs_(q).rearrange("p (b i) r d g -> p b i r (d g)", i=8)
                for n, (power, to, of, apart) in enumerate(steps):
                    t = n % 2
                    x_to, x_of = v[:, to[0], to[1]], v[:, of[0], of[1]]
                    nb = count[n]
                    i0 = scan[:, t, 0, 0:nb * 32].rearrange("p (b r n) -> p b r n", b=nb, r=2)
                    i1 = scan[:, t, 1, 0:nb * 32].rearrange("p (b r n) -> p b r n", b=nb, r=2)
                    r = over(powR[:, power - 1, q * 16:q * 16 + 1], (0, nb), (0, 2), (1, 16))
                    m = over(powN[:, power - 1, q, 0, 0:1], (0, nb), (16, 2), (1, 16))
                    if n >= 2 and apart:
                        dve.wait_ge(*S.at("states", (q, n - 2)))
                    elif n:
                        dve.wait_ge(*S.at("states", (q, n - 1)))
                    tt(i0, x_of, r, ALU.mult).then_inc(*S.up("states_re", (q, n)))
                    tt(i1, x_of[:, :, ::-1, :], m, ALU.mult).then_inc(*S.up("states_im", (q, n)))
                    yield
                    dve.wait_ge(*S.at("states_re", (q, n)))
                    tt(i0, x_to, i0, ALU.add).then_inc(*S.up("states_sum", (q, n)))
                    yield
                    dve.wait_ge(*S.at("states_im", (q, n)))
                    dve.wait_ge(*S.at("states_sum", (q, n)))
                    tt(x_to, i0, i1, ALU.add).then_inc(*S.up("states", (q, n)))
                    yield

            for _ in power_steps(0):
                pass
            for q in range(NQ):
                dve.wait_ge(*S.at("xs", (q, 1, 0)))
                dve.wait_ge(*S.at("xs", (q, 1, 1)))
                if q:
                    dve.wait_ge(*S.at("states", (q - 1, 20)))
                steps = [(1, (slice(0, 8), i), (slice(0, 8), i - 1), False) for i in range(1, 8)]
                steps += [(8, (slice(b, b + 1), 7), (slice(b - 1, b), 7), False) for b in range(1, 8)]
                steps += [(i + 1, (slice(4, 8), i), (slice(3, 7), 7), i > 0) for i in range(7)]
                powers = None
                for n, _ in enumerate(state_steps(q, steps, [8] * 7 + [1] * 7 + [4] * 7)):
                    if q + 1 < NQ and n >= 12:
                        if powers is None:
                            powers = power_steps(q + 1)
                        next(powers, None)
                if powers is not None:
                    for _ in powers:
                        pass

            for k in range(KE):
                dve.wait_ge(*S.at("yT_load%d" % (k // 4)))
                stt(yT[:, k, :], uT[:, k, :], column("s5_d", k), yT[:, k, :], ALU.mult, ALU.add).then_inc(*S.up("y_d", k))
            for ct in range(4):
                for f in range(4):
                    i = 4 * ct + f
                    dve.wait_ge(*S.at("glu_k", (ct, 0, 1)))
                    if i >= 4:
                        dve.wait_ge(*S.at("z", i - 4))
                    ts(ya.rearrange("p a b t -> p (a b) t")[:, i % 4, :], at_bank("glu", ct, 0, f // 2)[:, (f % 2) * T:(f % 2 + 1) * T],
                             column("b_glu", i), None, ALU.add).then_inc(*S.up("glu_a", (ct, f)))
                for f in range(4):
                    i = 4 * ct + f
                    dve.wait_ge(*S.at("glu_b", (ct, f)))
                    dve.wait_ge(*S.at("glu_a", (ct, f)))
                    m = ya.rearrange("p a b t -> p (a b) t")[:, i % 4, :]
                    link(tt(m, m, yb.rearrange("p a b t -> p (a b) t")[:, i % 4, :], ALU.mult))
                    jc = lambda v: v.rearrange("p (j c) -> p j c", j=L)
                    tt(zT[:, i, :].rearrange("p (c j) -> p j c", j=L), jc(m), jc(gsT[:, i, :]), ALU.mult).then_inc(*S.up("z", i))
            for n in range(2):
                for t in range(2):
                    residual(1, n, t)
            layernorm(1, 2, lnbc1)

            def rms(i):
                for t in range(2):
                    if i == 0:
                        V.tensor_copy(small[0:1, 252 + t:253 + t], small[0:1, 200:201]).then_inc(*S.up("x_rms", (i, t)))
                for t in range(2):
                    dve.wait_ge(*S.at("rms", (i, t)))
                    link(V.reciprocal(st2[:, 4 + t:5 + t], st2[:, 2 + t:3 + t]))
                    ts(hn[:, t, :], x[:, t, :], st2[:, 4 + t:5 + t], None, ALU.mult).then_inc(*S.up("hn", (i, t)))

            dve.wait_ge(*S.at("x2", 1))
            rms(0)
            for ct in range(6):
                if ct in (2, 5):
                    continue
                for t in range(2):
                    b = at_bank("in2", ct, t)
                    if ct > 0:
                        prev = {1: 0, 3: 1, 4: 3}[ct]
                        dve.wait_ge(*S.at("qkT_mm", (prev, 1)))
                    if ct < 2:
                        dve.wait_ge(*S.at("qk_sq", (ct, t)))
                        V.tensor_reduce(st2[:, 8 + 8 * t:16 + 8 * t], qk_sq[:, t, :].rearrange("p (h d) -> p h d", h=8), AX, ALU.add).then_inc(*S.up("qk_ss", (ct, t)))
                        dve.wait_ge(*S.at("qk_rms", (ct, t)))
                        rr = small[:, 176 + 8 * t:184 + 8 * t]
                        link(V.reciprocal(rr, st2[:, 24 + 8 * t:32 + 8 * t]))
                        tt(qk_sb[:, t, :].rearrange("p (h d) -> p h d", h=8), b.rearrange("p (h d) -> p h d", h=8),
                                 over(rr, (1, 8), (0, HD)), ALU.mult).then_inc(*S.up("qk_n", (ct, t)))
                    else:
                        dve.wait_ge(*S.at("in2_mm", (ct, t)))
                        V.tensor_copy(qk_sb[:, t, :], b).then_inc(*S.up("qk_n", (ct, t)))

            for h in range(NH2 + 1):
                if h < NH2:
                    c = 2 * (h % 2)
                    dve.wait_ge(*S.at("sa_mm", h))
                    if h >= 2:
                        dve.wait_ge(*S.at("pa", (h - 2, 1)))
                    b = at_bank("sa", h)
                    V.tensor_reduce(st2[:, 48 + c:49 + c], b[:, 0:P], AX, ALU.max).then_inc(*S.up("vec_link"))
                    link(V.tensor_reduce(st2[:, 49 + c:50 + c], b[:, P:3 * P], AX, ALU.max))
                    ts(st2[:, 40 + c:42 + c], st2[:, 48 + c:50 + c], -1.0, None, ALU.mult).then_inc(*S.up("nmax_a", h))
                    dve.wait_ge(*S.at("z_mm", h))
                    zz = at_bank("z", h)[:, 0:384]
                    dve.wait_ge(*S.at("lz", h))
                    if h >= 2:
                        dve.wait_ge(*S.at("zl_mm", h - 2))
                    o = lk[:, h % 2, :]
                    stt(o, zz, 0.0, az[:, h % 2, :], ALU.max, ALU.add).then_inc(*S.up("sp", h))
                    dve.wait_ge(*S.at("sp", h))
                    dg = over(o[:, 0:1], (T, 2), (1, P))
                    tt(dg, dg, over(cst[:, 2, 0:1], (0, 2), (1, P)), ALU.mult).then_inc(*S.up("lk", h))
                    for t in range(2):
                        dve.wait_ge(*S.at("pa", (h, t)))
                    link(V.reciprocal(st2[:, 52 + c:54 + c], st2[:, 44 + c:46 + c]))
                    for t, (c0, c1) in enumerate(((0, P), (P, 3 * P))):
                        ts(pa[:, h % 2, c0:c1], pa[:, h % 2, c0:c1], st2[:, 52 + c + t:53 + c + t], None, ALU.mult).then_inc(*S.up("pan", (h, t)))
                if h >= 1:
                    g = h - 1
                    dve.wait_ge(*S.at("pat_mm", g))
                    if g >= 2:
                        dve.wait_ge(*S.at("oa_mm", g - 2))
                    V.tensor_copy(pat[:, g % 2, :], at_bank("pat", g)[:, 0:384]).then_inc(*S.up("pat", g))

            for br in range(2):
                for n in range(2):
                    for t in range(2):
                        dve.wait_ge(*S.at("branch_mm", (br, n, t)))
                        dve.wait_ge(*S.at("gates", ((6 if br == 0 else 8) + n, t)))
                        cols = slice(n * 512, (n + 1) * 512)
                        b = at_bank("branch", br, n, t)
                        if br == 0:
                            tt(mixed[:, t, cols], b, ga[:, t, cols], ALU.mult).then_inc(*S.up("mix", (br, n, t)))
                        else:
                            link(tt(gb[:, t, cols], b, gb[:, t, cols], ALU.mult))
                            tt(mixed[:, t, cols], mixed[:, t, cols], gb[:, t, cols], ALU.add).then_inc(*S.up("mix", (br, n, t)))
            for n in range(2):
                for t in range(2):
                    dve.wait_ge(*S.at("out2_mm", (n, t)))
                    cols = slice(n * 512, (n + 1) * 512)
                    tt(x[:, t, cols], at_bank("out2", n, t), x[:, t, cols], ALU.add).then_inc(*S.up("res2", (n, t)))
            dve.wait_ge(*S.at("res2", (1, 1)))
            for t in range(2):
                V.tensor_copy(small[0:1, 252 + t:253 + t], small[0:1, 200:201]).then_inc(*S.up("x_rms", (1, t)))
            rms(1)
            for f in range(KF // 2):
                for half in range(2):
                    for i in range(2):
                        fb = half * KF + 2 * f + i
                        n = (2 * f + i) % 4
                        b = at_bank("up", f, half)[:, i * T:(i + 1) * T]
                        o = cg[:, n, half, :]
                        dve.wait_ge(*S.at("tap2", (f, half, 1)))
                        link(stt(o[:, 1:T], b[:, 0:T - 1], column("conv_w1", fb), o[:, 1:T], ALU.mult, ALU.add))
                        stt(o[:, 2:T], b[:, 0:T - 2], column("conv_w0", fb), o[:, 2:T], ALU.mult, ALU.add).then_inc(*S.up("conv", (f, half, i)))
                for i in range(2):
                    n = (2 * f + i) % 4
                    dve.wait_ge(*S.at("up_silu", (f, i)))
                    dve.wait_ge(*S.at("conv", (f, 1, i)))
                    tt(fT[:, 2 * f + i, :], cg[:, n, 0, :], cg[:, n, 1, :], ALU.mult).then_inc(*S.up("ffn", 2 * f + i))
            for n in range(2):
                for t in range(2):
                    if t == 0:
                        dve.wait_ge(*S.at("down_mm", (n, t)))
                    else:
                        dve.wait_ge(*S.at("down_k", (n, 2)))
                    cols = slice(n * 512, (n + 1) * 512)
                    tt(x[:, t, cols], at_bank("down", n, t), x[:, t, cols], ALU.add).then_inc(*S.up("res3", (n, t)))

        @block.gpsimd
        def _(pool):
            G = nc.gpsimd
            pool.wait_ge(*S.at("lam_tables"))
            pool.wait_ge(*S.at("x1", 3))
            G.memset(bbd.rearrange("p a b -> p (a b)"), 0.0).then_inc(*S.up("bbd_zero"))
            pool.wait_ge(*S.at("bbd_zero"))

            def parts(dr, o, src, r, n):
                t0 = tmpp[:, dr, 0, :].rearrange("p (g r s) -> p g r s", g=GQ, r=2)
                t1 = tmpp[:, dr, 1, :].rearrange("p (g r s) -> p g r s", g=GQ, r=2)
                G.tensor_tensor(t0, src, over(r, (1, GQ), (64, 2), (0, GS)), ALU.mult).then_inc(*S.up("pool_re"))
                G.tensor_tensor(t1, src[:, :, ::-1, :], over(n, (1, GQ), (64, 2), (0, GS)), ALU.mult).then_inc(*S.up("pool_im"))
                counts_now = S.last("pool_re"), S.last("pool_im")
                return lambda: (pool.wait_ge(*counts_now[0]), pool.wait_ge(*counts_now[1]), G.tensor_tensor(o, t0, t1, ALU.add))[2]

            for q in range(NQ):
                g0 = q * GQ
                pool.wait_ge(*S.at("b_load%d" % (q % 2), q))
                sums = [parts(dr, bbar[:, dr], braw_(q)[:, dr], wR[:, dr, 0, g0:g0 + 1], wN[:, dr, 0, g0:g0 + 1]) for dr in range(2)]
                for dr in range(2):
                    sums[dr]().then_inc(*S.up("bbar", (q, dr)))
                pool.wait_ge(*S.at("bbar", (q, 1)))
                if q >= 2:
                    pool.wait_ge(*S.at("kern_mm", q - 2))
                for par in range(2):
                    r = slice(64 * par, 64 * par + 64)
                    for dr in range(2):
                        G.tensor_copy(bbd_(q)[r, dr, :, :, 16 * par:16 * par + 16], bbar[r, dr]).then_inc(*S.up("bbd", q))
                        pool.wait_ge(*S.last("bbd"))
                if q:
                    pool.wait_ge(*S.at("mbT_mm", (q - 1, 1, 1, 1)))
                at_ = lambda dr, n: 7 - n if dr == 0 else n
                for dr in range(2):
                    G.tensor_copy(mb[:, dr, :, :, at_(dr, 0), :], bbar[:, dr]).then_inc(*S.up("mb_power", (q, -1, dr)))
                for n in range(7):
                    sums = []
                    for dr in range(2):
                        pool.wait_ge(*S.at("mb_power", (q, n - 1, dr)))
                        sums.append(parts(dr, mb[:, dr, :, :, at_(dr, n + 1), :], mb[:, dr, :, :, at_(dr, n), :],
                                          lamL[:, dr, 0, g0:g0 + 1], lamN[:, dr, 0, g0:g0 + 1]))
                    for dr in range(2):
                        sums[dr]().then_inc(*(S.up("mb", (q, dr)) if n == 6 else S.up("mb_power", (q, n, dr))))
                pool.wait_ge(*S.at("mb", (q, 1)))

        @block.sync
        def _(sp):
            def ring_load(i):
                src, shape, freed, parts = loads[i]
                if i >= SLOTS:
                    sp.wait_ge(*S.at(*loads[i - SLOTS][2]))
                o = slot(i, *shape)
                if parts is None:
                    sp.dma_start(o, src).then_inc(*S.up(f"slot{i % SLOTS}", i, by=16))
                else:
                    for n, part in enumerate(parts):
                        sp.dma_start(o[:, n], part).then_inc(*S.up(f"slot{i % SLOTS}", i, by=16))

            def bias(l, ct):
                if ct >= 2 or l:
                    sp.wait_ge(*S.at("mod_row", (l, ct - 2) if ct >= 2 else (l - 1, ct + 4)))
                src = dview(a["b_mod"], l * 3 * D + ct * 512, (0, 2), (1, 512))
                sp.dma_start(bmod[0:2, ct % 2, :], src).then_inc(*S.up("bmod%d" % (ct % 2), (l, ct), by=16))

            for i in range(first_glu):
                for l in range(2):
                    for ct in range(6):
                        if load_no[("mod", l, ct)] == i:
                            bias(l, ct)
                ring_load(i)
                if i == load_no[("mod", 1, 0)]:
                    sp.wait_ge(*S.at("vg", H - 1))
                    sp.wait_ge(*S.at("out0_k", (1, 1)))
                    for ri, nm in enumerate(("s5_lam_re", "s5_lam_im")):
                        for dr in range(2):
                            for par in range(2):
                                sp.dma_start(lam[64 * dr:64 * dr + 64, ri, 64 * par:64 * par + 64],
                                                   a[nm][0, dr, 64 * par:64 * par + 64, :]).then_inc(*S.up("lam_in", by=16))
                    for dr in range(2):
                        for par in range(2):
                            sp.dma_start(ldt[64 * dr:64 * dr + 64, par:par + 1],
                                               dview(a["s5_log_dt"], dr * NG + 64 * par, (1, 64), (1, 1))).then_inc(*S.up("lam_in", by=16))

            def b_and_c(q):
                if q >= 2:
                    sp.wait_ge(*S.at("bbd", q - 2))
                    sp.wait_ge(*S.at("cT_mm", q - 2))
                for ri, nm in enumerate(("s5_b_re", "s5_b_im")):
                    for par in range(2):
                        g0 = par * 64 + q * GQ
                        for dr in range(2):
                            sp.dma_start(braw_(q)[64 * par:64 * par + 64, dr, :, ri, :],
                                         a[nm][0, dr, g0:g0 + GQ, :, :].rearrange("g p s -> p g s")).then_inc(*S.up("b_load%d" % (q % 2), q, by=16))
                for ri, nm in enumerate(("s5_c_re", "s5_c_im")):
                    for par in range(2):
                        r0 = (par * 64 + q * GQ) * GS
                        src = a[nm][0].rearrange("d g s p -> (g s) d p")[r0:r0 + P]
                        sp.dma_start(cn_(q)[:, ri, :, 64 * par:64 * par + 64], src).then_inc(*S.up("cn%d" % (q % 2), q, by=16))

            def u_chunks(q):
                if q >= 2:
                    sp.wait_ge(*S.at("y_mm", (q - 2, 1)))
                for j in range(L):
                    for par in range(2):
                        src = dview(u_dram, (par * 64 + q * GQ) * GS * 2 * T + j * NC, (2 * T, GS), (GS * 2 * T, GQ), (1, NC))
                        sp.dma_start(u_(q)[16 * j:16 * j + 16, par, :, :], src).then_inc(*S.up("u_load%d" % (q % 2), q, by=16))

            def toeplitz(q):
                sp.wait_ge(*S.at("k_out", q))
                if q >= 2:
                    sp.wait_ge(*S.at("y_mm", (q - 2, 1)))
                n = GS * 15 * GS
                for j in range(L):
                    for par in range(2):
                        src = dview(k_dram, (par * 64 + q * GQ) * n + (7 - j) * GS, (15 * GS, GS), (n, GQ), (1, P))
                        sp.dma_start(tt_(q)[16 * j:16 * j + 16, par, :, :], src).then_inc(*S.up("t_load%d" % (q % 2), q, by=16))

            sp.wait_ge(*S.at("res0", (1, 3)))
            b_and_c(0)
            b_and_c(1)
            for f in range(14, 16):
                sp.wait_ge(*S.at("u_out%d" % (f % 2), f))
            sp.wait_ge(*S.at("s5in_mm", 31))
            u_chunks(0)
            u_chunks(1)
            toeplitz(0)
            for q in range(2, NQ):
                b_and_c(q)
                toeplitz(q - 1)
                u_chunks(q)
            toeplitz(NQ - 1)
            sp.wait_ge(*S.at("y_mm", (NQ - 1, 1)))
            for i in range(SLOTS):
                ring_load(first_glu + i)
            for q in range(NQ - 2, NQ):
                sp.wait_ge(*S.at("y_out%d" % (q % 2), q))
            for part in range(4):
                ks = slice(4 * part, 4 * part + 4)
                sp.dma_start(yT[:, ks, :], y_dram.rearrange("(k p) t -> p k t", p=P)[:, ks, :]).then_inc(*S.up("yT_load%d" % part, by=16))
                for k in range(4 * part, 4 * part + 4):
                    sp.dma_start(uT[:, k, :].rearrange("p (j c) -> p j c", j=L),
                                 u_dram[k * P:(k + 1) * P, :].rearrange("p (j s c) -> p j s c", j=L, s=2)[:, :, 1, :]).then_inc(*S.up("yT_load%d" % part, by=16))
            for i in range(first_glu + SLOTS, len(loads)):
                ring_load(i)

        return S.seen


def h2v(flat):
    return flat[:, 0:KD * T].rearrange("p (k t) -> p k t", k=KD)


def tables():
    i = np.arange(P)
    masks = np.zeros((6, P, P), np.float32)
    masks[0] = i[:, None] + i[None, :] == P - 1
    masks[1] = np.where((i[:, None] < 64) & (i[None, :] >= 64), LOW, 0.0)
    masks[2] = i[:, None] < i[None, :]
    masks[3] = -(i[:, None] >= i[None, :]).astype(np.float32)
    masks[4] = -1.0
    masks[5] = np.where(i[:, None] >= i[None, :], LOW, 0.0)
    sel = np.zeros((2, 2, P), np.float32)
    sel[0, 0] = sel[1, 1] = 1.0
    t = np.arange(T)
    quarter = ROPE // 4
    inv = np.float32(10000.0) ** (-np.arange(quarter, dtype=np.float32) / np.float32(quarter))
    ang_r = (t // GRID_W).astype(np.float32)[:, None] * inv
    ang_c = (t % GRID_W).astype(np.float32)[:, None] * inv
    ang = np.concatenate([ang_r, ang_r, ang_c, ang_c], axis=-1).astype(np.float32)
    sign = np.repeat(np.array([-1.0, 1.0, -1.0, 1.0], np.float32), quarter)
    rope = np.stack([np.cos(ang), np.sin(ang) * sign]).astype(np.float32)
    return {"c_ident": np.eye(P, dtype=np.float32)[None], "c_masks": masks, "c_sel": sel, "c_rope": rope}


_INS = ["x", "c", "ctx", "c_ctx", "w_mod", "b_mod", "ln_g", "ln_b", "mla_w_in", "mla_q_norm", "mla_kv_norm", "mla_w_uq",
        "mla_w_uk", "mla_w_uv", "mla_w_out", "s5_w_in", "s5_lam_re", "s5_lam_im", "s5_log_dt", "s5_b_re", "s5_b_im",
        "s5_c_re", "s5_c_im", "s5_d", "s5_w_glu", "s5_b_glu", "s5_w_out", "norm1_g_2", "w_in_2", "q_norm_g_2",
        "k_norm_g_2", "w_branch_a_2", "w_branch_b_2", "w_out_2", "norm2_g_2", "w_ffn_up_2", "ffn_conv_w_2",
        "ffn_conv_b_2", "w_ffn_down_2"]


def kernel(**inputs):
    import concourse.bacc as _bacc
    from concourse.bass_utils import run_bass_kernel_spmd as _run

    arrays = {n: np.ascontiguousarray(inputs[n]) for n in _INS}
    arrays.update(tables())
    rel = np.asarray(inputs["rel_bias_2"])[0]
    arrays["c_rel"] = np.ascontiguousarray(rel[:, np.clip(255 - np.arange(384), -MAX_REL, MAX_REL) + MAX_REL])

    counts, places = None, {}
    for _ in range(2):
        nc = _bacc.Bacc("TRN2", target_bir_lowering=False, num_devices=1)
        aps = {n: nc.dram_tensor("in_" + n, v.shape, F32, kind="ExternalInput").ap() for n, v in arrays.items()}
        o = nc.dram_tensor("out", (1, T, D), F32, kind="ExternalOutput").ap()
        counts = build(nc, aps, o, counts, places)
    r = _run(nc, [{"in_" + n: v for n, v in arrays.items()}], core_ids=[0])
    return r.results[0]["out"]
```
